# Optimizing a Trainium2 kernel written in Bass

```python
import functools
import jax, jax.numpy as jnp
from jax import lax
import numpy as np

D_MODEL = 1024
BATCH = 1
SEQ = 128
DEPTH = 1
DEC_BATCH = 1
DEC_SEQ = 256
PAST_LEN = 128

GRID_W = 64
NA_HEADS = 8
NA_HEAD_DIM = 64
NA_WIDTH = NA_HEADS * NA_HEAD_DIM
WIN_H_MAX = 8
WIN_W = 16
COL_BLOCK = 16
COL_SPAN = COL_BLOCK + WIN_W
CTX_Q_BLOCK = 128
FNET_GROUPS = 4
FNET_GROUP_DIM = 64
FNET_WIDTH = FNET_GROUPS * FNET_GROUP_DIM
CONV_WIDTH = 256
CONV_KERNEL = 31
N_BRANCH = 3
IN_COLS = 3 * NA_WIDTH + FNET_WIDTH + 2 * CONV_WIDTH + N_BRANCH * D_MODEL
N_MOD = 6
MOE_GROUPS = 4
EXPERTS_PER_GROUP = 8
N_EXPERTS = MOE_GROUPS * EXPERTS_PER_GROUP
EXPERT_TOPK = 2
EXPERT_HIDDEN = 256
EPS = 1e-6
NEG_INF = -1e30

kernel_name = 'hybrid_na_fnet_conv_hmoe_diffusion_step'

def rms_norm(x, g):
    xf = x.astype(jnp.float32)
    y = xf * lax.rsqrt(jnp.mean(xf * xf, axis=-1, keepdims=True) + EPS)
    return (y * g.astype(jnp.float32)).astype(x.dtype)

def layer_norm(x, g, b):
    xf = x.astype(jnp.float32)
    mu = jnp.mean(xf, axis=-1, keepdims=True)
    xc = xf - mu
    y = xc * lax.rsqrt(jnp.mean(xc * xc, axis=-1, keepdims=True) + EPS)
    return (y * g.astype(jnp.float32) + b.astype(jnp.float32)).astype(x.dtype)

def ada_mod(cond, w_mod, b_mod):
    m = jax.nn.silu(cond) @ w_mod + b_mod
    return m.reshape(cond.shape[0], N_MOD, 1, D_MODEL)

def ctx_attention(q, k, v):
    b, h, l, d = q.shape
    nb = l // CTX_Q_BLOCK
    scale = d ** -0.5
    qb = q.reshape(b, h, nb, CTX_Q_BLOCK, d).transpose(2, 0, 1, 3, 4)

    def one(qi):
        s = jnp.einsum('bhqd,bhkd->bhqk', qi, k).astype(jnp.float32) * scale
        p = jax.nn.softmax(s, axis=-1).astype(v.dtype)
        return jnp.einsum('bhqk,bhkd->bhqd', p, v)

    o = lax.map(one, qb)
    return o.transpose(1, 2, 0, 3, 4).reshape(b, h, l, d)

def neighbourhood_attention(q, k, v, k_ctx, v_ctx, rpb):
    b, h, l, d = q.shape
    rows = l // GRID_W
    kh = min(WIN_H_MAX, rows)
    n_cb = GRID_W // COL_BLOCK
    scale = d ** -0.5
    r_ar = np.arange(rows)
    row_start = np.clip(r_ar - kh // 2, 0, rows - kh)
    row_idx = row_start[:, None] + np.arange(kh)[None, :]
    dr = row_idx - r_ar[:, None]
    qcol = np.arange(n_cb)[:, None] * COL_BLOCK + np.arange(COL_BLOCK)[None, :]
    blk_start = np.clip(np.arange(n_cb) * COL_BLOCK - WIN_W // 2, 0, GRID_W - COL_SPAN)
    key_cols = blk_start[:, None] + np.arange(COL_SPAN)[None, :]
    win_start = np.clip(qcol - WIN_W // 2, 0, GRID_W - WIN_W)
    kc_b = key_cols[:, None, :]
    col_ok = (kc_b >= win_start[..., None]) & (kc_b < win_start[..., None] + WIN_W)
    dc = np.clip(kc_b - qcol[..., None], -(WIN_W - 1), WIN_W - 1)
    bias = rpb[:, (dr + WIN_H_MAX - 1)[:, None, None, :, None], (dc + WIN_W - 1)[None, :, :, None, :]]
    kg = k.reshape(b, h, rows, GRID_W, d)[:, :, row_idx]
    vg = v.reshape(b, h, rows, GRID_W, d)[:, :, row_idx]
    k_blk = jnp.take(kg, key_cols, axis=4)
    v_blk = jnp.take(vg, key_cols, axis=4)
    qb = q.reshape(b, h, rows, n_cb, COL_BLOCK, d)
    s_win = jnp.einsum('bhrcqd,bhrickd->bhrcqik', qb, k_blk).astype(jnp.float32) * scale
    s_win = s_win + bias[None].astype(jnp.float32)
    s_win = jnp.where(col_ok[:, :, None, :], s_win, NEG_INF)
    s_win = s_win.reshape(b, h, rows, n_cb, COL_BLOCK, kh * COL_SPAN)
    s_ctx = jnp.einsum('bhrcqd,bhkd->bhrcqk', qb, k_ctx).astype(jnp.float32) * scale
    p = jax.nn.softmax(jnp.concatenate([s_win, s_ctx], axis=-1), axis=-1).astype(v.dtype)
    p_win = p[..., : kh * COL_SPAN].reshape(b, h, rows, n_cb, COL_BLOCK, kh, COL_SPAN)
    p_ctx = p[..., kh * COL_SPAN:]
    o = jnp.einsum('bhrcqik,bhrickd->bhrcqd', p_win, v_blk) + jnp.einsum('bhrcqk,bhkd->bhrcqd', p_ctx, v_ctx)
    return o.reshape(b, h, l, d)

def fourier_mix(u, w_fnet):
    b, l, _ = u.shape
    uf = u.astype(jnp.float32).reshape(b, l, FNET_GROUPS, FNET_GROUP_DIM)
    f = jnp.fft.fft2(uf, axes=(1, 3), norm='ortho').real
    return f.reshape(b, l, FNET_WIDTH).astype(u.dtype) @ w_fnet

def conv_module(u, conv_dw, conv_b, conv_ln_g, conv_ln_b, w_conv_o):
    a, gt = jnp.split(u, 2, axis=-1)
    z = a * jax.nn.sigmoid(gt)
    z = lax.conv_general_dilated(
        z, conv_dw[:, None, :], window_strides=(1,),
        padding=[(CONV_KERNEL // 2, CONV_KERNEL // 2)],
        dimension_numbers=('NWC', 'WIO', 'NWC'),
        feature_group_count=CONV_WIDTH) + conv_b
    z = jax.nn.silu(layer_norm(z, conv_ln_g, conv_ln_b))
    return z @ w_conv_o

def hier_moe(h, w_group, b_group, w_router, b_router, w1, w3, w2):
    b, l, _ = h.shape
    hf = h.reshape(b * l, D_MODEL)
    n = hf.shape[0]
    gp = jax.nn.softmax((hf @ w_group + b_group).astype(jnp.float32), axis=-1)
    g_top, g_idx = lax.top_k(gp, 1)
    el = (hf @ w_router + b_router).astype(jnp.float32).reshape(n, MOE_GROUPS, EXPERTS_PER_GROUP)
    el_sel = jnp.take_along_axis(el, g_idx[:, :, None], axis=1)[:, 0]
    ep = jax.nn.softmax(el_sel, axis=-1)
    e_top, e_idx = lax.top_k(ep, EXPERT_TOPK)
    wts = g_top * e_top / jnp.sum(e_top, axis=-1, keepdims=True)
    expert_id = g_idx * EXPERTS_PER_GROUP + e_idx
    comb = jnp.sum(jax.nn.one_hot(expert_id, N_EXPERTS, dtype=jnp.float32) * wts[..., None], axis=1)
    hid = jax.nn.silu(jnp.einsum('nd,edf->nef', hf, w1)) * jnp.einsum('nd,edf->nef', hf, w3)
    hid = hid * comb[:, :, None].astype(hid.dtype)
    out = jnp.einsum('nef,efd->nd', hid, w2)
    return out.reshape(b, l, D_MODEL)

def trunk_layer(x, mod, attn_fn, norm1_g, w_in, w_attn_o, w_fnet, conv_dw, conv_b, conv_ln_g,
                conv_ln_b, w_conv_o, w_out, norm2_g, w_group, b_group, w_router, b_router, w1, w3, w2):
    b, l, _ = x.shape
    h = rms_norm(x, norm1_g) * (1 + mod[:, 1]) + mod[:, 0]
    u = h @ w_in
    cuts = [NA_WIDTH, 2 * NA_WIDTH, 3 * NA_WIDTH, 3 * NA_WIDTH + FNET_WIDTH,
            3 * NA_WIDTH + FNET_WIDTH + 2 * CONV_WIDTH]
    q, k, v, uf, uc, ug = jnp.split(u, cuts, axis=-1)

    def heads(t):
        return t.reshape(b, l, NA_HEADS, NA_HEAD_DIM).transpose(0, 2, 1, 3)

    q, k, v = heads(q), heads(k), heads(v)
    oa = attn_fn(q, k, v).transpose(0, 2, 1, 3).reshape(b, l, NA_WIDTH) @ w_attn_o
    of = fourier_mix(uf, w_fnet)
    oc = conv_module(uc, conv_dw, conv_b, conv_ln_g, conv_ln_b, w_conv_o)
    g = jax.nn.sigmoid(ug.reshape(b, l, N_BRANCH, D_MODEL))
    merged = g[:, :, 0] * oa + g[:, :, 1] * of + g[:, :, 2] * oc
    x = x + mod[:, 2] * (merged @ w_out)
    h2 = rms_norm(x, norm2_g) * (1 + mod[:, 4]) + mod[:, 3]
    x = x + mod[:, 5] * hier_moe(h2, w_group, b_group, w_router, b_router, w1, w3, w2)
    return x, k, v

def setup_inputs(seed: int = 0) -> dict:
    key = jax.random.key(seed)
    ks = iter(jax.random.split(key, 40))

    def nrm(shape, scale):
        return jax.random.normal(next(ks), shape, jnp.float32) * scale

    d = D_MODEL
    return {
        'x_prompt': nrm((BATCH, SEQ, d), 1.0),
        'x_sample': nrm((DEC_BATCH, DEC_SEQ, d), 1.0),
        'cache_k': nrm((DEC_BATCH, DEPTH, NA_HEADS, PAST_LEN, NA_HEAD_DIM), 1.0),
        'cache_v': nrm((DEC_BATCH, DEPTH, NA_HEADS, PAST_LEN, NA_HEAD_DIM), 1.0),
        'c': nrm((DEC_BATCH, d), 1.0),
        'c_ctx': nrm((d,), 1.0),
        'w_mod': nrm((DEPTH, d, N_MOD * d), 0.5 * d ** -0.5),
        'b_mod': nrm((DEPTH, N_MOD * d), 0.02),
        'norm1_g': 1.0 + nrm((DEPTH, d), 0.05),
        'w_in': nrm((DEPTH, d, IN_COLS), d ** -0.5),
        'rpb': nrm((DEPTH, NA_HEADS, 2 * WIN_H_MAX - 1, 2 * WIN_W - 1), 0.1),
        'w_attn_o': nrm((DEPTH, NA_WIDTH, d), NA_WIDTH ** -0.5),
        'w_fnet': nrm((DEPTH, FNET_WIDTH, d), FNET_WIDTH ** -0.5),
        'conv_dw': nrm((DEPTH, CONV_KERNEL, CONV_WIDTH), CONV_KERNEL ** -0.5),
        'conv_b': nrm((DEPTH, CONV_WIDTH), 0.02),
        'conv_ln_g': 1.0 + nrm((DEPTH, CONV_WIDTH), 0.05),
        'conv_ln_b': nrm((DEPTH, CONV_WIDTH), 0.02),
        'w_conv_o': nrm((DEPTH, CONV_WIDTH, d), CONV_WIDTH ** -0.5),
        'w_out': nrm((DEPTH, d, d), d ** -0.5),
        'norm2_g': 1.0 + nrm((DEPTH, d), 0.05),
        'w_group': nrm((DEPTH, d, MOE_GROUPS), d ** -0.5),
        'b_group': nrm((DEPTH, MOE_GROUPS), 0.01),
        'w_router': nrm((DEPTH, d, N_EXPERTS), d ** -0.5),
        'b_router': nrm((DEPTH, N_EXPERTS), 0.01),
        'w1': nrm((DEPTH, N_EXPERTS, d, EXPERT_HIDDEN), d ** -0.5),
        'w3': nrm((DEPTH, N_EXPERTS, d, EXPERT_HIDDEN), d ** -0.5),
        'w2': nrm((DEPTH, N_EXPERTS, EXPERT_HIDDEN, d), EXPERT_HIDDEN ** -0.5),
        'final_g': 1.0 + nrm((d,), 0.05),
    }

def reference(x_prompt, x_sample, cache_k, cache_v, c, c_ctx, w_mod, b_mod, norm1_g, w_in, rpb,
              w_attn_o, w_fnet, conv_dw, conv_b, conv_ln_g, conv_ln_b, w_conv_o, w_out, norm2_g,
              w_group, b_group, w_router, b_router, w1, w3, w2, final_g):
    xp = x_prompt
    xs = x_sample
    ks = []
    vs = []
    for l in range(DEPTH):
        lw = (norm1_g[l], w_in[l], w_attn_o[l], w_fnet[l], conv_dw[l], conv_b[l], conv_ln_g[l],
              conv_ln_b[l], w_conv_o[l], w_out[l], norm2_g[l], w_group[l], b_group[l],
              w_router[l], b_router[l], w1[l], w3[l], w2[l])
        mod_ctx = ada_mod(c_ctx[None, :], w_mod[l], b_mod[l])
        xp, k_l, v_l = trunk_layer(xp, mod_ctx, ctx_attention, *lw)
        ks.append(k_l)
        vs.append(v_l)
        mod_lat = ada_mod(c, w_mod[l], b_mod[l])
        attn_lat = functools.partial(neighbourhood_attention, k_ctx=cache_k[:, l], v_ctx=cache_v[:, l], rpb=rpb[l])
        xs, _, _ = trunk_layer(xs, mod_lat, attn_lat, *lw)
    y_prompt = rms_norm(xp, final_g)
    y_sample = rms_norm(xs, final_g)
    new_k = jnp.stack(ks, axis=1)
    new_v = jnp.stack(vs, axis=1)
    return (y_prompt, y_sample, new_k, new_v)


_drawn_inputs = setup_inputs


def setup_inputs(seed=0):
    import zlib

    import numpy as np

    out = dict(_drawn_inputs(seed))
    spreads = {}
    factors = {'cache_k': 3.934,
     'cache_v': 3.151,
     'rpb': 64.0,
     'conv_b': 8.0,
     'conv_ln_g': 6.199,
     'conv_ln_b': 8.0,
     'norm2_g': 2.68,
     'b_group': 8.0,
     'b_router': 8.0}
    for name, (base, spread) in spreads.items():
        noise = np.random.default_rng([zlib.crc32(name.encode()), seed]).standard_normal(out[name].shape)
        drawn = base * np.exp(spread * noise) if base else spread * noise
        out[name] = __import__('jax').numpy.asarray(drawn.astype(out[name].dtype))
    for name, factor in factors.items():
        out[name] = (out[name] * factor).astype(out[name].dtype)
    return out
```

```python
from contextlib import ExitStack

import concourse.bass as bass
from concourse import mybir

F32 = mybir.dt.float32
F32R = mybir.dt.float32r
I32 = mybir.dt.int32
ALU = mybir.AluOpType
ACT = mybir.ActivationFunctionType
AX = mybir.AxisListType.X

P = 128
D = 1024
KT = D // P
NCTX, NLAT = 128, 256
N = NCTX + NLAT
NT = N // P
SEG = ((0, NCTX, 0), (NCTX, N, 1))
HEADS, HD = 8, 64
PAIRS = HEADS // 2
GRID_W, GRID_H = 64, 4
NDR = 6
RPB_R, RPB_C = 15, 31
FW, FG = 256, 64
CW, CK = 256, 31
PAD = CK // 2
ZW = PAD + NCTX + PAD + NLAT + PAD
CO = ZW - 2 * PAD
LAT0 = NCTX + PAD
COL_Q, COL_K, COL_V = 0, 512, 1024
COL_F = 1536
COL_C = COL_F + FW
COL_G = COL_C + 2 * CW
GROUPS, EPG, EH = 4, 8, 256
NE = GROUPS * EPG
ROUNDS = (N + P - 1) // P
EPS = 1e-6
NEG = -1e30

RING = 6
SLOT = 2048
CH = SLOT // 2
SPLIT = 4

V_CTX, V_C, V_N1, V_N2, V_BM, V_CB, V_LG, V_LB = 0, 8, 16, 24, 32, 80, 82, 84
V_ROWS = 86

SLOTS = ([("mod", j) for j in range(8)] + [("q", j) for j in range(2)] + [("k", j) for j in range(2)]
         + [("uf", 0), ("v", 0), ("v", 1), ("uc", 0), ("uc", 1)])
UG0 = len(SLOTS)
for _d in range(KT):
    SLOTS += [("br", _d), ("g12", _d), ("mod", 8 + 2 * _d), ("mod", 9 + 2 * _d)]
WO0 = len(SLOTS)
SLOTS += [("wo", j) for j in range(4)]
PRE = len(SLOTS)
PRE_CH = 2 * PRE
BY_COLUMNS = ("q", "k", "uc", "wo")

ITEM = [("A", 0), ("B", 0)]
for _e in range(1, EPG):
    ITEM += [("A", _e), ("B", _e), ("C", _e - 1)]
ITEM += [("C", EPG - 1)]
ITEM_CH = 2 * len(ITEM)
assert len(ITEM) % RING == 0 and ITEM_CH % SPLIT == 0

UNITS = 3 * HEADS


def first_chunk(kind, j=0):
    return 2 * SLOTS.index((kind, j))


WINDOW = [("chunk", first_chunk("uf")), ("chunk", first_chunk("uf") + 1), ("fnet", 0), ("fnet", 1)]
_fill = {0: [("chunk", first_chunk("v"))], 1: [("chunk", first_chunk("v") + 1)],
         2: [("chunk", first_chunk("v", 1))], 3: [("chunk", first_chunk("v", 1) + 1)],
         5: [("chunk", first_chunk("uc"))], 6: [("chunk", first_chunk("uc") + 1)],
         8: [("chunk", first_chunk("uc", 1))], 9: [("chunk", first_chunk("uc", 1) + 1)]}
for _u in range(UNITS + 2):
    WINDOW += [("unit", _u)] + _fill.get(_u, []) + [("turn", _u - 2)]


def build(nc, x_prompt, x_sample, cache_k, cache_v, c, c_ctx, w_mod, b_mod, norm1_g, w_in, rpb, w_attn_o,
          w_fnet, conv_dw, conv_b, conv_ln_g, conv_ln_b, w_conv_o, w_out, norm2_g, w_group, b_group,
          w_router, b_router, w1, w3, w2, final_g, dft_lat, dft_ctx, dft_feat,
          y_prompt, y_sample, new_k, new_v):
    ctx = ExitStack()
    with ctx:
        base = (nc.sbuf_base + 31) // 32 * 32
        top = nc.sbuf_usable_end

        class Region:

            def __init__(self, start, size=None):
                self.start, self.at, self.end = start, start, start + size if size else top

            def tile(self, name, shape, dt=F32):
                size = 4
                for s in shape[1:]:
                    size *= s
                t = nc.alloc_sbuf_tensor_at(name, shape, dt, offset=self.at)
                self.at += (size + 31) // 32 * 32
                assert self.at <= self.end, (name, self.at, self.end)
                return t

        R = Region(base)
        raw = R.tile("raw", [P, RING, SLOT])
        w_hi = R.tile("w_hi", [P, SPLIT, CH], F32R)
        w_lo = R.tile("w_lo", [P, SPLIT, CH], F32R)
        xT = R.tile("xT", [P, KT, N])
        ident = R.tile("ident", [P, P])
        ones = R.tile("ones", [P, P])
        tri = R.tile("tri", [P, P])
        iota_s = R.tile("iota_s", [P, P])
        vec_t = R.tile("vec_t", [P, V_ROWS])
        taps = R.tile("taps", [P, 2, CK])
        cond = R.tile("cond", [P, 2, KT])
        cond_t = R.tile("cond_t", [P, 2, KT])
        cond4 = R.tile("cond4", [P, KT, 4], F32R)
        modT = R.tile("modT", [P, 48, 2])
        scale1 = R.tile("scale1", [P, KT, 2])
        scale2 = R.tile("scale2", [P, KT, 2])
        eps_t = R.tile("eps_t", [P, 1])
        rstd = R.tile("rstd", [P, N])
        sq = R.tile("sq", [P, 2, N])
        modrow = R.tile("modrow", [4, 2, 256])
        w_gr = R.tile("w_gr", [P, KT, GROUPS + NE])
        b_gr = R.tile("b_gr", [P, GROUPS + NE])
        mod_tmp = R.tile("mod_tmp", [P, 32, 4])
        stats = R.tile("stats", [P, 3, 8])
        rt = R.tile("rt", [P, 3, 64])
        start_h = R.at
        Rh = Region(start_h, 2 * 4 * KT * N)
        h_hi = Rh.tile("h_hi", [P, KT, N], F32R)
        h_lo = Rh.tile("h_lo", [P, KT, N], F32R)
        start_b = Rh.at
        Rb = Region(start_b, 4 * 16 * N)
        at_hi = Rb.tile("at_hi", [P, PAIRS, N], F32R)
        at_lo = Rb.tile("at_lo", [P, PAIRS, N], F32R)
        fn_hi = Rb.tile("fn_hi", [P, 2, N], F32R)
        fn_lo = Rb.tile("fn_lo", [P, 2, N], F32R)
        start_cv = Rb.at
        cv_hi = Rb.tile("cv_hi", [P, 2, N], F32R)
        cv_lo = Rb.tile("cv_lo", [P, 2, N], F32R)
        k_out = Region(start_cv, 4 * 4 * N).tile("k_out", [P, HEADS * HD])
        start_x = Rb.at
        Rx = Region(start_x)
        qT = Rx.tile("qT", [P, PAIRS, N])
        kT = Rx.tile("kT", [P, PAIRS, N])
        v_tok = Rx.tile("v_tok", [P, NT, HEADS * HD])
        ckT = Rx.tile("ckT", [P, PAIRS, P])
        cv_tok = Rx.tile("cv_tok", [P, HEADS, HD])
        bias = Rx.tile("bias", [P, HEADS, NDR, GRID_W])
        probs = Rx.tile("probs", [P, 3, N])
        ptl = Rx.tile("ptl", [P, 3, 2, P])
        ptc = Rx.tile("ptc", [P, P])
        start_y = Rx.at
        h32 = Region(start_x, 4 * KT * N).tile("h32", [P, KT, N])
        ck_tok = Region(start_x + 4 * KT * N, 2048 * 3).tile("ck_tok", [P, HEADS, HD])
        Rs = Region(start_y)
        x_tok = Rs.tile("x_tok", [P, NT, D])
        Rs2 = Region(start_b)
        vec_rows = Rs2.tile("vec_rows", [V_ROWS, P])
        tap_rows = Rs2.tile("tap_rows", [2 * CK, P])
        Ry = Region(start_y)
        u_tok = Ry.tile("u_tok", [P, NT, FW])
        lat_w = Ry.tile("lat_w", [P, 2, 2 * NLAT])
        ctx_w = Ry.tile("ctx_w", [P, 2 * NCTX])
        feat_w = Ry.tile("feat_w", [P, 2, P])
        z_cs = Ry.tile("z_cs", [P, 2, N])
        Rc = Region(start_y)
        zpad = Rc.tile("zpad", [P, 2, ZW])
        acc = Rc.tile("acc", [P, 2, CO])
        csq = Rc.tile("csq", [P, 2, CO])
        crs = Rc.tile("crs", [P, CO])
        prod = Rc.tile("prod", [P, CO])
        Rg = Region(start_x)
        mg_hi = Rg.tile("mg_hi", [P, KT, N], F32R)
        mg_lo = Rg.tile("mg_lo", [P, KT, N], F32R)
        th = Rg.tile("th", [P, 3, N])
        mg = Rg.tile("mg", [P, 2, N])
        mt = Rg.tile("mt", [P, 2, N])
        Rm = Region(start_h, 2 * 4 * KT * N)
        ht_hi = Rm.tile("ht_hi", [P, NT, D], F32R)
        ht_lo = Rm.tile("ht_lo", [P, NT, D], F32R)
        Rm = Region(start_b, 4 * 16 * N)
        sel = Rm.tile("sel", [P, NT, P], F32R)
        selT = Rm.tile("selT", [P, N], F32R)
        hg_hi = Rm.tile("hg_hi", [P, KT, P], F32R)
        hg_lo = Rm.tile("hg_lo", [P, KT, P], F32R)
        hd_hi = Rm.tile("hd_hi", [P, 2, P], F32R)
        hd_lo = Rm.tile("hd_lo", [P, 2, P], F32R)
        Rm = Region(start_x)
        y_hi = Rm.tile("y_hi", [P, D], F32R)
        y_lo = Rm.tile("y_lo", [P, D], F32R)
        hg32 = Rm.tile("hg32", [P, D])
        th_e = Rm.tile("th_e", [P, 2, EH])
        s_e = Rm.tile("s_e", [P, 2, EH])
        hid = Rm.tile("hid", [P, 2, EH])
        out_t = Rm.tile("out_t", [P, 2, D])
        junk = Rm.tile("junk", [P, D])
        fg_b = Rm.tile("fg_b", [P, D])
        Rm = Region(start_x + 6 * 4 * KT * N // 2)
        h2T = Rm.tile("h2T", [P, KT, N])
        lgT = Rm.tile("lgT", [GROUPS + NE, N])
        lg = Rm.tile("lg", [P, NT, GROUPS + NE])
        og = Rm.tile("og", [P, NT, GROUPS])
        pr = Rm.tile("pr", [P, NT, EPG, GROUPS])
        e_sel = Rm.tile("e_sel", [P, NT, EPG])
        o1 = Rm.tile("o1", [P, NT, EPG])
        o2 = Rm.tile("o2", [P, NT, EPG])
        comb = Rm.tile("comb", [P, NT, EPG])
        rk = Rm.tile("rk", [P, NT, GROUPS])
        key = Rm.tile("key", [P, NT])
        i_base = Rm.tile("i_base", [P, 16])
        keysh = Rm.tile("keysh", [P, 16, NT])
        goff = Rm.tile("goff", [P, GROUPS])
        tot = Rm.tile("tot", [P, NT, GROUPS])
        cmb = Rm.tile("cmb", [P, EPG])
        over = Rm.tile("over", [P, 1], I32)
        fin = Rm.tile("fin", [P, 8])

        ps = ctx.enter_context(nc.psum_tensor("ps", [P, 8, 512], F32))

        def sem(name):
            return ctx.enter_context(nc.semaphore(name))

        raw_ready = [sem(f"raw_ready{i}") for i in range(RING)]
        hi_ready, lo_ready, chunk_done = sem("hi_ready"), sem("lo_ready"), sem("chunk_done")
        rows_in, taps_in, x_in, ck_in, cv_in, dft_in, bias_in, gr_in, fg_in = (
            sem(n) for n in ("rows_in", "taps_in", "x_in", "ck_in", "cv_in", "dft_in", "bias_in", "gr_in", "fg_in"))
        ident_step, consts_ready, mask_step, pool_step = (
            sem(n) for n in ("ident_step", "consts_ready", "mask_step", "pool_step"))
        vec_turned, vec_ready, cond_tanh, cond_ready = (
            sem(n) for n in ("vec_turned", "vec_ready", "cond_tanh", "cond_ready"))
        x_turned, x_ready, sq_ready, ssq_step, std_ready, norm_ready = (
            sem(n) for n in ("x_turned", "x_ready", "sq_ready", "ssq_step", "std_ready", "norm_ready"))
        modrow_ready, mod_turned, mod_copied, mod_ready = (
            sem(n) for n in ("modrow_ready", "mod_turned", "mod_copied", "mod_ready"))
        h32_ready, h_hi_ready, h_ready = sem("h32_ready"), sem("h_hi_ready"), sem("h_ready")
        q_ready, k_ready, ck_turned, ck_ready, kctx_turned, kout_ready, store_k, store_v, u_ready, v_ready = (
            sem(n) for n in ("q_ready", "k_ready", "ck_turned", "ck_ready", "kctx_turned", "kout_ready", "store_k",
                             "store_v", "u_ready", "v_ready"))
        fnet_pos, z_ready, fnet_feat, fn_hi_ready, fn_ready = (
            sem(n) for n in ("fnet_pos", "z_ready", "fnet_feat", "fn_hi_ready", "fn_ready"))
        glu_tanh, zpad_zero, z_conv, conv_done, ln_mean, ln_centred, ln_sq, ln_var, ln_std, ln_out, ln_tanh = (
            sem(n) for n in ("glu_tanh", "zpad_zero", "z_conv", "conv_done", "ln_mean", "ln_centred", "ln_sq",
                             "ln_var", "ln_std", "ln_out", "ln_tanh"))
        silu_ready, cv_hi_ready, cv_ready = sem("silu_ready"), sem("cv_hi_ready"), sem("cv_ready")
        scores, negmax, exps, probs_ready, turned, turned_out, pv_done, at_hi_ready, at_ready = (
            sem(n) for n in ("scores", "negmax", "exps", "probs_ready", "turned", "turned_out", "pv_done",
                             "at_hi_ready", "at_ready"))
        gate_tanh, merged, mg_hi_ready, mg_ready, x1_ready, h2_ready = (
            sem(n) for n in ("gate_tanh", "merged", "mg_hi_ready", "mg_ready", "x1_ready", "h2_ready"))
        logits, logits_out, logits_turned, h2_turned, ht_hi_ready, ht_ready, grp_shift, grp_exp, exp_gap, exp2 = (
            sem(n) for n in ("logits", "logits_out", "logits_turned", "h2_turned", "ht_hi_ready", "ht_ready",
                             "grp_shift", "grp_exp", "exp_gap", "exp2"))
        group_hot, ranks, routed = sem("group_hot"), sem("ranks"), sem("routed")
        sel_ready, gathered, hg_out, hg_turned, hg_hi_ready, hg_ready, sel_turned, selT_ready, cmb_ready = (
            sem(n) for n in ("sel_ready", "gathered", "hg_out", "hg_turned", "hg_hi_ready", "hg_ready",
                             "sel_turned", "selT_ready", "cmb_ready"))
        silu_e, x2_ready = sem("silu_e"), sem("x2_ready")
        e_tanh, hid_ready, hid_turned, hd_hi_ready, hd_ready, y_hi_ready, y_ready, combined, added = (
            sem(n) for n in ("e_tanh", "hid_ready", "hid_turned", "hd_hi_ready", "hd_ready", "y_hi_ready",
                             "y_ready", "combined", "added"))
        out_turned, out_std, out_ready = sem("out_turned"), sem("out_std"), sem("out_ready")
        store_y = [sem(f"store_y{t}") for t in range(NT)]
        act_step, dve_step = sem("act_step"), sem("dve_step")

        w_mod_v = w_mod[0].rearrange("(k p) c -> p k c", p=P)
        w_in_v = w_in[0].rearrange("(k p) c -> p k c", p=P)
        w_out_v = w_out[0].rearrange("(k p) c -> p k c", p=P)
        w_at_v = w_attn_o[0].rearrange("(k p) c -> p k c", p=P)
        w_fn_v = w_fnet[0].rearrange("(k p) c -> p k c", p=P)
        w_cv_v = w_conv_o[0].rearrange("(k p) c -> p k c", p=P)
        w1_v = w1[0].rearrange("e (k p) f -> e p k f", p=P)
        w3_v = w3[0].rearrange("e (k p) f -> e p k f", p=P)
        w2_v = w2[0].rearrange("e (k p) d -> e p k d", p=P)

        def slot_loads(kind, j, r):
            full = raw[:, r, :].rearrange("p (k c) -> p k c", k=KT)
            halves = raw[:, r, :].rearrange("p (h k c) -> p h k c", h=2, k=KT)
            if kind == "mod":
                return [(full, w_mod_v[:, :, 256 * j:256 * j + 256])]
            if kind in ("q", "k", "v", "uf"):
                c0 = {"q": COL_Q, "k": COL_K, "v": COL_V, "uf": COL_F}[kind] + 256 * j
                return [(full, w_in_v[:, :, c0:c0 + 256])]
            if kind == "uc":
                return [(full[:, :, 128 * i:128 * i + 128], w_in_v[:, :, COL_C + CW * i + P * j:COL_C + CW * i + P * j + P])
                        for i in range(2)]
            cols = slice(P * j, P * j + P)
            gate = lambda b: w_in_v[:, :, COL_G + D * b + P * j:COL_G + D * b + P * j + P]
            if kind == "br":
                return [(halves[:, 0, 0:4, :], w_at_v[:, :, cols]), (halves[:, 0, 4:6, :], w_fn_v[:, :, cols]),
                        (halves[:, 0, 6:8, :], w_cv_v[:, :, cols]), (halves[:, 1, :, :], gate(0))]
            if kind == "g12":
                return [(halves[:, i, :, :], gate(1 + i)) for i in range(2)]
            return [(full, w_out_v[:, :, 256 * j:256 * j + 256])]

        def item_loads(kind, e, g, r):
            ex = bass.ds(g * EPG + e, 1)
            if kind == "C":
                return [(raw[:, r, :].rearrange("p (k c) -> p k c", k=2), w2_v[ex].rearrange("e p k d -> (e p) k d"))]
            full = raw[:, r, :].rearrange("p (k w c) -> p k w c", k=4, w=2)
            ks = slice(0, 4) if kind == "A" else slice(4, 8)
            return [(full[:, :, i, :], w[ex].rearrange("e p k f -> (e p) k f")[:, ks, :]) for i, w in enumerate((w1_v, w3_v))]

        N_LOADS = {"mod": 1, "q": 1, "k": 1, "v": 1, "uf": 1, "uc": 2, "br": 4, "g12": 2, "wo": 1, "A": 2, "B": 2, "C": 1}
        seen = [0] * RING
        pre_count = []
        for s, (kind, j) in enumerate(SLOTS):
            seen[s % RING] += 16 * N_LOADS[kind]
            pre_count.append(seen[s % RING])
        per_item = [0] * RING
        item_count = []
        for s, (kind, e) in enumerate(ITEM):
            r = (PRE + s) % RING
            per_item[r] += 16 * N_LOADS[kind]
            item_count.append(seen[r] + per_item[r])

        def raw_chunk(slot_kind, r, half):
            if slot_kind in BY_COLUMNS:
                return raw[:, r, :].rearrange("p (k c) -> p k c", k=KT)[:, :, P * half:P * half + P]
            return raw[:, r, CH * half:CH * half + CH]

        def cut_chunk(t, slot_kind, b):
            return t[:, b, :].rearrange("p (k c) -> p k c", k=KT) if slot_kind in BY_COLUMNS else t[:, b, :]

        def act_split(act, i):
            kind, r = SLOTS[i // 2][0], (i // 2) % RING
            if i % 2 == 0:
                act.wait_ge(raw_ready[r], pre_count[i // 2])
            if i >= SPLIT:
                act.wait_ge(chunk_done, i - SPLIT + 1)
            act.activation(cut_chunk(w_hi, kind, i % SPLIT), raw_chunk(kind, r, i % 2), ACT.Copy).then_inc(hi_ready, 1)

        def dve_split(dve, i):
            kind, r = SLOTS[i // 2][0], (i // 2) % RING
            dve.wait_ge(hi_ready, i + 1)
            dve.tensor_tensor(cut_chunk(w_lo, kind, i % SPLIT), raw_chunk(kind, r, i % 2),
                              cut_chunk(w_hi, kind, i % SPLIT).bitcast(F32), ALU.subtract).then_inc(lo_ready, 1)

        def act_split_item(act, it, i):
            r, b = (PRE + i // 2) % RING, (PRE_CH + i) % SPLIT
            if i % 2 == 0:
                act.wait_ge(raw_ready[r], it * per_item[r] + item_count[i // 2])
            act.wait_ge(chunk_done, it * ITEM_CH + (PRE_CH + i - SPLIT + 1))
            act.activation(w_hi[:, b, :], raw[:, r, CH * (i % 2):CH * (i % 2) + CH], ACT.Copy).then_inc(hi_ready, 1)

        def dve_split_item(dve, it, i):
            r, b = (PRE + i // 2) % RING, (PRE_CH + i) % SPLIT
            dve.wait_ge(hi_ready, it * ITEM_CH + (PRE_CH + i + 1))
            dve.tensor_tensor(w_lo[:, b, :], raw[:, r, CH * (i % 2):CH * (i % 2) + CH], w_hi[:, b, :].bitcast(F32),
                              ALU.subtract).then_inc(lo_ready, 1)

        up_chunks, down_chunks, order = {}, {}, []
        for s, (kind, e) in enumerate(ITEM):
            (down_chunks if kind == "C" else up_chunks).setdefault(e, []).extend([2 * s, 2 * s + 1])
        for s, (kind, e) in enumerate(ITEM):
            for half in range(2):
                order.append(("down" if kind == "C" else "up", e, (2 if kind == "B" else 0) + half, 2 * s + half))

        def rounds(eng, item):
            with eng.Fori(0, GROUPS) as g:
                item(g, g)
            eng.wait_ge(routed, 1)
            n_over = eng.value_load(over[0:1, 0:1])
            with eng.If(n_over > 0):
                with eng.Fori(1, ROUNDS) as r:
                    with eng.Fori(0, GROUPS) as g:
                        item(r * GROUPS + g, g)

        block = ctx.enter_context(nc.Block())

        @block.sync
        def _(sp):
            for t in range(NT):
                src = x_prompt[0] if t == 0 else x_sample[0, (t - 1) * P:t * P, :]
                sp.dma_start(x_tok[:, t, :], src).then_inc(x_in, 16)
            for s, (kind, j) in enumerate(SLOTS):
                if s >= RING:
                    sp.wait_ge(lo_ready, 2 * (s - RING) + 2)
                for dst, src in slot_loads(kind, j, s % RING):
                    sp.dma_start(dst, src).then_inc(raw_ready[s % RING], 16)

            def item(it, g):
                for s, (kind, e) in enumerate(ITEM):
                    sp.wait_ge(lo_ready, it * ITEM_CH + 2 * (PRE + s - RING) + 2)
                    r = (PRE + s) % RING
                    for dst, src in item_loads(kind, e, g, r):
                        sp.dma_start(dst, src).then_inc(raw_ready[r], 16)

            rounds(sp, item)
            for t in range(NT):
                dst = y_prompt[0] if t == 0 else y_sample[0, (t - 1) * P:t * P, :]
                sp.wait_ge(out_ready, t + 1)
                sp.dma_start(dst, out_t[:, t % 2, :]).then_inc(store_y[t], 16)
            for t in range(NT):
                sp.wait_ge(store_y[t], 16)
            sp.wait_ge(store_k, 16)
            sp.wait_ge(store_v, 16)

        @block.gpsimd
        def _(pool):
            pool.memset(ident[:], 0.0).then_inc(ident_step, 1)
            pool.memset(tri[:], 1.0).then_inc(ident_step, 1)
            pool.wait_ge(ident_step, 2)
            pool.affine_select(out=ident[:], in_=ident[:], compare_op=ALU.not_equal, fill=1.0, base=0,
                               pattern=[[-1, P]], channel_multiplier=1).then_inc(consts_ready, 1)
            pool.memset(ones[:], 1.0).then_inc(consts_ready, 1)
            pool.memset(eps_t[:], EPS).then_inc(consts_ready, 1)
            pool.affine_select(out=tri[:], in_=tri[:], compare_op=ALU.is_gt, fill=0.0, base=0,
                               pattern=[[1, P]], channel_multiplier=-1).then_inc(consts_ready, 1)
            pool.iota(iota_s[:], pattern=[[1, P]], base=0, channel_multiplier=0,
                      allow_small_or_imprecise_dtypes=True).then_inc(consts_ready, 1)
            pool.wait_ge(bias_in, 16 * 2 * HEADS)
            for half in range(2):
                b = bias[64 * half:64 * half + 64].rearrange("p h s c -> p (h s) c")
                lo, hi = b[:, :, 0:GRID_W - 16], b[:, :, 16:GRID_W]
                pool.affine_select(out=lo, in_=lo, compare_op=ALU.is_ge, fill=NEG, base=8,
                                   pattern=[[0, HEADS * NDR], [1, GRID_W - 16]], channel_multiplier=-1)\
                    .then_inc(mask_step, 1)
                pool.wait_ge(mask_step, 2 * half + 1)
                pool.affine_select(out=hi, in_=hi, compare_op=ALU.is_ge, fill=NEG, base=7 - 16,
                                   pattern=[[0, HEADS * NDR], [-1, GRID_W - 16]], channel_multiplier=1)\
                    .then_inc(mask_step, 1)
            pool.wait_ge(z_conv, 2)
            step = 0
            for t in range(CK):
                if t == 0:
                    pool.tensor_scalar(acc[:, 1, :], zpad[:, 1, 0:CO], taps[:, 1, 0:1], vec_t[:, V_CB + 1:V_CB + 2],
                                       ALU.mult, ALU.add).then_inc(pool_step, 1)
                    step += 1
                    continue
                pool.tensor_scalar(prod[:], zpad[:, 1, t:t + CO], taps[:, 1, t:t + 1], None, ALU.mult)\
                    .then_inc(pool_step, 1)
                step += 1
                pool.wait_ge(pool_step, step)
                pool.tensor_tensor(acc[:, 1, :], acc[:, 1, :], prod[:], ALU.add)\
                    .then_inc(conv_done if t == CK - 1 else pool_step, 1)
                if t < CK - 1:
                    step += 1
                    pool.wait_ge(pool_step, step)
            pool.wait_ge(mg_ready, KT)
            pool.iota(i_base[:], pattern=[[P, 4], [N, 4]], base=0, channel_multiplier=0,
                      allow_small_or_imprecise_dtypes=True).then_inc(consts_ready, 1)
            pool.iota(goff[:], pattern=[[N, GROUPS]], base=0, channel_multiplier=0,
                      allow_small_or_imprecise_dtypes=True).then_inc(consts_ready, 1)

        @block.scalar
        def _(act):
            rows = 0
            for at, src, n in ((V_CTX, c_ctx, 8), (V_C, c[0], 8), (V_N1, norm1_g[0], 8), (V_N2, norm2_g[0], 8),
                               (V_BM, b_mod[0], 48), (V_CB, conv_b[0], 2), (V_LG, conv_ln_g[0], 2), (V_LB, conv_ln_b[0], 2)):
                act.dma_start(vec_rows[at:at + n, :], src.rearrange("(a p) -> a p", p=P)).then_inc(rows_in, 16)
                rows += 16
            for i in range(2):
                act.dma_start(tap_rows[CK * i:CK * i + CK, :], conv_dw[0, :, P * i:P * i + P]).then_inc(taps_in, 16)
            act.dma_start(ck_tok[:], cache_k[0, 0].rearrange("h n d -> n h d")).then_inc(ck_in, 16)
            act.dma_start(cv_tok[:], cache_v[0, 0].rearrange("h n d -> n h d")).then_inc(cv_in, 16)
            for half in range(2):
                for h in range(HEADS):
                    at = (h * RPB_R + 5 - half) * RPB_C * GRID_W + 15
                    act.dma_start(bias[64 * half:64 * half + 64, h, :, :],
                                  bass.AP(rpb.tensor, at, [[RPB_C - 1, 64], [RPB_C * GRID_W, NDR], [1, GRID_W]])).then_inc(bias_in, 16)
            act.dma_start(w_gr[:, :, 0:GROUPS], w_group[0].rearrange("(k p) g -> p k g", p=P)).then_inc(gr_in, 16)
            act.dma_start(w_gr[:, :, GROUPS:], w_router[0].rearrange("(k p) g -> p k g", p=P)).then_inc(gr_in, 16)
            act.dma_start(b_gr[:, 0:GROUPS], b_group.to_broadcast([P, GROUPS])).then_inc(gr_in, 16)
            act.dma_start(b_gr[:, GROUPS:], b_router.to_broadcast([P, NE])).then_inc(gr_in, 16)

            step = 0

            def link(ins):
                nonlocal step
                step += 1
                ins.then_inc(act_step, 1)
                act.wait_ge(act_step, step)

            split_at = 0

            def split_to(n):
                nonlocal split_at
                while split_at < min(n, PRE_CH):
                    act_split(act, split_at)
                    split_at += 1

            act.wait_ge(vec_ready, 1)
            act.activation(cond_t[:].rearrange("p a k -> p (a k)"), vec_t[:, V_CTX:V_CTX + 16], ACT.Tanh, scale=0.5)\
                .then_inc(cond_tanh, 1)

            def square(n, src):
                if n >= 2:
                    act.wait_ge(ssq_step, n - 1)
                act.activation(sq[:, n % 2, :], src, ACT.Square).then_inc(sq_ready, 1)

            def std(n, bank):
                act.wait_ge(ssq_step, KT * (n + 1))
                act.activation(rstd[:], ps[:, bank, 0:N], ACT.Sqrt, bias=eps_t[:, 0:1], scale=1.0 / D)\
                    .then_inc(std_ready, 1)

            act.wait_ge(consts_ready, 3)
            for k in range(KT):
                act.wait_ge(x_ready, k + 1)
                square(k, xT[:, k, :])
            split_to(4)
            std(0, 7)
            for a in range(2):
                act.dma_start(lat_w[:, a, :], dft_lat[P * a:P * a + P, :]).then_inc(dft_in, 16)
            act.dma_start(ctx_w[:], dft_ctx).then_inc(dft_in, 16)
            act.dma_start(feat_w[:].rearrange("p a c -> p (a c)"), dft_feat).then_inc(dft_in, 16)

            def mod_row(j, c0):
                act.wait_ge(chunk_done, c0 + 2)
                if j >= 2:
                    act.wait_ge(mod_turned, j - 1)
                bank = j % 2 if j < 8 else 5 + j % 2
                act.activation(modrow[:, j % 2, :], ps[0:4, bank, 0:256], ACT.Copy).then_inc(modrow_ready, 1)

            for j in range(8):
                split_to(2 * j + 4)
                mod_row(j, 2 * j)
                split_to(2 * j + 5)
            for k in range(KT):
                act.wait_ge(h32_ready, k + 1)
                act.activation(h_hi[:, k, :], h32[:, k, :], ACT.Copy).then_inc(h_hi_ready, 1)
            c_q, c_k = first_chunk("q"), first_chunk("k")
            for n in range(4):
                split_to(c_q + n + 4)
                act.wait_ge(chunk_done, c_q + n + 1)
                if n == 0:
                    act.wait_ge(h_ready, KT)
                act.activation(qT[:, n, :], ps[:, n % 2, 0:N], ACT.Copy, scale=HD ** -0.5).then_inc(q_ready, 1)
            for n in range(4):
                split_to(c_k + n + 4)
            act.wait_ge(ck_turned, 1)
            act.activation(ckT[:].rearrange("p a n -> p (a n)"), ps[:, 5, :], ACT.Copy).then_inc(ck_ready, 1)
            act.wait_ge(kout_ready, 1)
            act.dma_start(new_k[0, 0].rearrange("h n d -> n h d"), k_out[:].rearrange("p (h d) -> p h d", h=HEADS))\
                .then_inc(store_k, 16)

            def exp_unit(u):
                b, part = u % 3, u % 3
                act.wait_ge(negmax, u + 1)
                if part == 0:
                    act.activation(probs[:, b, 0:NCTX], ps[:, 3 + u % 2, 0:NCTX], ACT.Exp, bias=stats[:, b, 2:3],
                                   accum_out=stats[:, b, 3:4]).then_inc(exps, 1)
                else:
                    act.activation(probs[:, b, 0:NLAT], probs[:, b, 0:NLAT], ACT.Exp, bias=stats[:, b, 2:3],
                                   accum_out=stats[:, b, 3:4])
                    act.activation(probs[:, b, NLAT:N], ps[:, 3 + u % 2, NLAT:N], ACT.Exp, bias=stats[:, b, 2:3],
                                   accum_out=stats[:, b, 4:5]).then_inc(exps, 1)

            def turned_copy(u):
                h, part = u // 3, u % 3
                act.wait_ge(turned, u + 1)
                if h >= 1:
                    act.wait_ge(pv_done, h)
                if part == 0:
                    act.activation(ptc[:], ps[:, 5 + u % 2, 0:P], ACT.Copy).then_inc(turned_out, 1)
                else:
                    act.activation(ptl[:, :, part - 1, :], ps[:, 5 + u % 2, 0:3 * P].rearrange("p (a q) -> p a q", a=3),
                                   ACT.Copy).then_inc(turned_out, 1)

            for what, n in WINDOW:
                if what == "chunk":
                    kind, j = SLOTS[n // 2]
                    split_to(n + 4)
                    if kind == "uc" and n % 2 == 1:
                        act.wait_ge(chunk_done, n + 1)
                        act.wait_ge(zpad_zero, 1)
                        act.activation(csq[:, j, 0:N], ps[:, 1, 0:N], ACT.Tanh, scale=0.5).then_inc(glu_tanh, 1)
                elif what == "fnet":
                    act.wait_ge(fnet_pos, 2 * n + 1)
                    if n == 1:
                        act.wait_ge(fnet_feat, 1)
                    act.activation(z_cs[:, :, 0:NCTX], ps[:, 0, 0:2 * NCTX].rearrange("p (a n) -> p a n", a=2), ACT.Copy)
                    act.wait_ge(fnet_pos, 2 * n + 2)
                    act.activation(z_cs[:, :, NCTX:N], ps[:, 1, 0:2 * NLAT].rearrange("p (a n) -> p a n", a=2), ACT.Copy)\
                        .then_inc(z_ready, 1)
                    act.wait_ge(fnet_feat, n + 1)
                    act.activation(fn_hi[:, n, :], ps[:, 2, 0:N], ACT.Copy).then_inc(fn_hi_ready, 1)
                elif what == "unit" and n < UNITS:
                    exp_unit(n)
                elif what == "turn" and 0 <= n:
                    turned_copy(n)
                    if n % 6 == 5:
                        pair = n // 6
                        act.wait_ge(pv_done, 2 * pair + 2)
                        act.activation(at_hi[:, pair, :], ps[:, 7, 0:N], ACT.Copy).then_inc(at_hi_ready, 1)
            act.wait_ge(v_ready, 2)
            act.dma_start(new_v[0, 0].rearrange("h n d -> n h d"), v_tok[:, 0, :].rearrange("p (h d) -> p h d", h=HEADS))\
                .then_inc(store_v, 16)
            act.wait_ge(ln_centred, 1)
            act.activation(csq[:], acc[:], ACT.Square).then_inc(ln_sq, 1)
            act.wait_ge(ln_var, 1)
            act.activation(crs[:], ps[:, 1, 0:CO], ACT.Sqrt, bias=eps_t[:, 0:1], scale=1.0 / CW).then_inc(ln_std, 1)
            act.wait_ge(ln_out, 1)
            act.activation(csq[:], acc[:], ACT.Tanh, scale=0.5).then_inc(ln_tanh, 1)
            act.wait_ge(silu_ready, 1)
            act.wait_ge(store_k, 16)
            for at, o in ((0, 0), (LAT0, NCTX)):
                w = NCTX if o == 0 else NLAT
                act.activation(cv_hi[:, :, o:o + w], acc[:, :, at:at + w], ACT.Copy, scale=0.5).then_inc(cv_hi_ready, 1)

            for d in range(KT):
                c0 = 2 * (UG0 + 4 * d)
                for b in range(3):
                    split_to(c0 + 1 + b + 4)
                    act.wait_ge(chunk_done, c0 + 2 + b)
                    if d >= 1:
                        act.wait_ge(merged, d)
                    else:
                        act.wait_ge(store_v, 16)
                    act.activation(th[:, b, :], ps[:, 3 + (3 * d + b) % 2, 0:N], ACT.Tanh, scale=0.5).then_inc(gate_tanh, 1)
                for i in range(2):
                    split_to(c0 + 4 + 2 * i + 4)
                    mod_row(8 + 2 * d + i, c0 + 4 + 2 * i)
                    split_to(c0 + 4 + 2 * i + 5)
                    if i == 0:
                        act.wait_ge(merged, d + 1)
                        act.activation(mg_hi[:, d, :], mg[:, d % 2, :], ACT.Copy, scale=0.5).then_inc(mg_hi_ready, 1)
            for n in range(KT):
                split_to(2 * WO0 + n + 4)
                act.wait_ge(x1_ready, n + 1)
                square(KT + n, xT[:, n, :])
            std(1, 2)
            act.wait_ge(logits, 1)
            act.activation(lgT[:], ps[0:GROUPS + NE, 3, 0:N], ACT.Copy).then_inc(logits_out, 1)
            tok_banks = (0, 4, 6)
            for t in range(NT):
                act.wait_ge(h2_turned, t + 1)
                act.activation(ht_hi[:, t, :], ps[:, tok_banks[t]:tok_banks[t] + 2, :].rearrange("p a n -> p (a n)"),
                               ACT.Copy).then_inc(ht_hi_ready, 1)
            act.wait_ge(grp_shift, 1)
            act.activation(rt[:, :, 8:12], rt[:, :, 4:8], ACT.Exp).then_inc(grp_exp, 1)
            act.wait_ge(exp_gap, 1)
            act.activation(rt[:, :, 21:22], rt[:, :, 20:21], ACT.Exp).then_inc(exp2, 1)

            def hg_copy(nx):
                act.wait_ge(gathered, nx + 1)
                act.activation(hg32[:], ps[:, 5:7, :].rearrange("p a n -> p (a n)"), ACT.Copy).then_inc(hg_out, 1)

            def hg_high(nx):
                act.wait_ge(hg_turned, nx + 1)
                act.activation(hg_hi[:].rearrange("p k s -> p (k s)"), ps[:, 5:7, :].rearrange("p a n -> p (a n)"),
                               ACT.Copy).then_inc(hg_hi_ready, 1)

            hg_copy(0)
            hg_high(0)
            act.dma_start(fg_b[:], final_g.rearrange("(a n) -> a n", a=1).to_broadcast([P, D])).then_inc(fg_in, 16)

            def item(it, g):
                for i in range(3):
                    act_split_item(act, it, i)
                act.wait_ge(sel_turned, it + 1)
                act.activation(cmb[:], ps[:, 7, 0:EPG], ACT.Copy).then_inc(cmb_ready, 1)
                act.activation(selT[:], ps[:, 7, P:4 * P], ACT.Copy).then_inc(selT_ready, 1)

                def tanh_e(e):
                    act.wait_ge(chunk_done, it * ITEM_CH + PRE_CH + up_chunks[e][3] + 1)
                    if e >= 2:
                        act.wait_ge(hid_ready, it * EPG + e - 1)
                    act.activation(th_e[:, e % 2, :], ps[:, e % 2, 0:EH], ACT.Tanh, scale=0.5).then_inc(e_tanh, 1)

                def hd_high(e):
                    act.wait_ge(hid_turned, it * EPG + e + 1)
                    act.activation(hd_hi[:].rearrange("p a n -> p (a n)"), ps[:, 4, 0:2 * P], ACT.Copy).then_inc(hd_hi_ready, 1)

                for what, e, part, i in order:
                    if i + 3 < ITEM_CH:
                        act_split_item(act, it, i + 3)
                    if what == "up" and part == 0 and e >= 1:
                        tanh_e(e - 1)
                    if what == "up" and part == 3 and e >= 1:
                        hd_high(e - 1)
                    if what == "up" and part == 3 and e == EPG - 1:
                        hg_copy(it + 1)
                    if what == "down" and part == 0 and e == EPG - 2:
                        tanh_e(EPG - 1)
                hg_high(it + 1)
                hd_high(EPG - 1)
                act.wait_ge(chunk_done, it * ITEM_CH + PRE_CH + ITEM_CH)
                act.activation(y_hi[:], ps[:, 2:4, :].rearrange("p a n -> p (a n)"), ACT.Copy).then_inc(y_hi_ready, 1)

            rounds(act, item)
            out_banks = (0, 2, 5)
            for t in range(NT):
                act.wait_ge(out_turned, t + 1)
                link(act.activation(junk[:], ps[:, out_banks[t]:out_banks[t] + 2, :].rearrange("p a n -> p (a n)"),
                                    ACT.Square, accum_out=fin[:, t:t + 1]))
            act.activation(fin[:, 3:6], fin[:, 0:3], ACT.Sqrt, bias=eps_t[:, 0:1], scale=1.0 / D).then_inc(out_std, 1)

        @block.vector
        def _(dve):
            step = 0

            def link(ins):
                nonlocal step
                step += 1
                ins.then_inc(dve_step, 1)
                dve.wait_ge(dve_step, step)

            split_at = 0

            def split_to(n):
                nonlocal split_at
                while split_at < min(n, PRE_CH):
                    dve_split(dve, split_at)
                    split_at += 1

            dve.wait_ge(vec_turned, 1)
            dve.tensor_copy(vec_t[:], ps[:, 3, 0:V_ROWS]).then_inc(vec_ready, 1)
            dve.wait_ge(vec_turned, 2)
            link(dve.tensor_scalar(taps[:].rearrange("p a t -> p (a t)"), ps[:, 2, 0:2 * CK], 0.5, None, ALU.mult))
            dve.wait_ge(cond_tanh, 1)
            both = cond[:].rearrange("p a k -> p (a k)")
            link(dve.scalar_tensor_tensor(out=both, in0=cond_t[:].rearrange("p a k -> p (a k)"), scalar=1.0,
                                          in1=vec_t[:, V_CTX:V_CTX + 16], op0=ALU.add, op1=ALU.mult))
            link(dve.tensor_scalar(both, both, 0.5, None, ALU.mult))
            link(dve.tensor_copy(cond4[:, :, 0:2], cond[:].rearrange("p a k -> p k a")))
            dve.tensor_tensor(cond4[:, :, 2:4], cond[:].rearrange("p a k -> p k a"), cond4[:, :, 0:2].bitcast(F32),
                              ALU.subtract).then_inc(cond_ready, 1)
            for k in range(KT):
                dve.wait_ge(x_turned, k + 1)
                dve.tensor_copy(xT[:, k, :], ps[:, 4 + k % 3, 0:N]).then_inc(x_ready, 1)
            dve.wait_ge(std_ready, 1)
            link(dve.reciprocal(rstd[:], rstd[:]))
            for k in range(KT):
                split_to(2 * k + 4)
                dve.tensor_tensor(h32[:, k, :], xT[:, k, :], rstd[:], ALU.mult)
                split_to(2 * k + 5)

            def mod_finish(first, n, bank):
                link(dve.tensor_copy(mod_tmp[:, 0:n, :], ps[:, bank, 4 * first:4 * (first + n)]
                                     .rearrange("p (t r) -> p t r", r=4)))
                m = modT[:, first:first + n, :]
                link(dve.tensor_tensor(m, mod_tmp[:, 0:n, 0:2], mod_tmp[:, 0:n, 2:4], ALU.add))
                for a in range(2):
                    ins = dve.tensor_tensor(modT[:, first:first + n, a], modT[:, first:first + n, a],
                                            vec_t[:, V_BM + first:V_BM + first + n], ALU.add)
                    link(ins)

            def norm_scale(dst, mod, vec):
                for a in range(2):
                    link(dve.scalar_tensor_tensor(out=dst[:, :, a], in0=modT[:, 8 * mod:8 * mod + 8, a], scalar=1.0,
                                                  in1=vec_t[:, vec:vec + 8], op0=ALU.add, op1=ALU.mult))

            def modulate(k, t, scale, shift):
                for a, b, which in SEG:
                    ins = dve.tensor_scalar(t[:, k, a:b], t[:, k, a:b], scale[:, k, which:which + 1],
                                            modT[:, 8 * shift + k, which:which + 1], ALU.mult, ALU.add)
                return ins

            dve.wait_ge(mod_turned, 8)
            mod_finish(0, 16, 2)
            norm_scale(scale1, 1, V_N1)
            for k in range(KT):
                modulate(k, h32, scale1, 0).then_inc(h32_ready, 1)
            for k in range(KT):
                dve.wait_ge(h_hi_ready, k + 1)
                dve.tensor_tensor(h_lo[:, k, :], h32[:, k, :], h_hi[:, k, :].bitcast(F32), ALU.subtract).then_inc(h_ready, 1)
            c_q, c_k = first_chunk("q"), first_chunk("k")
            for n in range(4):
                split_to(c_q + n + 4)
            dve.wait_ge(h_ready, KT)
            for n in range(4):
                split_to(c_k + n + 4)
                dve.wait_ge(chunk_done, c_k + n + 1)
                dve.tensor_copy(kT[:, n, :], ps[:, n % 2, 0:N]).then_inc(k_ready, 1)
            dve.wait_ge(kctx_turned, 1)
            dve.tensor_copy(k_out[:], ps[:, 6, :]).then_inc(kout_ready, 1)

            def max_unit(u):
                b, part, h = u % 3, u % 3, u // 3
                dve.wait_ge(scores, u + 1)
                if u >= 3:
                    dve.wait_ge(turned, u - 2)
                s = ps[:, 3 + u % 2, :]
                if part == 0:
                    link(dve.reduce_max(stats[:, b, 0:1], s[:, 0:NCTX], AX))
                    dve.tensor_scalar(stats[:, b, 2:3], stats[:, b, 0:1], -1.0, None, ALU.mult).then_inc(negmax, 1)
                    return
                t = part - 1
                if u == 1:
                    dve.wait_ge(mask_step, 4)
                rows = bias[:, h, 2 - 2 * t:6 - 2 * t, :].rearrange("p s c -> p (s c)")
                dve.reduce_max(stats[:, b, 0:1], s[:, NLAT:N], AX)
                link(dve.tensor_tensor_reduce(out=probs[:, b, 0:NLAT], in0=s[:, 0:NLAT], in1=rows, scale=1.0,
                                              scalar=-3e38, op0=ALU.add, op1=ALU.max, accum_out=stats[:, b, 1:2]))
                dve.tensor_scalar(stats[:, b, 2:3], stats[:, b, 0:1], stats[:, b, 1:2], -1.0, ALU.max, ALU.mult)\
                    .then_inc(negmax, 1)

            def normalise_unit(u):
                b, part = u % 3, u % 3
                dve.wait_ge(exps, u + 1)
                total, w = stats[:, b, 3:4], NCTX
                if part:
                    link(dve.tensor_tensor(stats[:, b, 5:6], stats[:, b, 3:4], stats[:, b, 4:5], ALU.add))
                    total, w = stats[:, b, 5:6], N
                link(dve.reciprocal(stats[:, b, 6:7], total))
                dve.tensor_scalar(probs[:, b, 0:w], probs[:, b, 0:w], stats[:, b, 6:7], None, ALU.mult)\
                    .then_inc(probs_ready, 1)

            conv_t = 0

            def conv_taps(n):
                nonlocal conv_t
                for _ in range(n):
                    if conv_t == CK:
                        return
                    t = conv_t
                    if t == 0:
                        ins = dve.tensor_scalar(acc[:, 0, :], zpad[:, 0, 0:CO], taps[:, 0, 0:1], vec_t[:, V_CB:V_CB + 1],
                                                ALU.mult, ALU.add)
                    else:
                        ins = dve.scalar_tensor_tensor(out=acc[:, 0, :], in0=zpad[:, 0, t:t + CO], scalar=taps[:, 0, t:t + 1],
                                                       in1=acc[:, 0, :], op0=ALU.mult, op1=ALU.add)
                    if t == CK - 1:
                        ins.then_inc(conv_done, 1)
                    else:
                        link(ins)
                    conv_t += 1

            conv_open = False
            for what, n in WINDOW:
                if what == "chunk":
                    kind, j = SLOTS[n // 2]
                    split_to(n + 4)
                    if kind in ("uf", "v") and n % 2 == 1:
                        dve.wait_ge(chunk_done, n + 1)
                        dst = u_tok[:] if kind == "uf" else v_tok[:, :, 256 * j:256 * j + 256]
                        dve.tensor_copy(dst, ps[:, 0:3, 0:256]).then_inc(u_ready if kind == "uf" else v_ready, 1)
                    if kind == "uc" and n % 2 == 1:
                        dve.wait_ge(glu_tanh, j + 1)
                        for i, (a, b, which) in enumerate(SEG):
                            at = PAD if which == 0 else PAD + LAT0
                            ins = dve.scalar_tensor_tensor(out=zpad[:, j, at:at + b - a], in0=csq[:, j, a:b], scalar=1.0,
                                                           in1=ps[:, 2 * j, a:b], op0=ALU.add, op1=ALU.mult)
                            if i == 0:
                                link(ins)
                            else:
                                ins.then_inc(z_conv, 1)
                        conv_open = conv_open or j == 1
                elif what == "fnet":
                    dve.wait_ge(fn_hi_ready, n + 1)
                    dve.tensor_tensor(fn_lo[:, n, :], ps[:, 2, 0:N], fn_hi[:, n, :].bitcast(F32), ALU.subtract)\
                        .then_inc(fn_ready, 1)
                    if n == 1:
                        dve.memset(zpad[:].rearrange("p a z -> p (a z)"), 0.0).then_inc(zpad_zero, 1)
                        dve.wait_ge(zpad_zero, 1)
                elif what == "unit":
                    if n < UNITS:
                        max_unit(n)
                    if 1 <= n <= UNITS:
                        normalise_unit(n - 1)
                    if conv_open:
                        if conv_t == 0:
                            dve.wait_ge(z_conv, 2)
                        conv_taps(2)
                elif what == "turn" and n >= 0 and n % 6 == 5:
                    pair = n // 6
                    dve.wait_ge(at_hi_ready, pair + 1)
                    dve.tensor_tensor(at_lo[:, pair, :], ps[:, 7, 0:N], at_hi[:, pair, :].bitcast(F32), ALU.subtract)\
                        .then_inc(at_ready, 1)
            conv_taps(CK)
            dve.wait_ge(ln_mean, 1)
            for a in range(2):
                ins = dve.scalar_tensor_tensor(out=acc[:, a, :], in0=ps[:, 0, 0:CO], scalar=-1.0 / CW, in1=acc[:, a, :],
                                               op0=ALU.mult, op1=ALU.add)
            ins.then_inc(ln_centred, 1)
            dve.wait_ge(ln_centred, 1)
            dve.wait_ge(ln_std, 1)
            link(dve.reciprocal(crs[:], crs[:]))
            dve.wait_ge(ln_sq, 1)
            for a in range(2):
                link(dve.tensor_tensor(acc[:, a, :], acc[:, a, :], crs[:], ALU.mult))
            for a in range(2):
                ins = dve.tensor_scalar(acc[:, a, :], acc[:, a, :], vec_t[:, V_LG + a:V_LG + a + 1],
                                        vec_t[:, V_LB + a:V_LB + a + 1], ALU.mult, ALU.add)
                if a == 0:
                    link(ins)
                else:
                    ins.then_inc(ln_out, 1)
            dve.wait_ge(ln_tanh, 1)
            dve.scalar_tensor_tensor(out=acc[:], in0=csq[:], scalar=1.0, in1=acc[:], op0=ALU.add, op1=ALU.mult)\
                .then_inc(silu_ready, 1)
            for i, (at, o) in enumerate(((0, 0), (LAT0, NCTX))):
                w = NCTX if o == 0 else NLAT
                dve.wait_ge(cv_hi_ready, i + 1)
                dve.scalar_tensor_tensor(out=cv_lo[:, :, o:o + w], in0=acc[:, :, at:at + w], scalar=0.5,
                                         in1=cv_hi[:, :, o:o + w].bitcast(F32), op0=ALU.mult, op1=ALU.subtract)\
                    .then_inc(cv_ready, 1)

            for d in range(KT):
                c0 = 2 * (UG0 + 4 * d)
                for b in range(3):
                    split_to(c0 + 1 + b + 4)
                    dve.wait_ge(gate_tanh, 3 * d + b + 1)
                    if b == 0:
                        if d >= 2:
                            dve.wait_ge(mg_ready, d - 1)
                        link(dve.scalar_tensor_tensor(out=mg[:, d % 2, :], in0=th[:, 0, :], scalar=1.0, in1=ps[:, 0, 0:N],
                                                      op0=ALU.add, op1=ALU.mult))
                        continue
                    link(dve.scalar_tensor_tensor(out=mt[:, b - 1, :], in0=th[:, b, :], scalar=1.0, in1=ps[:, b, 0:N],
                                                  op0=ALU.add, op1=ALU.mult))
                    ins = dve.tensor_tensor(mg[:, d % 2, :], mg[:, d % 2, :], mt[:, b - 1, :], ALU.add)
                    if b == 1:
                        link(ins)
                    else:
                        ins.then_inc(merged, 1)
                for i in range(2):
                    split_to(c0 + 4 + 2 * i + 4)
                    split_to(c0 + 4 + 2 * i + 5)
                    if i == 0:
                        dve.wait_ge(mg_hi_ready, d + 1)
                        dve.scalar_tensor_tensor(out=mg_lo[:, d, :], in0=mg[:, d % 2, :], scalar=0.5,
                                                 in1=mg_hi[:, d, :].bitcast(F32), op0=ALU.mult, op1=ALU.subtract)\
                            .then_inc(mg_ready, 1)
            split_to(2 * WO0 + 4)
            dve.wait_ge(mod_turned, 24)
            mod_finish(16, 32, 7)
            norm_scale(scale2, 4, V_N2)
            for n in range(KT):
                split_to(2 * WO0 + n + 4)
                dve.wait_ge(chunk_done, 2 * WO0 + n + 1)
                for a, b, which in SEG:
                    ins = dve.scalar_tensor_tensor(out=xT[:, n, a:b], in0=ps[:, n % 2, a:b],
                                                   scalar=modT[:, 16 + n, which:which + 1], in1=xT[:, n, a:b],
                                                   op0=ALU.mult, op1=ALU.add)
                ins.then_inc(x1_ready, 1)
            dve.wait_ge(x1_ready, KT)
            dve.wait_ge(std_ready, 2)
            link(dve.reciprocal(rstd[:], rstd[:]))
            for k in range(KT):
                link(dve.tensor_tensor(h2T[:, k, :], xT[:, k, :], rstd[:], ALU.mult))
                modulate(k, h2T, scale2, 3).then_inc(h2_ready, 1)
            dve.wait_ge(logits_turned, 1)
            dve.wait_ge(gr_in, 64)
            for t in range(NT):
                ins = dve.tensor_tensor(lg[:, t, :], ps[:, 2, 36 * t:36 * t + 36], b_gr[:], ALU.add)
            link(ins)

            def bc(ap, n):
                return ap.to_broadcast([P, NT, n])

            def first_max(dst, src, n, m, scratch):
                link(dve.tensor_reduce(m, src, axis=AX, op=ALU.max))
                link(dve.tensor_tensor(dst, src, bc(m, n), ALU.is_equal))
                w = iota_s[:, P - n:P].rearrange("p (a e) -> p a e", a=1).to_broadcast([P, NT, n])
                link(dve.tensor_scalar(scratch[1], w, -1.0, float(P), ALU.mult, ALU.add))
                link(dve.tensor_tensor(dst, dst, scratch[1], ALU.mult))
                link(dve.tensor_reduce(scratch[0], dst, axis=AX, op=ALU.max))
                return dve.tensor_tensor(dst, dst, bc(scratch[0], n), ALU.is_equal)

            glog = lg[:, :, 0:GROUPS]
            first_max(og[:], glog, GROUPS, rt[:, :, 0:1], (rt[:, :, 14:15], rt[:, :, 24:28])).then_inc(group_hot, 1)
            dve.wait_ge(group_hot, 1)
            dve.tensor_tensor(rt[:, :, 4:8], glog, bc(rt[:, :, 0:1], GROUPS), ALU.subtract).then_inc(grp_shift, 1)
            for t in range(NT):
                el = lg[:, t, GROUPS:].rearrange("p (g e) -> p e g", g=GROUPS)
                ins = dve.tensor_tensor(pr[:, t, :, :], el, og[:, t:t + 1, :].to_broadcast([P, EPG, GROUPS]), ALU.mult)
            link(ins)
            link(dve.tensor_reduce(e_sel[:].rearrange("p t e -> p (t e)"), pr[:].rearrange("p t e g -> p (t e) g"),
                                   axis=AX, op=ALU.add))
            link(first_max(o1[:], e_sel[:], EPG, rt[:, :, 16:17], (rt[:, :, 14:15], rt[:, :, 24:32])))
            link(dve.scalar_tensor_tensor(out=e_sel[:], in0=o1[:], scalar=NEG, in1=e_sel[:], op0=ALU.mult, op1=ALU.add))
            link(first_max(o2[:], e_sel[:], EPG, rt[:, :, 17:18], (rt[:, :, 14:15], rt[:, :, 24:32])))
            dve.tensor_tensor(rt[:, :, 20:21], rt[:, :, 17:18], rt[:, :, 16:17], ALU.subtract).then_inc(exp_gap, 1)
            dve.wait_ge(grp_exp, 1)
            link(dve.tensor_reduce(rt[:, :, 12:13], rt[:, :, 8:12], axis=AX, op=ALU.add))
            dve.wait_ge(ranks, 1)
            link(dve.tensor_copy(rk[:], ps[:, 3, 0:12].rearrange("p (t g) -> p t g", t=NT)))
            link(dve.tensor_copy(tot[:], ps[:, 3, 16:28].rearrange("p (t g) -> p t g", t=NT)))
            for t in range(1, NT):
                link(dve.tensor_tensor(rk[:, t, :], rk[:, t, :], tot[:, t - 1, :], ALU.add))
                link(dve.tensor_tensor(tot[:, t, :], tot[:, t, :], tot[:, t - 1, :], ALU.add))
            dve.wait_ge(consts_ready, 7)
            link(dve.tensor_tensor(rk[:], rk[:], goff[:].rearrange("p (a g) -> p a g", a=1).to_broadcast([P, NT, GROUPS]),
                                   ALU.add))
            link(dve.tensor_tensor(rk[:], rk[:], og[:], ALU.mult))
            link(dve.tensor_reduce(key[:], rk[:], axis=AX, op=ALU.add))
            link(dve.tensor_tensor(keysh[:], key[:].rearrange("p (a t) -> p a t", a=1).to_broadcast([P, 16, NT]),
                                   i_base[:].rearrange("p (i a) -> p i a", a=1).to_broadcast([P, 16, NT]), ALU.subtract))
            link(dve.tensor_reduce(rt[:, 0, 15:16], tot[:, NT - 1, :], axis=AX, op=ALU.max))
            dve.tensor_scalar(over[:], rt[:, 0, 15:16], float(P), None, ALU.is_gt).then_inc(routed, 1)
            dve.wait_ge(exp2, 1)
            link(dve.tensor_scalar(rt[:, :, 22:23], rt[:, :, 21:22], 1.0, None, ALU.add))
            link(dve.tensor_tensor(rt[:, :, 22:23], rt[:, :, 22:23], rt[:, :, 12:13], ALU.mult))
            link(dve.reciprocal(rt[:, :, 23:24], rt[:, :, 22:23]))
            link(dve.tensor_scalar(rt[:, :, 23:24], rt[:, :, 23:24], 0.5, None, ALU.mult))
            link(dve.tensor_tensor(rt[:, :, 21:22], rt[:, :, 21:22], rt[:, :, 23:24], ALU.mult))
            link(dve.tensor_tensor(o1[:], o1[:], bc(rt[:, :, 23:24], EPG), ALU.mult))
            link(dve.tensor_tensor(o2[:], o2[:], bc(rt[:, :, 21:22], EPG), ALU.mult))
            link(dve.tensor_tensor(comb[:], o1[:], o2[:], ALU.add))

            def select(nx):
                for t in range(NT):
                    ins = dve.tensor_scalar(sel[:, t, :], iota_s[:], keysh[:, bass.ds(nx, 1), t] if not isinstance(nx, int)
                                            else keysh[:, nx:nx + 1, t], None, ALU.is_equal)
                    ins.then_inc(sel_ready, 1)

            def hg_low(nx):
                dve.wait_ge(hg_hi_ready, nx + 1)
                dve.tensor_tensor(hg_lo[:].rearrange("p k s -> p (k s)"), ps[:, 5:7, :].rearrange("p a n -> p (a n)"),
                                  hg_hi[:].rearrange("p k s -> p (k s)").bitcast(F32), ALU.subtract).then_inc(hg_ready, 1)

            select(0)
            tok_banks = (0, 4, 6)
            for t in range(NT):
                dve.wait_ge(ht_hi_ready, t + 1)
                dve.tensor_tensor(ht_lo[:, t, :], ps[:, tok_banks[t]:tok_banks[t] + 2, :].rearrange("p a n -> p (a n)"),
                                  ht_hi[:, t, :].bitcast(F32), ALU.subtract).then_inc(ht_ready, 1)
            hg_low(0)

            def item(it, g):
                for i in range(3):
                    dve_split_item(dve, it, i)

                def hid_e(e):
                    n = it * EPG + e
                    dve.wait_ge(e_tanh, n + 1)
                    if e == 0:
                        dve.wait_ge(cmb_ready, it + 1)
                    if e >= 2:
                        dve.wait_ge(hid_turned, n - 1)
                    dve.scalar_tensor_tensor(out=s_e[:, e % 2, :], in0=th_e[:, e % 2, :], scalar=1.0, in1=ps[:, e % 2, 0:EH],
                                             op0=ALU.add, op1=ALU.mult).then_inc(silu_e, 1)
                    dve.wait_ge(silu_e, n + 1)
                    dve.scalar_tensor_tensor(out=hid[:, e % 2, :], in0=s_e[:, e % 2, :], scalar=cmb[:, e:e + 1],
                                             in1=ps[:, e % 2, EH:2 * EH], op0=ALU.mult, op1=ALU.mult).then_inc(hid_ready, 1)

                def hd_low(e):
                    dve.wait_ge(hd_hi_ready, it * EPG + e + 1)
                    dve.tensor_tensor(hd_lo[:].rearrange("p a n -> p (a n)"), ps[:, 4, 0:2 * P],
                                      hd_hi[:].rearrange("p a n -> p (a n)").bitcast(F32), ALU.subtract).then_inc(hd_ready, 1)

                for what, e, part, i in order:
                    if i + 3 < ITEM_CH:
                        dve_split_item(dve, it, i + 3)
                    if what == "up" and part == 0 and e >= 1:
                        hid_e(e - 1)
                    if what == "up" and part == 3 and e >= 1:
                        hd_low(e - 1)
                    if what == "up" and part == 1 and e == EPG - 2:
                        dve.wait_ge(sel_turned, it + 1)
                        select(it + 1)
                    if what == "down" and part == 0 and e == EPG - 2:
                        hid_e(EPG - 1)
                hg_low(it + 1)
                hd_low(EPG - 1)
                dve.wait_ge(y_hi_ready, it + 1)
                dve.tensor_tensor(y_lo[:], ps[:, 2:4, :].rearrange("p a n -> p (a n)"), y_hi[:].bitcast(F32), ALU.subtract)\
                    .then_inc(y_ready, 1)
                for k in range(KT):
                    dve.wait_ge(combined, it * KT + k + 1)
                    for i, (a, b, which) in enumerate(SEG):
                        dve.scalar_tensor_tensor(out=xT[:, k, a:b], in0=ps[:, 5 + k % 2, a:b],
                                                 scalar=modT[:, 40 + k, which:which + 1], in1=xT[:, k, a:b],
                                                 op0=ALU.mult, op1=ALU.add).then_inc(added, 1)

            rounds(dve, item)
            dve.memset(fin[:, 6:7], 0.0).then_inc(x2_ready, 1)
            dve.wait_ge(out_std, 1)
            dve.wait_ge(fg_in, 16)
            link(dve.reciprocal(fin[:, 3:6], fin[:, 3:6]))
            out_banks = (0, 2, 5)
            for t in range(NT):
                if t >= 2:
                    dve.wait_ge(store_y[t - 2], 16)
                dve.scalar_tensor_tensor(out=out_t[:, t % 2, :],
                                         in0=ps[:, out_banks[t]:out_banks[t] + 2, :].rearrange("p a n -> p (a n)"),
                                         scalar=fin[:, 3 + t:4 + t], in1=fg_b[:], op0=ALU.mult, op1=ALU.mult)\
                    .then_inc(out_ready, 1)

        @block.tensor
        def _(pe):
            def three(out, a_hi, a_lo, b_hi, b_lo, start, stop):
                pe.matmul(out, a_hi, b_hi, start=start, stop=False)
                pe.matmul(out, a_hi, b_lo, start=False, stop=False)
                return pe.matmul(out, a_lo, b_hi, start=False, stop=stop)

            def column_chunk(i, bank, x_hi, x_lo, k0=0, kn=KT, x0=0, first=True):
                b = i % SPLIT
                for k in range(k0, k0 + kn):
                    w = slice(P * k, P * k + P)
                    ins = three(ps[:, bank, 0:N], w_hi[:, b, w], w_lo[:, b, w], x_hi[:, x0 + k - k0, :], x_lo[:, x0 + k - k0, :],
                                k == k0, k == k0 + kn - 1)
                return ins

            def token_chunk(i):
                b, half = i % SPLIT, i % 2
                for k in range(4):
                    w = slice(256 * k, 256 * k + 256)
                    for t in range(NT):
                        x = slice(P * t, P * t + P)
                        ins = three(ps[:, t, 0:256], h_hi[:, 4 * half + k, x], h_lo[:, 4 * half + k, x],
                                    w_hi[:, b, w], w_lo[:, b, w], half == 0 and k == 0, half == 1 and k == 3)
                return ins

            def mod_slot(j, c0):
                bank = j % 2 if j < 8 else 5 + j % 2
                if j >= 2:
                    pe.wait_ge(modrow_ready, j - 1)
                for half in range(2):
                    i = c0 + half
                    pe.wait_ge(lo_ready, i + 1)
                    for k in range(4):
                        w = slice(256 * k, 256 * k + 256)
                        pe.matmul(ps[0:4, bank, 0:256], cond4[:, 4 * half + k, :], w_hi[:, i % SPLIT, w],
                                  start=half == 0 and k == 0, stop=False)
                        ins = pe.matmul(ps[0:4, bank, 0:256], cond4[:, 4 * half + k, :], w_lo[:, i % SPLIT, w],
                                        start=False, stop=half == 1 and k == 3)
                    ins.then_inc(chunk_done, 1)

            def mod_turn(j):
                pe.wait_ge(modrow_ready, j + 1)
                bank = 2 if j < 8 else 7
                for t in range(2):
                    at = 4 * (2 * j + t)
                    ins = pe.transpose(ps[:, bank, at:at + 4], modrow[:, j % 2, P * t:P * t + P], ident[0:4, 0:4])
                ins.then_inc(mod_turned, 1)

            def ssq(n, bank):
                pe.wait_ge(sq_ready, n + 1)
                pe.matmul(ps[:, bank, 0:N], ones[:], sq[:, n % 2, :], start=n % KT == 0, stop=n % KT == KT - 1)\
                    .then_inc(ssq_step, 1)

            pe.wait_ge(consts_ready, 5)
            pe.wait_ge(rows_in, 16 * 8)
            pe.transpose(ps[:, 3, 0:V_ROWS], vec_rows[:], ident[0:V_ROWS, 0:V_ROWS]).then_inc(vec_turned, 1)
            pe.wait_ge(taps_in, 32)
            pe.transpose(ps[:, 2, 0:2 * CK], tap_rows[:], ident[0:2 * CK, 0:2 * CK]).then_inc(vec_turned, 1)
            pe.wait_ge(x_in, 16 * NT)
            for k in range(KT + 1):
                if k < KT:
                    if k >= 3:
                        pe.wait_ge(x_ready, k - 2)
                    for t in range(NT):
                        ins = pe.transpose(ps[:, 4 + k % 3, P * t:P * t + P], x_tok[:, t, P * k:P * k + P], ident[:])
                    ins.then_inc(x_turned, 1)
                if k >= 1:
                    ssq(k - 1, 7)
            pe.wait_ge(ck_in, 16)
            pe.wait_ge(cond_ready, 1)
            for j in range(8):
                mod_slot(j, 2 * j)
                if j:
                    mod_turn(j - 1)
            for pair in range(PAIRS):
                ins = pe.transpose(ps[:, 5, P * pair:P * pair + P], ck_tok[:, 2 * pair:2 * pair + 2, :]
                                   .rearrange("p a d -> p (a d)"), ident[:])
            ins.then_inc(ck_turned, 1)
            mod_turn(7)
            c_q = first_chunk("q")
            for n in range(8):
                i = c_q + n
                if n == 0:
                    pe.wait_ge(modrow_ready, 8)
                if n >= 2:
                    pe.wait_ge(q_ready if n < 6 else k_ready, n - 1 if n < 6 else n - 5)
                pe.wait_ge(lo_ready, i + 1)
                for k in range(KT):
                    if n == 0:
                        pe.wait_ge(h_ready, k + 1)
                    w = slice(P * k, P * k + P)
                    ins = three(ps[:, n % 2, 0:N], w_hi[:, i % SPLIT, w], w_lo[:, i % SPLIT, w], h_hi[:, k, :], h_lo[:, k, :],
                                k == 0, k == KT - 1)
                ins.then_inc(chunk_done, 1)
            pe.wait_ge(k_ready, 4)
            for pair in range(PAIRS):
                ins = pe.transpose(ps[:, 6, P * pair:P * pair + P], kT[:, pair, 0:NCTX], ident[:])
            ins.then_inc(kctx_turned, 1)

            def score_unit(u):
                h, part = u // 3, u % 3
                rows, pair = slice(HD * (h % 2), HD * (h % 2) + HD), h // 2
                bank = 3 + u % 2
                if u >= 2:
                    pe.wait_ge(exps, u - 1)
                if part == 0:
                    pe.matmul(ps[:, bank, 0:NCTX], qT[rows, pair, 0:NCTX], kT[rows, pair, 0:NCTX], start=True, stop=True)\
                        .then_inc(scores, 1)
                    return
                q = qT[rows, pair, P * part:P * part + P]
                pe.matmul(ps[:, bank, 0:NLAT], q, kT[rows, pair, NCTX:N], start=True, stop=True)
                pe.matmul(ps[:, bank, NLAT:N], q, ckT[rows, pair, :], start=True, stop=True).then_inc(scores, 1)

            def turn_unit(u):
                h, part = u // 3, u % 3
                pe.wait_ge(probs_ready, u + 1)
                if u >= 2:
                    pe.wait_ge(turned_out, u - 1)
                for a in range(1 if part == 0 else 3):
                    ins = pe.transpose(ps[:, 5 + u % 2, P * a:P * a + P], probs[:, u % 3, P * a:P * a + P], ident[:])
                ins.then_inc(turned, 1)
                if part < 2:
                    return
                pair, out = h // 2, slice(HD * (h % 2), HD * (h % 2) + HD)
                cols = slice(HD * h, HD * h + HD)
                if h == 0:
                    pe.wait_ge(v_ready, 2)
                    pe.wait_ge(cv_in, 16)
                if h % 2 == 0 and pair:
                    pe.wait_ge(at_ready, pair)
                pe.wait_ge(turned_out, u + 1)
                pe.matmul(ps[out, 7, 0:NCTX], v_tok[:, 0, cols], ptc[:], start=True, stop=True)
                for a in range(3):
                    v = v_tok[:, 1 + a, cols] if a < 2 else cv_tok[:, h, :]
                    ins = pe.matmul(ps[out, 7, NCTX:N], v, ptl[:, a, :, :].rearrange("p t q -> p (t q)"),
                                    start=a == 0, stop=a == 2)
                ins.then_inc(pv_done, 1)

            for what, n in WINDOW:
                if what == "chunk":
                    kind, j = SLOTS[n // 2]
                    pe.wait_ge(lo_ready, n + 1)
                    if kind in ("uf", "v"):
                        if kind == "uf" and n % 2 == 0:
                            pe.wait_ge(k_ready, 4)
                        if kind == "v" and n % 2 == 0:
                            pe.wait_ge(fn_ready, 2) if j == 0 else pe.wait_ge(v_ready, j)
                        token_chunk(n).then_inc(chunk_done, 1)
                    else:
                        if n % 2 == 0:
                            pe.wait_ge(v_ready, 2)
                        elif j == 1:
                            pe.wait_ge(glu_tanh, 1)
                        column_chunk(n, 1 if n % 2 else 2 * j, h_hi, h_lo).then_inc(chunk_done, 1)
                elif what == "fnet":
                    if n == 0:
                        pe.wait_ge(u_ready, 1)
                        pe.wait_ge(dft_in, 16 * 4)
                    else:
                        pe.wait_ge(z_ready, 1)
                    f = slice(P * n, P * n + P)
                    pe.matmul(ps[:, 0, 0:2 * NCTX], u_tok[:, 0, f], ctx_w[:], start=True, stop=True).then_inc(fnet_pos, 1)
                    for a in range(2):
                        ins = pe.matmul(ps[:, 1, 0:2 * NLAT], u_tok[:, 1 + a, f], lat_w[:, a, :], start=a == 0, stop=a == 1)
                    ins.then_inc(fnet_pos, 1)
                    pe.wait_ge(z_ready, n + 1)
                    if n == 1:
                        pe.wait_ge(fn_ready, 1)
                    for a in range(2):
                        ins = pe.matmul(ps[:, 2, 0:N], feat_w[:, a, :], z_cs[:, a, :], start=a == 0, stop=a == 1)
                    ins.then_inc(fnet_feat, 1)
                elif what == "unit" and n < UNITS:
                    if n == 0:
                        pe.wait_ge(ck_ready, 1)
                        pe.wait_ge(kout_ready, 1)
                    score_unit(n)
                elif what == "turn" and n >= 0:
                    turn_unit(n)
            pe.wait_ge(conv_done, 2)
            pe.wait_ge(z_conv, 2)
            for a in range(2):
                ins = pe.matmul(ps[:, 0, 0:CO], ones[:], acc[:, a, :], start=a == 0, stop=a == 1)
            ins.then_inc(ln_mean, 1)
            pe.wait_ge(ln_sq, 1)
            for a in range(2):
                ins = pe.matmul(ps[:, 1, 0:CO], ones[:], csq[:, a, :], start=a == 0, stop=a == 1)
            ins.then_inc(ln_var, 1)

            for d in range(KT):
                c0 = 2 * (UG0 + 4 * d)
                pe.wait_ge(lo_ready, c0 + 1)
                if d == 0:
                    pe.wait_ge(at_ready, PAIRS)
                    pe.wait_ge(cv_ready, 2)
                else:
                    pe.wait_ge(merged, d)
                column_chunk(c0, 0, at_hi, at_lo, 0, 4)
                column_chunk(c0, 1, fn_hi, fn_lo, 4, 2)
                column_chunk(c0, 2, cv_hi, cv_lo, 6, 2).then_inc(chunk_done, 1)
                for b in range(3):
                    pe.wait_ge(lo_ready, c0 + 2 + b)
                    if 3 * d + b >= 2:
                        pe.wait_ge(gate_tanh, 3 * d + b - 1)
                    column_chunk(c0 + 1 + b, 3 + (3 * d + b) % 2, h_hi, h_lo).then_inc(chunk_done, 1)
                for i in range(2):
                    mod_slot(8 + 2 * d + i, c0 + 4 + 2 * i)
                    if 2 * d + i:
                        mod_turn(7 + 2 * d + i)
            mod_turn(23)
            for n in range(KT + 1):
                if n < KT:
                    pe.wait_ge(lo_ready, 2 * WO0 + n + 1)
                    if n == 0:
                        pe.wait_ge(mg_ready, KT)
                    if n >= 2:
                        pe.wait_ge(x1_ready, n - 1)
                    column_chunk(2 * WO0 + n, n % 2, mg_hi, mg_lo).then_inc(chunk_done, 1)
                if n >= 1:
                    ssq(KT + n - 1, 2)
            pe.wait_ge(gr_in, 64)
            tok_banks = (0, 4, 6)
            for k in range(KT):
                pe.wait_ge(h2_ready, k + 1)
                ins = pe.matmul(ps[0:GROUPS + NE, 3, 0:N], w_gr[:, k, :], h2T[:, k, :], start=k == 0, stop=k == KT - 1)
            ins.then_inc(logits, 1)
            for t in range(NT):
                for k in range(KT):
                    ins = pe.transpose(ps[:, tok_banks[t] + k // 4, P * (k % 4):P * (k % 4) + P],
                                       h2T[:, k, P * t:P * t + P], ident[:])
                ins.then_inc(h2_turned, 1)
                if t == 0:
                    pe.wait_ge(logits_out, 1)
                    for q in range(NT):
                        ins = pe.transpose(ps[:, 2, 36 * q:36 * q + 36], lgT[:, P * q:P * q + P], ident[0:36, 0:36])
                    ins.then_inc(logits_turned, 1)
            pe.wait_ge(group_hot, 1)
            hot = og[:].rearrange("p t g -> p (t g)")
            pe.matmul(ps[:, 3, 0:12], tri[:], hot, start=True, stop=True)
            pe.matmul(ps[:, 3, 16:28], ones[:], hot, start=True, stop=True).then_inc(ranks, 1)

            def gather(nx):
                pe.wait_ge(sel_ready, NT * nx + NT)
                for half in range(2):
                    d = slice(512 * half, 512 * half + 512)
                    for t in range(NT):
                        pe.matmul(ps[:, 5 + half, :], sel[:, t, :], ht_hi[:, t, d], start=t == 0, stop=False)
                        ins = pe.matmul(ps[:, 5 + half, :], sel[:, t, :], ht_lo[:, t, d], start=False, stop=t == NT - 1)
                ins.then_inc(gathered, 1)
                for t in range(NT):
                    pe.matmul(ps[:, 7, 0:EPG], sel[:, t, :].bitcast(F32), comb[:, t, :], start=t == 0, stop=t == NT - 1)

            def hg_turn(nx):
                pe.wait_ge(hg_out, nx + 1)
                for k in range(KT):
                    ins = pe.transpose(ps[:, 5 + k // 4, P * (k % 4):P * (k % 4) + P], hg32[:, P * k:P * k + P], ident[:])
                ins.then_inc(hg_turned, 1)

            pe.wait_ge(ht_ready, NT)
            gather(0)
            hg_turn(0)

            def item(it, g):
                for t in range(NT):
                    ins = pe.transpose(ps[:, 7, P * (t + 1):P * (t + 1) + P], sel[:, t, :].bitcast(F32), ident[:])
                ins.then_inc(sel_turned, 1)

                def hid_turn(e):
                    n = it * EPG + e
                    pe.wait_ge(hid_ready, n + 1)
                    for a in range(2):
                        ins = pe.transpose(ps[:, 4, P * a:P * a + P], hid[:, e % 2, P * a:P * a + P], ident[:])
                    ins.then_inc(hid_turned, 1)

                for what, e, part, i in order:
                    b = (PRE_CH + i) % SPLIT
                    pe.wait_ge(lo_ready, it * ITEM_CH + PRE_CH + i + 1)
                    if what == "up":
                        if part == 0 and e == 0:
                            pe.wait_ge(hg_ready, it + 1)
                        if part == 0 and e >= 2:
                            pe.wait_ge(hid_ready, it * EPG + e - 1)
                        if part == 0 and e == EPG - 1:
                            gather(it + 1)
                        for k in range(2):
                            w, kk = slice(512 * k, 512 * k + 512), 2 * part + k
                            ins = three(ps[:, e % 2, :], hg_hi[:, kk, :], hg_lo[:, kk, :], w_hi[:, b, w], w_lo[:, b, w],
                                        kk == 0, kk == KT - 1)
                        ins.then_inc(chunk_done, 1)
                        if part == 1 and e >= 1:
                            hid_turn(e - 1)
                    else:
                        if part == 0 and e == EPG - 1:
                            hg_turn(it + 1)
                            hid_turn(e)
                        if part == 0:
                            pe.wait_ge(hd_ready, it * EPG + e + 1)
                        for half in range(2):
                            w = slice(512 * half, 512 * half + 512)
                            ins = three(ps[:, 2 + half, :], hd_hi[:, part, :], hd_lo[:, part, :], w_hi[:, b, w], w_lo[:, b, w],
                                        e == 0 and part == 0, e == EPG - 1 and part == 1)
                        ins.then_inc(chunk_done, 1)
                pe.wait_ge(y_ready, it + 1)
                pe.wait_ge(selT_ready, it + 1)
                pe.wait_ge(hg_ready, it + 2)
                for k in range(KT):
                    if k >= 2:
                        pe.wait_ge(added, it * 2 * KT + 2 * (k - 1))
                    d = slice(P * k, P * k + P)
                    pe.matmul(ps[:, 5 + k % 2, 0:N], y_hi[:, d], selT[:], start=True, stop=False)
                    pe.matmul(ps[:, 5 + k % 2, 0:N], y_lo[:, d], selT[:], start=False, stop=True).then_inc(combined, 1)

            rounds(pe, item)
            pe.wait_ge(x2_ready, 1)
            out_banks = (0, 2, 5)
            for t in range(NT):
                for k in range(KT):
                    ins = pe.transpose(ps[:, out_banks[t] + k // 4, P * (k % 4):P * (k % 4) + P], xT[:, k, P * t:P * t + P],
                                       ident[:])
                ins.then_inc(out_turned, 1)


_INS = ['x_prompt', 'x_sample', 'cache_k', 'cache_v', 'c', 'c_ctx', 'w_mod', 'b_mod', 'norm1_g', 'w_in', 'rpb',
        'w_attn_o', 'w_fnet', 'conv_dw', 'conv_b', 'conv_ln_g', 'conv_ln_b', 'w_conv_o', 'w_out', 'norm2_g',
        'w_group', 'b_group', 'w_router', 'b_router', 'w1', 'w3', 'w2', 'final_g']
_OUTS = [("y_prompt", (1, NCTX, D)), ("y_sample", (1, NLAT, D)), ("new_k", (1, 1, HEADS, NCTX, HD)),
         ("new_v", (1, 1, HEADS, NCTX, HD))]


def _dft(n, norm):
    import numpy as np
    a = 2.0 * np.pi * ((np.arange(n)[:, None] * np.arange(n)[None, :]) % n) / n
    return np.concatenate([np.cos(a) * norm, np.sin(a) * norm], axis=1)


def _constants():
    import numpy as np
    f = _dft(FG, 1.0)
    feat = np.zeros((P, 2 * P))
    for g in range(P // FG):
        rows = slice(FG * g, FG * g + FG)
        feat[rows, FG * g:FG * g + FG] = f[:, 0:FG]
        feat[rows, P + FG * g:P + FG * g + FG] = -f[:, FG:]
    return {"dft_lat": _dft(NLAT, (NLAT * FG) ** -0.5).astype(np.float32),
            "dft_ctx": _dft(NCTX, (NCTX * FG) ** -0.5).astype(np.float32), "dft_feat": feat.astype(np.float32)}


def _lay_out(inputs):
    import numpy as np
    arrays = {name: np.ascontiguousarray(a) for name, a in inputs.items()}
    arrays["rpb"] = np.tile(arrays["rpb"], (1, 1, 1, GRID_W))
    arrays.update(_constants())
    return arrays


def kernel(**inputs):
    import concourse.bacc as bacc
    from concourse.bass_utils import run_bass_kernel_spmd

    nc = bacc.Bacc("TRN2", target_bir_lowering=False, num_devices=1)
    arrays = _lay_out({name: inputs[name] for name in _INS})
    args = {}
    for name, a in arrays.items():
        args[name] = nc.dram_tensor(name, a.shape, mybir.dt.from_np(a.dtype), kind="ExternalInput").ap()
    for name, shape in _OUTS:
        args[name] = nc.dram_tensor(name, shape, F32, kind="ExternalOutput").ap()
    build(nc, **args)
    r = run_bass_kernel_spmd(nc, [arrays], core_ids=[0])
    return tuple(r.results[0][name] for name, _ in _OUTS)
```

```python
from contextlib import ExitStack

import concourse.bass as bass
from concourse import mybir

F32 = mybir.dt.float32
F32R = mybir.dt.float32r
I32 = mybir.dt.int32
ALU = mybir.AluOpType
ACT = mybir.ActivationFunctionType
AX = mybir.AxisListType.X

P = 128
D = 1024
KT = D // P
NCTX, NLAT = 128, 256
N = NCTX + NLAT
NT = N // P
SEG = ((0, NCTX, 0), (NCTX, N, 1))
HEADS, HD = 8, 64
PAIRS = HEADS // 2
GRID_W, GRID_H = 64, 4
NDR = 6
RPB_R, RPB_C = 15, 31
FW, FG = 256, 64
CW, CK = 256, 31
PAD = CK // 2
ZW = PAD + NCTX + PAD + NLAT + PAD
CO = ZW - 2 * PAD
LAT0 = NCTX + PAD
COL_Q, COL_K, COL_V = 0, 512, 1024
COL_F = 1536
COL_C = COL_F + FW
COL_G = COL_C + 2 * CW
GROUPS, EPG, EH = 4, 8, 256
NE = GROUPS * EPG
ROUNDS = (N + P - 1) // P
EPS = 1e-6
NEG = -1e30

RING = 6
SLOT = 2048
CH = SLOT // 2
SPLIT = 4

V_CTX, V_C, V_N1, V_N2, V_BM, V_CB, V_LG, V_LB = 0, 8, 16, 24, 32, 80, 82, 84
V_ROWS = 86

SLOTS = ([("mod", j) for j in range(8)] + [("q", j) for j in range(2)] + [("k", j) for j in range(2)]
         + [("uf", 0), ("uc", 0), ("uc", 1), ("v", 0), ("v", 1)])
MOD_WINDOW = range(8, 18)
SLOTS += [("mod", j) for j in MOD_WINDOW]
MOD_LAST = range(MOD_WINDOW[-1] + 1, 24)
UG = [("g12", 0), ("mod", 18), ("mod", 19), ("g0b", 0), ("g12", 1), ("mod", 20), ("g0b", 1), ("g12", 2), ("mod", 21),
      ("g0b", 2), ("g12", 3), ("mod", 22), ("g0b", 3), ("g12", 4), ("mod", 23), ("g0b", 4)]
for _d in range(5, KT):
    UG += [("g12", _d), ("g0b", _d)]
SLOTS += UG
WO0 = len(SLOTS)
SLOTS += [("wo", j) for j in range(4)]
PRE = len(SLOTS)
PRE_CH = 2 * PRE
BY_COLUMNS = ("q", "k", "uc", "wo")

ITEM = [("A", 0), ("B", 0)]
for _e in range(1, EPG):
    ITEM += [("A", _e), ("B", _e), ("C", _e - 1)]
ITEM += [("C", EPG - 1)]
ITEM_CH = 2 * len(ITEM)
assert len(ITEM) % RING == 0 and ITEM_CH % SPLIT == 0

COMBINE0 = 4
SEL_TURN = 4

UNITS = 3 * HEADS


def first_chunk(kind, j=0):
    return 2 * SLOTS.index((kind, j))


_uf, _uc, _v = first_chunk("uf"), first_chunk("uc"), first_chunk("v")
WINDOW = [("chunk", _uf), ("chunk", _uf + 1), ("chunk", _uc), ("fpos", 0), ("chunk", _uc + 1), ("ffeat", 0),
          ("fpos", 1), ("chunk", _uc + 2), ("ffeat", 1), ("chunk", _uc + 3), ("glu", 0), ("chunk", _v), ("glu", 1)]
_fill = {0: [("chunk", _v + 1)], 1: [("chunk", _v + 2)], 2: [("chunk", _v + 3)]}
for _i, _j in enumerate(MOD_WINDOW):
    _fill[4 + 2 * _i] = [("mod", _j)]
for _u in range(UNITS + 2):
    WINDOW += [("unit", _u)] + _fill.get(_u, []) + [("turn", _u - 2)]


def build(nc, x_prompt, x_sample, cache_k, cache_v, c, c_ctx, w_mod, b_mod, norm1_g, w_in, rpb, w_attn_o,
          w_fnet, conv_dw, conv_b, conv_ln_g, conv_ln_b, w_conv_o, w_out, norm2_g, w_group, b_group,
          w_router, b_router, w1, w3, w2, final_g, dft_lat, dft_ctx, dft_feat,
          y_prompt, y_sample, new_k, new_v):
    ctx = ExitStack()
    with ctx:
        base = (nc.sbuf_base + 31) // 32 * 32
        top = nc.sbuf_usable_end

        class Region:

            def __init__(self, start, size=None):
                self.start, self.at, self.end = start, start, start + size if size else top

            def tile(self, name, shape, dt=F32):
                size = 4
                for s in shape[1:]:
                    size *= s
                t = nc.alloc_sbuf_tensor_at(name, shape, dt, offset=self.at)
                self.at += (size + 31) // 32 * 32
                assert self.at <= self.end, (name, self.at, self.end)
                return t

        R = Region(base)
        raw = R.tile("raw", [P, RING, SLOT])
        w_hi = R.tile("w_hi", [P, SPLIT, CH], F32R)
        w_lo = R.tile("w_lo", [P, SPLIT, CH], F32R)
        xT = R.tile("xT", [P, KT, N])
        ident = R.tile("ident", [P, P])
        ones = R.tile("ones", [P, P])
        tri = R.tile("tri", [P, P])
        iota_s = R.tile("iota_s", [P, P])
        vec_t = R.tile("vec_t", [P, V_ROWS])
        taps = R.tile("taps", [P, 2, CK])
        cond = R.tile("cond", [P, 2, KT])
        cond_t = R.tile("cond_t", [P, 2, KT])
        cond4 = R.tile("cond4", [P, KT, 4], F32R)
        modT = R.tile("modT", [P, 48, 2])
        scale1 = R.tile("scale1", [P, KT, 2])
        scale2 = R.tile("scale2", [P, KT, 2])
        eps_t = R.tile("eps_t", [P, 1])
        rstd = R.tile("rstd", [P, N])
        sq = R.tile("sq", [P, 2, N])
        modrow = R.tile("modrow", [4, 2, 256])
        w_gr = R.tile("w_gr", [P, KT, GROUPS + NE])
        b_gr = R.tile("b_gr", [P, GROUPS + NE])
        mod_tmp = R.tile("mod_tmp", [P, 32, 4])
        stats = R.tile("stats", [P, 3, 8])
        rt = R.tile("rt", [P, 3, 64])
        start_h = R.at
        Rh = Region(start_h, 2 * 4 * KT * N)
        h_hi = Rh.tile("h_hi", [P, KT, N], F32R)
        h_lo = Rh.tile("h_lo", [P, KT, N], F32R)
        start_b = Rh.at
        Rb = Region(start_b, 4 * 16 * N)
        at_hi = Rb.tile("at_hi", [P, PAIRS, N], F32R)
        at_lo = Rb.tile("at_lo", [P, PAIRS, N], F32R)
        fn_hi = Rb.tile("fn_hi", [P, 2, N], F32R)
        fn_lo = Rb.tile("fn_lo", [P, 2, N], F32R)
        start_cv = Rb.at
        cv_hi = Rb.tile("cv_hi", [P, 2, N], F32R)
        cv_lo = Rb.tile("cv_lo", [P, 2, N], F32R)
        k_out = Region(start_cv, 4 * 4 * N).tile("k_out", [P, HEADS * HD])
        start_x = Rb.at
        Rx = Region(start_x)
        qT = Rx.tile("qT", [P, PAIRS, N])
        kT = Rx.tile("kT", [P, PAIRS, N])
        v_tok = Rx.tile("v_tok", [P, NT, HEADS * HD])
        ckT = Rx.tile("ckT", [P, PAIRS, P])
        cv_tok = Rx.tile("cv_tok", [P, HEADS, HD])
        bias = Rx.tile("bias", [P, HEADS, NDR, GRID_W])
        probs = Rx.tile("probs", [P, 3, N])
        ptl = Rx.tile("ptl", [P, 3, 2, P])
        ptc = Rx.tile("ptc", [P, P])
        start_y = Rx.at
        h32 = Region(start_x, 4 * KT * N).tile("h32", [P, KT, N])
        ck_tok = Region(start_x + 4 * KT * N, 2048 * 3).tile("ck_tok", [P, HEADS, HD])
        Rs = Region(start_y)
        x_tok = Rs.tile("x_tok", [P, NT, D])
        Rs2 = Region(start_b)
        vec_rows = Rs2.tile("vec_rows", [V_ROWS, P])
        tap_rows = Rs2.tile("tap_rows", [2 * CK, P])
        Ry = Region(start_y)
        u_tok = Ry.tile("u_tok", [P, NT, FW])
        lat_w = Ry.tile("lat_w", [P, 2, 2 * NLAT])
        ctx_w = Ry.tile("ctx_w", [P, 2 * NCTX])
        feat_w = Ry.tile("feat_w", [P, 2, P])
        z_cs = Ry.tile("z_cs", [P, 2, N])
        Rc = Region(start_y)
        zpad = Rc.tile("zpad", [P, 2, ZW])
        acc = Rc.tile("acc", [P, 2, CO])
        csq = Rc.tile("csq", [P, 2, CO])
        crs = Rc.tile("crs", [P, CO])
        prod = Rc.tile("prod", [P, CO])
        Rg = Region(start_x)
        mg_hi = Rg.tile("mg_hi", [P, KT, N], F32R)
        mg_lo = Rg.tile("mg_lo", [P, KT, N], F32R)
        th = Rg.tile("th", [P, 3, N])
        mg = Rg.tile("mg", [P, 2, N])
        mt = Rg.tile("mt", [P, 2, N])
        Rm = Region(start_h, 2 * 4 * KT * N)
        ht_hi = Rm.tile("ht_hi", [P, NT, D], F32R)
        ht_lo = Rm.tile("ht_lo", [P, NT, D], F32R)
        Rm = Region(start_b, 4 * 16 * N)
        sel = Rm.tile("sel", [P, NT, P], F32R)
        selT = Rm.tile("selT", [P, N], F32R)
        hg_hi = Rm.tile("hg_hi", [P, KT, P], F32R)
        hg_lo = Rm.tile("hg_lo", [P, KT, P], F32R)
        hd_hi = Rm.tile("hd_hi", [P, 2, P], F32R)
        hd_lo = Rm.tile("hd_lo", [P, 2, P], F32R)
        Rm = Region(start_x)
        y_hi = Rm.tile("y_hi", [P, D], F32R)
        y_lo = Rm.tile("y_lo", [P, D], F32R)
        hg32 = Rm.tile("hg32", [P, D])
        th_e = Rm.tile("th_e", [P, 2, EH])
        s_e = Rm.tile("s_e", [P, 2, EH])
        hid = Rm.tile("hid", [P, 2, EH])
        out_t = Rm.tile("out_t", [P, 2, D])
        junk = Rm.tile("junk", [P, D])
        fg_b = Rm.tile("fg_b", [P, D])
        Rm = Region(start_x + 6 * 4 * KT * N // 2)
        h2T = Rm.tile("h2T", [P, KT, N])
        lgT = Rm.tile("lgT", [GROUPS + NE, N])
        lg = Rm.tile("lg", [P, NT, GROUPS + NE])
        og = Rm.tile("og", [P, NT, GROUPS])
        pr = Rm.tile("pr", [P, NT, EPG, GROUPS])
        e_sel = Rm.tile("e_sel", [P, NT, EPG])
        o1 = Rm.tile("o1", [P, NT, EPG])
        o2 = Rm.tile("o2", [P, NT, EPG])
        comb = Rm.tile("comb", [P, NT, EPG])
        rk = Rm.tile("rk", [P, NT, GROUPS])
        key = Rm.tile("key", [P, NT])
        i_base = Rm.tile("i_base", [P, 16])
        keysh = Rm.tile("keysh", [P, 16, NT])
        goff = Rm.tile("goff", [P, GROUPS])
        tot = Rm.tile("tot", [P, NT, GROUPS])
        cmb = Rm.tile("cmb", [P, EPG])
        over = Rm.tile("over", [P, 1], I32)
        fin = Rm.tile("fin", [P, 8])

        ps = ctx.enter_context(nc.psum_tensor("ps", [P, 8, 512], F32))

        def sem(name):
            return ctx.enter_context(nc.semaphore(name))

        raw_ready = [sem(f"raw_ready{i}") for i in range(RING)]
        hi_ready, lo_ready, chunk_done = sem("hi_ready"), sem("lo_ready"), sem("chunk_done")
        rows_in, taps_in, x_in, ck_in, cv_in, dft_in, bias_in, gr_in, fg_in = (
            sem(n) for n in ("rows_in", "taps_in", "x_in", "ck_in", "cv_in", "dft_in", "bias_in", "gr_in", "fg_in"))
        ident_step, consts_ready, mask_step, pool_step = (
            sem(n) for n in ("ident_step", "consts_ready", "mask_step", "pool_step"))
        vec_turned, vec_ready, cond_tanh, cond_ready = (
            sem(n) for n in ("vec_turned", "vec_ready", "cond_tanh", "cond_ready"))
        x_turned, x_ready, sq_ready, ssq_step, std_ready, norm_ready = (
            sem(n) for n in ("x_turned", "x_ready", "sq_ready", "ssq_step", "std_ready", "norm_ready"))
        modrow_ready, mod_turned, mod_copied, mod_ready = (
            sem(n) for n in ("modrow_ready", "mod_turned", "mod_copied", "mod_ready"))
        h32_ready, h_hi_ready, h_ready = sem("h32_ready"), sem("h_hi_ready"), sem("h_ready")
        q_ready, k_ready, ck_turned, ck_ready, kctx_turned, kout_ready, store_k, store_v, u_ready, v_ready = (
            sem(n) for n in ("q_ready", "k_ready", "ck_turned", "ck_ready", "kctx_turned", "kout_ready", "store_k",
                             "store_v", "u_ready", "v_ready"))
        fnet_pos, z_ready, fnet_feat, fn_hi_ready, fn_ready = (
            sem(n) for n in ("fnet_pos", "z_ready", "fnet_feat", "fn_hi_ready", "fn_ready"))
        glu_tanh, zpad_zero, z_conv, conv_done, ln_mean, ln_centred, ln_sq, ln_var, ln_std, ln_out, ln_tanh = (
            sem(n) for n in ("glu_tanh", "zpad_zero", "z_conv", "conv_done", "ln_mean", "ln_centred", "ln_sq",
                             "ln_var", "ln_std", "ln_out", "ln_tanh"))
        silu_ready, cv_hi_ready, cv_ready = sem("silu_ready"), sem("cv_hi_ready"), sem("cv_ready")
        scores, negmax, exps, probs_ready, turned, turned_out, pv_done, at_hi_ready, at_ready = (
            sem(n) for n in ("scores", "negmax", "exps", "probs_ready", "turned", "turned_out", "pv_done",
                             "at_hi_ready", "at_ready"))
        gate_tanh, merged, mg_hi_ready, mg_ready, x1_ready, h2_ready = (
            sem(n) for n in ("gate_tanh", "merged", "mg_hi_ready", "mg_ready", "x1_ready", "h2_ready"))
        logits, logits_out, logits_turned, h2_turned, ht_hi_ready, ht_ready, grp_shift, grp_exp, exp_gap, exp2 = (
            sem(n) for n in ("logits", "logits_out", "logits_turned", "h2_turned", "ht_hi_ready", "ht_ready",
                             "grp_shift", "grp_exp", "exp_gap", "exp2"))
        group_hot, ranks, routed = sem("group_hot"), sem("ranks"), sem("routed")
        sel_ready, gathered, hg_out, hg_turned, hg_hi_ready, hg_ready, sel_turned, selT_ready, cmb_ready = (
            sem(n) for n in ("sel_ready", "gathered", "hg_out", "hg_turned", "hg_hi_ready", "hg_ready",
                             "sel_turned", "selT_ready", "cmb_ready"))
        silu_e, x2_ready, y_zero, y_last, y_hi_last, y_lo_last, combined_last = (
            sem(n) for n in ("silu_e", "x2_ready", "y_zero", "y_last", "y_hi_last", "y_lo_last", "combined_last"))
        e_tanh, hid_ready, hid_turned, hd_hi_ready, hd_ready, y_hi_ready, y_ready, combined, added = (
            sem(n) for n in ("e_tanh", "hid_ready", "hid_turned", "hd_hi_ready", "hd_ready", "y_hi_ready",
                             "y_ready", "combined", "added"))
        out_turned, out_std, out_ready = sem("out_turned"), sem("out_std"), sem("out_ready")
        store_y = [sem(f"store_y{t}") for t in range(NT)]
        act_step, dve_step = sem("act_step"), sem("dve_step")

        w_mod_v = w_mod[0].rearrange("(k p) c -> p k c", p=P)
        w_in_v = w_in[0].rearrange("(k p) c -> p k c", p=P)
        w_out_v = w_out[0].rearrange("(k p) c -> p k c", p=P)
        w_at_v = w_attn_o[0].rearrange("(k p) c -> p k c", p=P)
        w_fn_v = w_fnet[0].rearrange("(k p) c -> p k c", p=P)
        w_cv_v = w_conv_o[0].rearrange("(k p) c -> p k c", p=P)
        w1_v = w1[0].rearrange("e (k p) f -> e p k f", p=P)
        w3_v = w3[0].rearrange("e (k p) f -> e p k f", p=P)
        w2_v = w2[0].rearrange("e (k p) d -> e p k d", p=P)

        def slot_loads(kind, j, r):
            full = raw[:, r, :].rearrange("p (k c) -> p k c", k=KT)
            halves = raw[:, r, :].rearrange("p (h k c) -> p h k c", h=2, k=KT)
            if kind == "mod":
                return [(full, w_mod_v[:, :, 256 * j:256 * j + 256])]
            if kind in ("q", "k", "v", "uf"):
                c0 = {"q": COL_Q, "k": COL_K, "v": COL_V, "uf": COL_F}[kind] + 256 * j
                return [(full, w_in_v[:, :, c0:c0 + 256])]
            if kind == "uc":
                return [(full[:, :, 128 * i:128 * i + 128], w_in_v[:, :, COL_C + CW * i + P * j:COL_C + CW * i + P * j + P])
                        for i in range(2)]
            cols = slice(P * j, P * j + P)
            gate = lambda b: w_in_v[:, :, COL_G + D * b + P * j:COL_G + D * b + P * j + P]
            if kind == "g0b":
                return [(halves[:, 0, :, :], gate(0)), (halves[:, 1, 0:4, :], w_at_v[:, :, cols]),
                        (halves[:, 1, 4:6, :], w_fn_v[:, :, cols]), (halves[:, 1, 6:8, :], w_cv_v[:, :, cols])]
            if kind == "g12":
                return [(halves[:, i, :, :], gate(1 + i)) for i in range(2)]
            return [(full, w_out_v[:, :, 256 * j:256 * j + 256])]

        def item_loads(kind, e, g, r):
            ex = bass.ds(g * EPG + e, 1)
            if kind == "C":
                return [(raw[:, r, :].rearrange("p (k c) -> p k c", k=2), w2_v[ex].rearrange("e p k d -> (e p) k d"))]
            full = raw[:, r, :].rearrange("p (k w c) -> p k w c", k=4, w=2)
            ks = slice(0, 4) if kind == "A" else slice(4, 8)
            return [(full[:, :, i, :], w[ex].rearrange("e p k f -> (e p) k f")[:, ks, :]) for i, w in enumerate((w1_v, w3_v))]

        N_LOADS = {"mod": 1, "q": 1, "k": 1, "v": 1, "uf": 1, "uc": 2, "g0b": 4, "g12": 2, "wo": 1, "A": 2, "B": 2, "C": 1}
        seen = [0] * RING
        pre_count = []
        for s, (kind, j) in enumerate(SLOTS):
            seen[s % RING] += 16 * N_LOADS[kind]
            pre_count.append(seen[s % RING])
        per_item = [0] * RING
        item_count = []
        for s, (kind, e) in enumerate(ITEM):
            r = (PRE + s) % RING
            per_item[r] += 16 * N_LOADS[kind]
            item_count.append(seen[r] + per_item[r])

        def raw_chunk(slot_kind, r, half):
            if slot_kind in BY_COLUMNS:
                return raw[:, r, :].rearrange("p (k c) -> p k c", k=KT)[:, :, P * half:P * half + P]
            return raw[:, r, CH * half:CH * half + CH]

        def cut_chunk(t, slot_kind, b):
            return t[:, b, :].rearrange("p (k c) -> p k c", k=KT) if slot_kind in BY_COLUMNS else t[:, b, :]

        def mod_bank(j):
            return 5 + j % 2 if j in MOD_LAST else j % 2

        def gate_bank(d, b):
            return 3 + (3 * d + (b + 2) % 3) % 2

        def act_split(act, i):
            kind, r = SLOTS[i // 2][0], (i // 2) % RING
            if i % 2 == 0:
                act.wait_ge(raw_ready[r], pre_count[i // 2])
            if i >= SPLIT:
                act.wait_ge(chunk_done, i - SPLIT + 1)
            act.activation(cut_chunk(w_hi, kind, i % SPLIT), raw_chunk(kind, r, i % 2), ACT.Copy).then_inc(hi_ready, 1)

        def dve_split(dve, i):
            kind, r = SLOTS[i // 2][0], (i // 2) % RING
            dve.wait_ge(hi_ready, i + 1)
            dve.tensor_tensor(cut_chunk(w_lo, kind, i % SPLIT), raw_chunk(kind, r, i % 2),
                              cut_chunk(w_hi, kind, i % SPLIT).bitcast(F32), ALU.subtract).then_inc(lo_ready, 1)

        def act_split_item(act, it, i):
            r, b = (PRE + i // 2) % RING, (PRE_CH + i) % SPLIT
            if i % 2 == 0:
                act.wait_ge(raw_ready[r], it * per_item[r] + item_count[i // 2])
            act.wait_ge(chunk_done, it * ITEM_CH + (PRE_CH + i - SPLIT + 1))
            act.activation(w_hi[:, b, :], raw[:, r, CH * (i % 2):CH * (i % 2) + CH], ACT.Copy).then_inc(hi_ready, 1)

        def dve_split_item(dve, it, i):
            r, b = (PRE + i // 2) % RING, (PRE_CH + i) % SPLIT
            dve.wait_ge(hi_ready, it * ITEM_CH + (PRE_CH + i + 1))
            dve.tensor_tensor(w_lo[:, b, :], raw[:, r, CH * (i % 2):CH * (i % 2) + CH], w_hi[:, b, :].bitcast(F32),
                              ALU.subtract).then_inc(lo_ready, 1)

        up_chunks, down_chunks, order = {}, {}, []
        for s, (kind, e) in enumerate(ITEM):
            (down_chunks if kind == "C" else up_chunks).setdefault(e, []).extend([2 * s, 2 * s + 1])
        for s, (kind, e) in enumerate(ITEM):
            for half in range(2):
                order.append(("down" if kind == "C" else "up", e, (2 if kind == "B" else 0) + half, 2 * s + half))

        def rounds(eng, item):
            with eng.Fori(0, GROUPS) as g:
                item(g, g)
            eng.wait_ge(routed, 1)
            n_over = eng.value_load(over[0:1, 0:1])
            with eng.If(n_over > 0):
                with eng.Fori(1, ROUNDS) as r:
                    with eng.Fori(0, GROUPS) as g:
                        item(r * GROUPS + g, g)

        block = ctx.enter_context(nc.Block())

        @block.sync
        def _(sp):
            for t in range(NT):
                src = x_prompt[0] if t == 0 else x_sample[0, (t - 1) * P:t * P, :]
                sp.dma_start(x_tok[:, t, :], src).then_inc(x_in, 16)
            for s, (kind, j) in enumerate(SLOTS):
                if s >= RING:
                    sp.wait_ge(lo_ready, 2 * (s - RING) + 2)
                for dst, src in slot_loads(kind, j, s % RING):
                    sp.dma_start(dst, src).then_inc(raw_ready[s % RING], 16)

            def item(it, g):
                for s, (kind, e) in enumerate(ITEM):
                    sp.wait_ge(lo_ready, it * ITEM_CH + 2 * (PRE + s - RING) + 2)
                    r = (PRE + s) % RING
                    for dst, src in item_loads(kind, e, g, r):
                        sp.dma_start(dst, src).then_inc(raw_ready[r], 16)

            rounds(sp, item)
            for t in range(NT):
                dst = y_prompt[0] if t == 0 else y_sample[0, (t - 1) * P:t * P, :]
                sp.wait_ge(out_ready, t + 1)
                sp.dma_start(dst, out_t[:, t % 2, :]).then_inc(store_y[t], 16)
            for t in range(NT):
                sp.wait_ge(store_y[t], 16)
            sp.wait_ge(store_k, 16)
            sp.wait_ge(store_v, 16)

        @block.gpsimd
        def _(pool):
            pool.memset(ident[:], 0.0).then_inc(ident_step, 1)
            pool.memset(tri[:], 1.0).then_inc(ident_step, 1)
            pool.wait_ge(ident_step, 2)
            pool.affine_select(out=ident[:], in_=ident[:], compare_op=ALU.not_equal, fill=1.0, base=0,
                               pattern=[[-1, P]], channel_multiplier=1).then_inc(consts_ready, 1)
            pool.memset(ones[:], 1.0).then_inc(consts_ready, 1)
            pool.memset(eps_t[:], EPS).then_inc(consts_ready, 1)
            pool.affine_select(out=tri[:], in_=tri[:], compare_op=ALU.is_gt, fill=0.0, base=0,
                               pattern=[[1, P]], channel_multiplier=-1).then_inc(consts_ready, 1)
            pool.iota(iota_s[:], pattern=[[1, P]], base=0, channel_multiplier=0,
                      allow_small_or_imprecise_dtypes=True).then_inc(consts_ready, 1)
            pool.wait_ge(bias_in, 16 * 2 * HEADS)
            for half in range(2):
                b = bias[64 * half:64 * half + 64].rearrange("p h s c -> p (h s) c")
                lo, hi = b[:, :, 0:GRID_W - 16], b[:, :, 16:GRID_W]
                pool.affine_select(out=lo, in_=lo, compare_op=ALU.is_ge, fill=NEG, base=8,
                                   pattern=[[0, HEADS * NDR], [1, GRID_W - 16]], channel_multiplier=-1)\
                    .then_inc(mask_step, 1)
                pool.wait_ge(mask_step, 2 * half + 1)
                pool.affine_select(out=hi, in_=hi, compare_op=ALU.is_ge, fill=NEG, base=7 - 16,
                                   pattern=[[0, HEADS * NDR], [-1, GRID_W - 16]], channel_multiplier=1)\
                    .then_inc(mask_step, 1)
            pool.wait_ge(mask_step, 4)
            pool.wait_ge(z_conv, 2)
            step = 0
            for t in range(CK):
                if t == 0:
                    pool.tensor_scalar(acc[:, 1, :], zpad[:, 1, 0:CO], taps[:, 1, 0:1], vec_t[:, V_CB + 1:V_CB + 2],
                                       ALU.mult, ALU.add).then_inc(pool_step, 1)
                    step += 1
                    continue
                pool.tensor_scalar(prod[:], zpad[:, 1, t:t + CO], taps[:, 1, t:t + 1], None, ALU.mult)\
                    .then_inc(pool_step, 1)
                step += 1
                pool.wait_ge(pool_step, step)
                pool.tensor_tensor(acc[:, 1, :], acc[:, 1, :], prod[:], ALU.add)\
                    .then_inc(conv_done if t == CK - 1 else pool_step, 1)
                if t < CK - 1:
                    step += 1
                    pool.wait_ge(pool_step, step)
            pool.wait_ge(mg_ready, KT)
            pool.iota(i_base[:], pattern=[[P, 4], [N, 4]], base=0, channel_multiplier=0,
                      allow_small_or_imprecise_dtypes=True).then_inc(consts_ready, 1)
            pool.iota(goff[:], pattern=[[N, GROUPS]], base=0, channel_multiplier=0,
                      allow_small_or_imprecise_dtypes=True).then_inc(consts_ready, 1)

        @block.scalar
        def _(act):
            rows = 0
            for at, src, n in ((V_CTX, c_ctx, 8), (V_C, c[0], 8), (V_N1, norm1_g[0], 8), (V_N2, norm2_g[0], 8),
                               (V_BM, b_mod[0], 48), (V_CB, conv_b[0], 2), (V_LG, conv_ln_g[0], 2), (V_LB, conv_ln_b[0], 2)):
                act.dma_start(vec_rows[at:at + n, :], src.rearrange("(a p) -> a p", p=P)).then_inc(rows_in, 16)
                rows += 16
            for i in range(2):
                act.dma_start(tap_rows[CK * i:CK * i + CK, :], conv_dw[0, :, P * i:P * i + P]).then_inc(taps_in, 16)
            act.dma_start(ck_tok[:], cache_k[0, 0].rearrange("h n d -> n h d")).then_inc(ck_in, 16)
            act.dma_start(cv_tok[:], cache_v[0, 0].rearrange("h n d -> n h d")).then_inc(cv_in, 16)
            for half in range(2):
                for h in range(HEADS):
                    at = (h * RPB_R + 5 - half) * RPB_C * GRID_W + 15
                    act.dma_start(bias[64 * half:64 * half + 64, h, :, :],
                                  bass.AP(rpb.tensor, at, [[RPB_C - 1, 64], [RPB_C * GRID_W, NDR], [1, GRID_W]])).then_inc(bias_in, 16)
            act.dma_start(w_gr[:, :, 0:GROUPS], w_group[0].rearrange("(k p) g -> p k g", p=P)).then_inc(gr_in, 16)
            act.dma_start(w_gr[:, :, GROUPS:], w_router[0].rearrange("(k p) g -> p k g", p=P)).then_inc(gr_in, 16)
            act.dma_start(b_gr[:, 0:GROUPS], b_group.to_broadcast([P, GROUPS])).then_inc(gr_in, 16)
            act.dma_start(b_gr[:, GROUPS:], b_router.to_broadcast([P, NE])).then_inc(gr_in, 16)

            step = 0

            def link(ins):
                nonlocal step
                step += 1
                ins.then_inc(act_step, 1)
                act.wait_ge(act_step, step)

            split_at = 0

            def split_to(n):
                nonlocal split_at
                while split_at < min(n, PRE_CH):
                    act_split(act, split_at)
                    split_at += 1

            act.wait_ge(vec_ready, 1)
            act.activation(cond_t[:].rearrange("p a k -> p (a k)"), vec_t[:, V_CTX:V_CTX + 16], ACT.Tanh, scale=0.5)\
                .then_inc(cond_tanh, 1)

            def square(n, src):
                if n >= 2:
                    act.wait_ge(ssq_step, n - 1)
                act.activation(sq[:, n % 2, :], src, ACT.Square).then_inc(sq_ready, 1)

            def std(n, bank):
                act.wait_ge(ssq_step, KT * (n + 1))
                act.activation(rstd[:], ps[:, bank, 0:N], ACT.Sqrt, bias=eps_t[:, 0:1], scale=1.0 / D)\
                    .then_inc(std_ready, 1)

            act.wait_ge(consts_ready, 3)
            for k in range(KT):
                act.wait_ge(x_ready, k + 1)
                square(k, xT[:, k, :])
            split_to(4)
            std(0, 7)
            for a in range(2):
                act.dma_start(lat_w[:, a, :], dft_lat[P * a:P * a + P, :]).then_inc(dft_in, 16)
            act.dma_start(ctx_w[:], dft_ctx).then_inc(dft_in, 16)
            act.dma_start(feat_w[:].rearrange("p a c -> p (a c)"), dft_feat).then_inc(dft_in, 16)

            def mod_row(j):
                act.wait_ge(chunk_done, first_chunk("mod", j) + 2)
                if j >= 2:
                    act.wait_ge(mod_turned, j - 1)
                bank = mod_bank(j)
                act.activation(modrow[:, j % 2, :], ps[0:4, bank, 0:256], ACT.Copy).then_inc(modrow_ready, 1)

            for j in range(8):
                split_to(2 * j + 4)
                mod_row(j)
                split_to(2 * j + 5)
            for k in range(KT):
                act.wait_ge(h32_ready, k + 1)
                act.activation(h_hi[:, k, :], h32[:, k, :], ACT.Copy).then_inc(h_hi_ready, 1)
            c_q, c_k = first_chunk("q"), first_chunk("k")
            for n in range(4):
                split_to(c_q + n + 4)
                act.wait_ge(chunk_done, c_q + n + 1)
                if n == 0:
                    act.wait_ge(h_ready, KT)
                act.activation(qT[:, n, :], ps[:, n % 2, 0:N], ACT.Copy, scale=HD ** -0.5).then_inc(q_ready, 1)
            for n in range(4):
                split_to(c_k + n + 4)
            act.wait_ge(ck_turned, 1)
            act.activation(ckT[:].rearrange("p a n -> p (a n)"), ps[:, 5, :], ACT.Copy).then_inc(ck_ready, 1)
            act.wait_ge(kout_ready, 1)
            act.dma_start(new_k[0, 0].rearrange("h n d -> n h d"), k_out[:].rearrange("p (h d) -> p h d", h=HEADS))\
                .then_inc(store_k, 16)

            def exp_unit(u):
                b, part = u % 3, u % 3
                act.wait_ge(negmax, u + 1)
                if part == 0:
                    act.activation(probs[:, b, 0:NCTX], ps[:, 3 + u % 2, 0:NCTX], ACT.Exp, bias=stats[:, b, 2:3],
                                   accum_out=stats[:, b, 3:4]).then_inc(exps, 1)
                else:
                    act.activation(probs[:, b, 0:NLAT], probs[:, b, 0:NLAT], ACT.Exp, bias=stats[:, b, 2:3],
                                   accum_out=stats[:, b, 3:4])
                    act.activation(probs[:, b, NLAT:N], ps[:, 3 + u % 2, NLAT:N], ACT.Exp, bias=stats[:, b, 2:3],
                                   accum_out=stats[:, b, 4:5]).then_inc(exps, 1)

            def turned_copy(u):
                h, part = u // 3, u % 3
                act.wait_ge(turned, u + 1)
                if h >= 1:
                    act.wait_ge(pv_done, h)
                if part == 0:
                    act.activation(ptc[:], ps[:, 5 + u % 2, 0:P], ACT.Copy).then_inc(turned_out, 1)
                else:
                    act.activation(ptl[:, :, part - 1, :], ps[:, 5 + u % 2, 0:3 * P].rearrange("p (a q) -> p a q", a=3),
                                   ACT.Copy).then_inc(turned_out, 1)

            for what, n in WINDOW:
                if what == "chunk":
                    kind, j = SLOTS[n // 2]
                    split_to(n + 4)
                elif what == "mod":
                    c0 = first_chunk("mod", n)
                    split_to(c0 + 5)
                    mod_row(n)
                elif what == "glu":
                    act.wait_ge(chunk_done, first_chunk("uc", n) + 2)
                    act.wait_ge(zpad_zero, 1)
                    act.activation(csq[:, n, 0:N], ps[:, 4 + 2 * n, 0:N], ACT.Tanh, scale=0.5).then_inc(glu_tanh, 1)
                elif what == "fpos":
                    act.wait_ge(fnet_pos, 2 * n + 1)
                    if n == 1:
                        act.wait_ge(fnet_feat, 1)
                    act.activation(z_cs[:, :, 0:NCTX], ps[:, 0, 0:2 * NCTX].rearrange("p (a n) -> p a n", a=2), ACT.Copy)
                    act.wait_ge(fnet_pos, 2 * n + 2)
                    act.activation(z_cs[:, :, NCTX:N], ps[:, 1, 0:2 * NLAT].rearrange("p (a n) -> p a n", a=2), ACT.Copy)\
                        .then_inc(z_ready, 1)
                elif what == "ffeat":
                    act.wait_ge(fnet_feat, n + 1)
                    act.activation(fn_hi[:, n, :], ps[:, 2, 0:N], ACT.Copy).then_inc(fn_hi_ready, 1)
                elif what == "unit" and n < UNITS:
                    exp_unit(n)
                elif what == "turn" and 0 <= n:
                    turned_copy(n)
                    if n % 6 == 5:
                        pair = n // 6
                        act.wait_ge(pv_done, 2 * pair + 2)
                        act.activation(at_hi[:, pair, :], ps[:, 7, 0:N], ACT.Copy).then_inc(at_hi_ready, 1)
            act.wait_ge(v_ready, 2)
            act.dma_start(new_v[0, 0].rearrange("h n d -> n h d"), v_tok[:, 0, :].rearrange("p (h d) -> p h d", h=HEADS))\
                .then_inc(store_v, 16)
            act.wait_ge(ln_centred, 1)
            act.activation(csq[:], acc[:], ACT.Square).then_inc(ln_sq, 1)
            act.wait_ge(ln_var, 1)
            act.activation(crs[:], ps[:, 1, 0:CO], ACT.Sqrt, bias=eps_t[:, 0:1], scale=1.0 / CW).then_inc(ln_std, 1)
            act.wait_ge(ln_out, 1)
            act.activation(csq[:], acc[:], ACT.Tanh, scale=0.5).then_inc(ln_tanh, 1)
            act.wait_ge(silu_ready, 1)
            act.wait_ge(store_k, 16)
            for at, o in ((0, 0), (LAT0, NCTX)):
                w = NCTX if o == 0 else NLAT
                act.activation(cv_hi[:, :, o:o + w], acc[:, :, at:at + w], ACT.Copy, scale=0.5).then_inc(cv_hi_ready, 1)

            act.wait_ge(store_v, 16)
            for kind, j in UG:
                c0 = first_chunk(kind, j)
                if kind == "mod":
                    split_to(c0 + 5)
                    mod_row(j)
                    continue
                for b, i in ((1, c0), (2, c0 + 1)) if kind == "g12" else ((0, c0),):
                    split_to(i + 4)
                    act.wait_ge(chunk_done, i + 1)
                    if j >= 1:
                        act.wait_ge(merged, j)
                    act.activation(th[:, b, :], ps[:, gate_bank(j, b), 0:N], ACT.Tanh, scale=0.5).then_inc(gate_tanh, 1)
                    if b == 1 and j >= 1:
                        act.activation(mg_hi[:, j - 1, :], mg[:, (j - 1) % 2, :], ACT.Copy, scale=0.5)\
                            .then_inc(mg_hi_ready, 1)
                if kind == "g0b":
                    split_to(c0 + 5)
            act.wait_ge(merged, KT)
            act.activation(mg_hi[:, KT - 1, :], mg[:, (KT - 1) % 2, :], ACT.Copy, scale=0.5).then_inc(mg_hi_ready, 1)
            for n in range(KT):
                split_to(2 * WO0 + n + 4)
                act.wait_ge(x1_ready, n + 1)
                square(KT + n, xT[:, n, :])
            std(1, 2)
            act.wait_ge(logits, 1)
            act.activation(lgT[:], ps[0:GROUPS + NE, 3, 0:N], ACT.Copy).then_inc(logits_out, 1)
            tok_banks = (0, 4, 6)
            for t in range(NT):
                act.wait_ge(h2_turned, t + 1)
                act.activation(ht_hi[:, t, :], ps[:, tok_banks[t]:tok_banks[t] + 2, :].rearrange("p a n -> p (a n)"),
                               ACT.Copy).then_inc(ht_hi_ready, 1)
            act.wait_ge(grp_shift, 1)
            act.activation(rt[:, :, 8:12], rt[:, :, 4:8], ACT.Exp).then_inc(grp_exp, 1)
            act.wait_ge(exp_gap, 1)
            act.activation(rt[:, :, 21:22], rt[:, :, 20:21], ACT.Exp).then_inc(exp2, 1)

            def hg_copy(nx):
                act.wait_ge(gathered, nx + 1)
                act.activation(hg32[:], ps[:, 5:7, :].rearrange("p a n -> p (a n)"), ACT.Copy).then_inc(hg_out, 1)

            def hg_high(nx):
                act.wait_ge(hg_turned, nx + 1)
                act.activation(hg_hi[:].rearrange("p k s -> p (k s)"), ps[:, 5:7, :].rearrange("p a n -> p (a n)"),
                               ACT.Copy).then_inc(hg_hi_ready, 1)

            hg_copy(0)
            hg_high(0)
            act.dma_start(fg_b[:], final_g.rearrange("(a n) -> a n", a=1).to_broadcast([P, D])).then_inc(fg_in, 16)

            def item(it, g):
                for i in range(3):
                    act_split_item(act, it, i)
                act.wait_ge(gathered, it + 1)
                act.activation(cmb[:], ps[:, 7, 0:EPG], ACT.Copy).then_inc(cmb_ready, 1)

                def tanh_e(e):
                    act.wait_ge(chunk_done, it * ITEM_CH + PRE_CH + up_chunks[e][3] + 1)
                    if e >= 2:
                        act.wait_ge(hid_ready, it * EPG + e - 1)
                    act.activation(th_e[:, e % 2, :], ps[:, e % 2, 0:EH], ACT.Tanh, scale=0.5).then_inc(e_tanh, 1)

                def hd_high(e):
                    act.wait_ge(hid_turned, it * EPG + e + 1)
                    act.activation(hd_hi[:].rearrange("p a n -> p (a n)"), ps[:, 4, 0:2 * P], ACT.Copy).then_inc(hd_hi_ready, 1)

                for what, e, part, i in order:
                    if what == "up" and part == 1 and e == 1:
                        tanh_e(0)
                    if what == "down" and part == 1 and e < EPG - 1:
                        tanh_e(e + 1)
                    if what == "up" and part == 3 and e >= 1:
                        hd_high(e - 1)
                    if i + 3 < ITEM_CH:
                        act_split_item(act, it, i + 3)
                    if i == 0:
                        act.wait_ge(y_zero, 1)
                        act.wait_ge(chunk_done, it * ITEM_CH + PRE_CH)
                        act.activation(y_hi[:], ps[:, 2:4, :].rearrange("p a n -> p (a n)"), ACT.Copy)\
                            .then_inc(y_hi_ready, 1)
                    if what == "up" and part == 2 and e == SEL_TURN:
                        act.wait_ge(sel_turned, it + 1)
                        act.activation(selT[:], ps[:, 7, P:4 * P], ACT.Copy).then_inc(selT_ready, 1)
                    if what == "up" and part == 3 and e == EPG - 1:
                        hg_copy(it + 1)
                    if what == "down" and part == 1 and e == EPG - 2:
                        hg_high(it + 1)
                        hd_high(EPG - 1)

            rounds(act, item)
            act.wait_ge(y_last, 1)
            act.activation(y_hi[:], ps[:, 2:4, :].rearrange("p a n -> p (a n)"), ACT.Copy).then_inc(y_hi_last, 1)
            out_banks = (0, 2, 5)
            for t in range(NT):
                act.wait_ge(out_turned, t + 1)
                link(act.activation(junk[:], ps[:, out_banks[t]:out_banks[t] + 2, :].rearrange("p a n -> p (a n)"),
                                    ACT.Square, accum_out=fin[:, t:t + 1]))
                act.activation(fin[:, 3 + t:4 + t], fin[:, t:t + 1], ACT.Sqrt, bias=eps_t[:, 0:1], scale=1.0 / D)\
                    .then_inc(out_std, 1)

        @block.vector
        def _(dve):
            step = 0

            def link(ins):
                nonlocal step
                step += 1
                ins.then_inc(dve_step, 1)
                dve.wait_ge(dve_step, step)

            split_at = 0

            def split_to(n):
                nonlocal split_at
                while split_at < min(n, PRE_CH):
                    dve_split(dve, split_at)
                    split_at += 1

            dve.wait_ge(vec_turned, 1)
            dve.tensor_copy(vec_t[:], ps[:, 3, 0:V_ROWS]).then_inc(vec_ready, 1)
            dve.wait_ge(vec_turned, 2)
            link(dve.tensor_scalar(taps[:].rearrange("p a t -> p (a t)"), ps[:, 2, 0:2 * CK], 0.5, None, ALU.mult))
            dve.wait_ge(cond_tanh, 1)
            both = cond[:].rearrange("p a k -> p (a k)")
            link(dve.scalar_tensor_tensor(out=both, in0=cond_t[:].rearrange("p a k -> p (a k)"), scalar=1.0,
                                          in1=vec_t[:, V_CTX:V_CTX + 16], op0=ALU.add, op1=ALU.mult))
            link(dve.tensor_scalar(both, both, 0.5, None, ALU.mult))
            link(dve.tensor_copy(cond4[:, :, 0:2], cond[:].rearrange("p a k -> p k a")))
            dve.tensor_tensor(cond4[:, :, 2:4], cond[:].rearrange("p a k -> p k a"), cond4[:, :, 0:2].bitcast(F32),
                              ALU.subtract).then_inc(cond_ready, 1)
            for k in range(KT):
                dve.wait_ge(x_turned, k + 1)
                dve.tensor_copy(xT[:, k, :], ps[:, 4 + k % 3, 0:N]).then_inc(x_ready, 1)
            dve.wait_ge(std_ready, 1)
            link(dve.reciprocal(rstd[:], rstd[:]))
            for k in range(KT):
                split_to(2 * k + 4)
                dve.tensor_tensor(h32[:, k, :], xT[:, k, :], rstd[:], ALU.mult)
                split_to(2 * k + 5)

            def mod_finish(first, n, bank):
                dve.tensor_copy(mod_tmp[:, 0:n, :], ps[:, bank, 4 * first:4 * (first + n)]
                                .rearrange("p (t r) -> p t r", r=4)).then_inc(mod_copied, 1)
                dve.wait_ge(mod_copied, {0: 1, 2 * MOD_WINDOW[0]: 2, 2 * MOD_LAST[0]: 3}[first])
                m = modT[:, first:first + n, :]
                link(dve.tensor_tensor(m, mod_tmp[:, 0:n, 0:2], mod_tmp[:, 0:n, 2:4], ALU.add))
                for a in range(2):
                    ins = dve.tensor_tensor(modT[:, first:first + n, a], modT[:, first:first + n, a],
                                            vec_t[:, V_BM + first:V_BM + first + n], ALU.add)
                    link(ins)

            def norm_scale(dst, mod, vec):
                for a in range(2):
                    link(dve.scalar_tensor_tensor(out=dst[:, :, a], in0=modT[:, 8 * mod:8 * mod + 8, a], scalar=1.0,
                                                  in1=vec_t[:, vec:vec + 8], op0=ALU.add, op1=ALU.mult))

            def modulate(k, t, scale, shift):
                for a, b, which in SEG:
                    ins = dve.tensor_scalar(t[:, k, a:b], t[:, k, a:b], scale[:, k, which:which + 1],
                                            modT[:, 8 * shift + k, which:which + 1], ALU.mult, ALU.add)
                return ins

            dve.wait_ge(mod_turned, 8)
            mod_finish(0, 16, 2)
            norm_scale(scale1, 1, V_N1)
            for k in range(KT):
                modulate(k, h32, scale1, 0).then_inc(h32_ready, 1)
            for k in range(KT):
                dve.wait_ge(h_hi_ready, k + 1)
                dve.tensor_tensor(h_lo[:, k, :], h32[:, k, :], h_hi[:, k, :].bitcast(F32), ALU.subtract).then_inc(h_ready, 1)
            c_q, c_k = first_chunk("q"), first_chunk("k")
            for n in range(4):
                split_to(c_q + n + 4)
            dve.wait_ge(h_ready, KT)
            for n in range(4):
                split_to(c_k + n + 4)
                dve.wait_ge(chunk_done, c_k + n + 1)
                dve.tensor_copy(kT[:, n, :], ps[:, n % 2, 0:N]).then_inc(k_ready, 1)
            dve.wait_ge(kctx_turned, 1)
            dve.tensor_copy(k_out[:], ps[:, 6, :]).then_inc(kout_ready, 1)

            def max_unit(u):
                b, part, h = u % 3, u % 3, u // 3
                dve.wait_ge(scores, u + 1)
                if u >= 3:
                    dve.wait_ge(turned, u - 2)
                s = ps[:, 3 + u % 2, :]
                if part == 0:
                    link(dve.reduce_max(stats[:, b, 0:1], s[:, 0:NCTX], AX))
                    dve.tensor_scalar(stats[:, b, 2:3], stats[:, b, 0:1], -1.0, None, ALU.mult).then_inc(negmax, 1)
                    return
                t = part - 1
                if u == 1:
                    dve.wait_ge(mask_step, 4)
                rows = bias[:, h, 2 - 2 * t:6 - 2 * t, :].rearrange("p s c -> p (s c)")
                dve.reduce_max(stats[:, b, 0:1], s[:, NLAT:N], AX)
                link(dve.tensor_tensor_reduce(out=probs[:, b, 0:NLAT], in0=s[:, 0:NLAT], in1=rows, scale=1.0,
                                              scalar=-3e38, op0=ALU.add, op1=ALU.max, accum_out=stats[:, b, 1:2]))
                dve.tensor_scalar(stats[:, b, 2:3], stats[:, b, 0:1], stats[:, b, 1:2], -1.0, ALU.max, ALU.mult)\
                    .then_inc(negmax, 1)

            def normalise_unit(u):
                b, part = u % 3, u % 3
                dve.wait_ge(exps, u + 1)
                total, w = stats[:, b, 3:4], NCTX
                if part:
                    link(dve.tensor_tensor(stats[:, b, 5:6], stats[:, b, 3:4], stats[:, b, 4:5], ALU.add))
                    total, w = stats[:, b, 5:6], N
                link(dve.reciprocal(stats[:, b, 6:7], total))
                dve.tensor_scalar(probs[:, b, 0:w], probs[:, b, 0:w], stats[:, b, 6:7], None, ALU.mult)\
                    .then_inc(probs_ready, 1)

            conv_t = 0

            def conv_taps(n):
                nonlocal conv_t
                for _ in range(n):
                    if conv_t == CK:
                        return
                    t = conv_t
                    if t == 0:
                        ins = dve.tensor_scalar(acc[:, 0, :], zpad[:, 0, 0:CO], taps[:, 0, 0:1], vec_t[:, V_CB:V_CB + 1],
                                                ALU.mult, ALU.add)
                    else:
                        ins = dve.scalar_tensor_tensor(out=acc[:, 0, :], in0=zpad[:, 0, t:t + CO], scalar=taps[:, 0, t:t + 1],
                                                       in1=acc[:, 0, :], op0=ALU.mult, op1=ALU.add)
                    if t == CK - 1:
                        ins.then_inc(conv_done, 1)
                    else:
                        link(ins)
                    conv_t += 1

            conv_open = False
            for what, n in WINDOW:
                if what == "chunk":
                    kind, j = SLOTS[n // 2]
                    split_to(n + 4)
                    if kind in ("uf", "v") and n % 2 == 1:
                        dve.wait_ge(chunk_done, n + 1)
                        dst = u_tok[:] if kind == "uf" else v_tok[:, :, 256 * j:256 * j + 256]
                        dve.tensor_copy(dst, ps[:, 0:3, 0:256]).then_inc(u_ready if kind == "uf" else v_ready, 1)
                elif what == "mod":
                    split_to(first_chunk("mod", n) + 5)
                elif what == "glu":
                    dve.wait_ge(glu_tanh, n + 1)
                    for i, (a, b, which) in enumerate(SEG):
                        at = PAD if which == 0 else PAD + LAT0
                        ins = dve.scalar_tensor_tensor(out=zpad[:, n, at:at + b - a], in0=csq[:, n, a:b], scalar=1.0,
                                                       in1=ps[:, 3 + 2 * n, a:b], op0=ALU.add, op1=ALU.mult)
                        if i == 0:
                            link(ins)
                        else:
                            ins.then_inc(z_conv, 1)
                    conv_open = conv_open or n == 1
                elif what == "ffeat":
                    dve.wait_ge(fn_hi_ready, n + 1)
                    dve.tensor_tensor(fn_lo[:, n, :], ps[:, 2, 0:N], fn_hi[:, n, :].bitcast(F32), ALU.subtract)\
                        .then_inc(fn_ready, 1)
                    if n == 1:
                        dve.memset(zpad[:].rearrange("p a z -> p (a z)"), 0.0).then_inc(zpad_zero, 1)
                        dve.wait_ge(zpad_zero, 1)
                elif what == "unit":
                    if n < UNITS:
                        max_unit(n)
                    if 1 <= n <= UNITS:
                        normalise_unit(n - 1)
                    if conv_open:
                        if conv_t == 0:
                            dve.wait_ge(z_conv, 2)
                        conv_taps(2)
                elif what == "turn" and n >= 0 and n % 6 == 5:
                    pair = n // 6
                    dve.wait_ge(at_hi_ready, pair + 1)
                    dve.tensor_tensor(at_lo[:, pair, :], ps[:, 7, 0:N], at_hi[:, pair, :].bitcast(F32), ALU.subtract)\
                        .then_inc(at_ready, 1)
            conv_taps(CK)
            dve.wait_ge(mod_turned, MOD_WINDOW[-1] + 1)
            mod_finish(2 * MOD_WINDOW[0], 2 * len(MOD_WINDOW), 2)
            dve.wait_ge(ln_mean, 1)
            for a in range(2):
                ins = dve.scalar_tensor_tensor(out=acc[:, a, :], in0=ps[:, 0, 0:CO], scalar=-1.0 / CW, in1=acc[:, a, :],
                                               op0=ALU.mult, op1=ALU.add)
            ins.then_inc(ln_centred, 1)
            dve.wait_ge(ln_centred, 1)
            dve.wait_ge(ln_std, 1)
            link(dve.reciprocal(crs[:], crs[:]))
            dve.wait_ge(ln_sq, 1)
            for a in range(2):
                link(dve.tensor_tensor(acc[:, a, :], acc[:, a, :], crs[:], ALU.mult))
            for a in range(2):
                ins = dve.tensor_scalar(acc[:, a, :], acc[:, a, :], vec_t[:, V_LG + a:V_LG + a + 1],
                                        vec_t[:, V_LB + a:V_LB + a + 1], ALU.mult, ALU.add)
                if a == 0:
                    link(ins)
                else:
                    ins.then_inc(ln_out, 1)
            dve.wait_ge(ln_tanh, 1)
            dve.scalar_tensor_tensor(out=acc[:], in0=csq[:], scalar=1.0, in1=acc[:], op0=ALU.add, op1=ALU.mult)\
                .then_inc(silu_ready, 1)
            for i, (at, o) in enumerate(((0, 0), (LAT0, NCTX))):
                w = NCTX if o == 0 else NLAT
                dve.wait_ge(cv_hi_ready, i + 1)
                dve.scalar_tensor_tensor(out=cv_lo[:, :, o:o + w], in0=acc[:, :, at:at + w], scalar=0.5,
                                         in1=cv_hi[:, :, o:o + w].bitcast(F32), op0=ALU.mult, op1=ALU.subtract)\
                    .then_inc(cv_ready, 1)

            def merge_low(d):
                dve.wait_ge(mg_hi_ready, d + 1)
                dve.scalar_tensor_tensor(out=mg_lo[:, d, :], in0=mg[:, d % 2, :], scalar=0.5,
                                         in1=mg_hi[:, d, :].bitcast(F32), op0=ALU.mult, op1=ALU.subtract)\
                    .then_inc(mg_ready, 1)

            for kind, j in UG:
                c0 = first_chunk(kind, j)
                if kind != "g0b":
                    split_to(c0 + 5)
                    if kind == "mod" and j == MOD_LAST[-1]:
                        dve.wait_ge(mod_turned, 24)
                        mod_finish(2 * MOD_LAST[0], 2 * len(MOD_LAST), 7)
                        norm_scale(scale2, 4, V_N2)
                    if kind == "g12" and j >= 1:
                        merge_low(j - 1)
                    continue
                split_to(c0 + 5)
                dve.wait_ge(gate_tanh, 3 * j + 3)
                dve.wait_ge(chunk_done, c0 + 2)
                m = mg[:, j % 2, :]
                link(dve.scalar_tensor_tensor(out=m, in0=th[:, 0, :], scalar=1.0, in1=ps[:, 0, 0:N],
                                              op0=ALU.add, op1=ALU.mult))
                for b in (1, 2):
                    link(dve.scalar_tensor_tensor(out=mt[:, b - 1, :], in0=th[:, b, :], scalar=1.0, in1=ps[:, b, 0:N],
                                                  op0=ALU.add, op1=ALU.mult))
                    ins = dve.tensor_tensor(m, m, mt[:, b - 1, :], ALU.add)
                    if b == 1:
                        link(ins)
                    else:
                        ins.then_inc(merged, 1)
            merge_low(KT - 1)
            for n in range(KT):
                split_to(2 * WO0 + n + 4)
                dve.wait_ge(chunk_done, 2 * WO0 + n + 1)
                for a, b, which in SEG:
                    ins = dve.scalar_tensor_tensor(out=xT[:, n, a:b], in0=ps[:, n % 2, a:b],
                                                   scalar=modT[:, 16 + n, which:which + 1], in1=xT[:, n, a:b],
                                                   op0=ALU.mult, op1=ALU.add)
                ins.then_inc(x1_ready, 1)
            dve.wait_ge(x1_ready, KT)
            dve.wait_ge(std_ready, 2)
            link(dve.reciprocal(rstd[:], rstd[:]))
            for k in range(KT):
                link(dve.tensor_tensor(h2T[:, k, :], xT[:, k, :], rstd[:], ALU.mult))
                modulate(k, h2T, scale2, 3).then_inc(h2_ready, 1)
            dve.wait_ge(logits_turned, 1)
            dve.wait_ge(gr_in, 64)
            for t in range(NT):
                ins = dve.tensor_tensor(lg[:, t, :], ps[:, 2, 36 * t:36 * t + 36], b_gr[:], ALU.add)
            link(ins)

            def bc(ap, n):
                return ap.to_broadcast([P, NT, n])

            def first_max(dst, src, n, m, scratch):
                link(dve.tensor_reduce(m, src, axis=AX, op=ALU.max))
                link(dve.tensor_tensor(dst, src, bc(m, n), ALU.is_equal))
                w = iota_s[:, P - n:P].rearrange("p (a e) -> p a e", a=1).to_broadcast([P, NT, n])
                link(dve.tensor_scalar(scratch[1], w, -1.0, float(P), ALU.mult, ALU.add))
                link(dve.tensor_tensor(dst, dst, scratch[1], ALU.mult))
                link(dve.tensor_reduce(scratch[0], dst, axis=AX, op=ALU.max))
                return dve.tensor_tensor(dst, dst, bc(scratch[0], n), ALU.is_equal)

            glog = lg[:, :, 0:GROUPS]
            first_max(og[:], glog, GROUPS, rt[:, :, 0:1], (rt[:, :, 14:15], rt[:, :, 24:28])).then_inc(group_hot, 1)
            dve.wait_ge(group_hot, 1)
            dve.tensor_tensor(rt[:, :, 4:8], glog, bc(rt[:, :, 0:1], GROUPS), ALU.subtract).then_inc(grp_shift, 1)
            for t in range(NT):
                el = lg[:, t, GROUPS:].rearrange("p (g e) -> p e g", g=GROUPS)
                ins = dve.tensor_tensor(pr[:, t, :, :], el, og[:, t:t + 1, :].to_broadcast([P, EPG, GROUPS]), ALU.mult)
            link(ins)
            link(dve.tensor_reduce(e_sel[:].rearrange("p t e -> p (t e)"), pr[:].rearrange("p t e g -> p (t e) g"),
                                   axis=AX, op=ALU.add))
            link(first_max(o1[:], e_sel[:], EPG, rt[:, :, 16:17], (rt[:, :, 14:15], rt[:, :, 24:32])))
            link(dve.scalar_tensor_tensor(out=e_sel[:], in0=o1[:], scalar=NEG, in1=e_sel[:], op0=ALU.mult, op1=ALU.add))
            link(first_max(o2[:], e_sel[:], EPG, rt[:, :, 17:18], (rt[:, :, 14:15], rt[:, :, 24:32])))
            dve.tensor_tensor(rt[:, :, 20:21], rt[:, :, 17:18], rt[:, :, 16:17], ALU.subtract).then_inc(exp_gap, 1)
            dve.wait_ge(grp_exp, 1)
            link(dve.tensor_reduce(rt[:, :, 12:13], rt[:, :, 8:12], axis=AX, op=ALU.add))
            dve.wait_ge(ranks, 1)
            link(dve.tensor_copy(rk[:], ps[:, 3, 0:12].rearrange("p (t g) -> p t g", t=NT)))
            link(dve.tensor_copy(tot[:], ps[:, 3, 16:28].rearrange("p (t g) -> p t g", t=NT)))
            for t in range(1, NT):
                link(dve.tensor_tensor(rk[:, t, :], rk[:, t, :], tot[:, t - 1, :], ALU.add))
                link(dve.tensor_tensor(tot[:, t, :], tot[:, t, :], tot[:, t - 1, :], ALU.add))
            dve.wait_ge(consts_ready, 7)
            link(dve.tensor_tensor(rk[:], rk[:], goff[:].rearrange("p (a g) -> p a g", a=1).to_broadcast([P, NT, GROUPS]),
                                   ALU.add))
            link(dve.tensor_tensor(rk[:], rk[:], og[:], ALU.mult))
            link(dve.tensor_reduce(key[:], rk[:], axis=AX, op=ALU.add))
            link(dve.tensor_tensor(keysh[:], key[:].rearrange("p (a t) -> p a t", a=1).to_broadcast([P, 16, NT]),
                                   i_base[:].rearrange("p (i a) -> p i a", a=1).to_broadcast([P, 16, NT]), ALU.subtract))
            link(dve.tensor_reduce(rt[:, 0, 15:16], tot[:, NT - 1, :], axis=AX, op=ALU.max))
            dve.tensor_scalar(over[:], rt[:, 0, 15:16], float(P), None, ALU.is_gt).then_inc(routed, 1)
            dve.wait_ge(exp2, 1)
            link(dve.tensor_scalar(rt[:, :, 22:23], rt[:, :, 21:22], 1.0, None, ALU.add))
            link(dve.tensor_tensor(rt[:, :, 22:23], rt[:, :, 22:23], rt[:, :, 12:13], ALU.mult))
            link(dve.reciprocal(rt[:, :, 23:24], rt[:, :, 22:23]))
            link(dve.tensor_scalar(rt[:, :, 23:24], rt[:, :, 23:24], 0.5, None, ALU.mult))
            link(dve.tensor_tensor(rt[:, :, 21:22], rt[:, :, 21:22], rt[:, :, 23:24], ALU.mult))
            link(dve.tensor_tensor(o1[:], o1[:], bc(rt[:, :, 23:24], EPG), ALU.mult))
            link(dve.tensor_tensor(o2[:], o2[:], bc(rt[:, :, 21:22], EPG), ALU.mult))
            link(dve.tensor_tensor(comb[:], o1[:], o2[:], ALU.add))

            def select(nx):
                for t in range(NT):
                    ins = dve.tensor_scalar(sel[:, t, :], iota_s[:], keysh[:, bass.ds(nx, 1), t] if not isinstance(nx, int)
                                            else keysh[:, nx:nx + 1, t], None, ALU.is_equal)
                    ins.then_inc(sel_ready, 1)

            def hg_low(nx):
                dve.wait_ge(hg_hi_ready, nx + 1)
                dve.tensor_tensor(hg_lo[:].rearrange("p k s -> p (k s)"), ps[:, 5:7, :].rearrange("p a n -> p (a n)"),
                                  hg_hi[:].rearrange("p k s -> p (k s)").bitcast(F32), ALU.subtract).then_inc(hg_ready, 1)

            select(0)
            dve.memset(selT[:].bitcast(F32), 0.0).then_inc(selT_ready, 1)
            dve.memset(ps[:, 2:4, :].rearrange("p a n -> p (a n)"), 0.0).then_inc(y_zero, 1)
            tok_banks = (0, 4, 6)
            for t in range(NT):
                dve.wait_ge(ht_hi_ready, t + 1)
                dve.tensor_tensor(ht_lo[:, t, :], ps[:, tok_banks[t]:tok_banks[t] + 2, :].rearrange("p a n -> p (a n)"),
                                  ht_hi[:, t, :].bitcast(F32), ALU.subtract).then_inc(ht_ready, 1)
            hg_low(0)

            def add_back(k, bank, combined, n, added):
                dve.wait_ge(combined, n)
                for a, b, which in SEG:
                    dve.scalar_tensor_tensor(out=xT[:, k, a:b], in0=ps[:, bank, a:b],
                                             scalar=modT[:, 40 + k, which:which + 1], in1=xT[:, k, a:b],
                                             op0=ALU.mult, op1=ALU.add).then_inc(added, 1)

            def item(it, g):
                for i in range(3):
                    dve_split_item(dve, it, i)

                def hid_e(e):
                    n = it * EPG + e
                    dve.wait_ge(e_tanh, n + 1)
                    if e == 0:
                        dve.wait_ge(cmb_ready, it + 1)
                    if e >= 2:
                        dve.wait_ge(hid_turned, n - 1)
                    dve.scalar_tensor_tensor(out=s_e[:, e % 2, :], in0=th_e[:, e % 2, :], scalar=1.0, in1=ps[:, e % 2, 0:EH],
                                             op0=ALU.add, op1=ALU.mult).then_inc(silu_e, 1)
                    dve.wait_ge(silu_e, n + 1)
                    dve.scalar_tensor_tensor(out=hid[:, e % 2, :], in0=s_e[:, e % 2, :], scalar=cmb[:, e:e + 1],
                                             in1=ps[:, e % 2, EH:2 * EH], op0=ALU.mult, op1=ALU.mult).then_inc(hid_ready, 1)

                def hd_low(e):
                    dve.wait_ge(hd_hi_ready, it * EPG + e + 1)
                    dve.tensor_tensor(hd_lo[:].rearrange("p a n -> p (a n)"), ps[:, 4, 0:2 * P],
                                      hd_hi[:].rearrange("p a n -> p (a n)").bitcast(F32), ALU.subtract).then_inc(hd_ready, 1)

                for what, e, part, i in order:
                    if (what == "up" and part == 2 and e == 1) or (what == "up" and part == 0 and e >= 2):
                        hid_e(e - 1)
                    if what == "up" and part == 3 and e >= 1:
                        hd_low(e - 1)
                    if i + 3 < ITEM_CH:
                        dve_split_item(dve, it, i + 3)
                    if i == 0:
                        dve.wait_ge(y_hi_ready, it + 1)
                        dve.tensor_tensor(y_lo[:], ps[:, 2:4, :].rearrange("p a n -> p (a n)"), y_hi[:].bitcast(F32),
                                          ALU.subtract).then_inc(y_ready, 1)
                    if COMBINE0 < i <= COMBINE0 + KT:
                        add_back(i - COMBINE0 - 1, 5 + (i - COMBINE0 - 1) % 2, combined, it * KT + i - COMBINE0, added)
                    if what == "up" and part == 1 and e == EPG - 2:
                        dve.wait_ge(sel_turned, it + 1)
                        select(it + 1)
                    if what == "down" and part == 0 and e == EPG - 2:
                        hid_e(EPG - 1)
                    if what == "down" and part == 1 and e == EPG - 2:
                        hg_low(it + 1)
                        hd_low(EPG - 1)

            rounds(dve, item)
            dve.wait_ge(y_hi_last, 1)
            dve.tensor_tensor(y_lo[:], ps[:, 2:4, :].rearrange("p a n -> p (a n)"), y_hi[:].bitcast(F32), ALU.subtract)\
                .then_inc(y_lo_last, 1)
            for k in range(KT):
                add_back(k, (4, 7)[k % 2], combined_last, k + 1, x2_ready)
            dve.wait_ge(fg_in, 16)
            out_banks = (0, 2, 5)
            for t in range(NT):
                dve.wait_ge(out_std, t + 1)
                link(dve.reciprocal(fin[:, 3 + t:4 + t], fin[:, 3 + t:4 + t]))
                if t >= 2:
                    dve.wait_ge(store_y[t - 2], 16)
                dve.scalar_tensor_tensor(out=out_t[:, t % 2, :],
                                         in0=ps[:, out_banks[t]:out_banks[t] + 2, :].rearrange("p a n -> p (a n)"),
                                         scalar=fin[:, 3 + t:4 + t], in1=fg_b[:], op0=ALU.mult, op1=ALU.mult)\
                    .then_inc(out_ready, 1)

        @block.tensor
        def _(pe):
            def three(out, a_hi, a_lo, b_hi, b_lo, start, stop):
                pe.matmul(out, a_hi, b_hi, start=start, stop=False)
                pe.matmul(out, a_hi, b_lo, start=False, stop=False)
                return pe.matmul(out, a_lo, b_hi, start=False, stop=stop)

            def column_chunk(i, bank, x_hi, x_lo, k0=0, kn=KT, x0=0, first=True):
                b = i % SPLIT
                for k in range(k0, k0 + kn):
                    w = slice(P * k, P * k + P)
                    ins = three(ps[:, bank, 0:N], w_hi[:, b, w], w_lo[:, b, w], x_hi[:, x0 + k - k0, :], x_lo[:, x0 + k - k0, :],
                                k == k0, k == k0 + kn - 1)
                return ins

            def token_chunk(i):
                b, half = i % SPLIT, i % 2
                for k in range(4):
                    w = slice(256 * k, 256 * k + 256)
                    for t in range(NT):
                        x = slice(P * t, P * t + P)
                        ins = three(ps[:, t, 0:256], h_hi[:, 4 * half + k, x], h_lo[:, 4 * half + k, x],
                                    w_hi[:, b, w], w_lo[:, b, w], half == 0 and k == 0, half == 1 and k == 3)
                return ins

            def mod_slot(j):
                bank, c0 = mod_bank(j), first_chunk("mod", j)
                if j >= 2:
                    pe.wait_ge(modrow_ready, j - 1)
                for half in range(2):
                    i = c0 + half
                    pe.wait_ge(lo_ready, i + 1)
                    for k in range(4):
                        w = slice(256 * k, 256 * k + 256)
                        pe.matmul(ps[0:4, bank, 0:256], cond4[:, 4 * half + k, :], w_hi[:, i % SPLIT, w],
                                  start=half == 0 and k == 0, stop=False)
                        ins = pe.matmul(ps[0:4, bank, 0:256], cond4[:, 4 * half + k, :], w_lo[:, i % SPLIT, w],
                                        start=False, stop=half == 1 and k == 3)
                    ins.then_inc(chunk_done, 1)

            def mod_turn(j):
                pe.wait_ge(modrow_ready, j + 1)
                bank = 7 if j in MOD_LAST else 2
                for t in range(2):
                    at = 4 * (2 * j + t)
                    ins = pe.transpose(ps[:, bank, at:at + 4], modrow[:, j % 2, P * t:P * t + P], ident[0:4, 0:4])
                ins.then_inc(mod_turned, 1)

            def ssq(n, bank):
                pe.wait_ge(sq_ready, n + 1)
                pe.matmul(ps[:, bank, 0:N], ones[:], sq[:, n % 2, :], start=n % KT == 0, stop=n % KT == KT - 1)\
                    .then_inc(ssq_step, 1)

            pe.wait_ge(consts_ready, 5)
            pe.wait_ge(rows_in, 16 * 8)
            pe.transpose(ps[:, 3, 0:V_ROWS], vec_rows[:], ident[0:V_ROWS, 0:V_ROWS]).then_inc(vec_turned, 1)
            pe.wait_ge(taps_in, 32)
            pe.transpose(ps[:, 2, 0:2 * CK], tap_rows[:], ident[0:2 * CK, 0:2 * CK]).then_inc(vec_turned, 1)
            pe.wait_ge(x_in, 16 * NT)
            for k in range(KT + 1):
                if k < KT:
                    if k >= 3:
                        pe.wait_ge(x_ready, k - 2)
                    for t in range(NT):
                        ins = pe.transpose(ps[:, 4 + k % 3, P * t:P * t + P], x_tok[:, t, P * k:P * k + P], ident[:])
                    ins.then_inc(x_turned, 1)
                if k >= 1:
                    ssq(k - 1, 7)
            pe.wait_ge(ck_in, 16)
            pe.wait_ge(cond_ready, 1)
            for j in range(8):
                mod_slot(j)
                if j:
                    mod_turn(j - 1)
            for pair in range(PAIRS):
                ins = pe.transpose(ps[:, 5, P * pair:P * pair + P], ck_tok[:, 2 * pair:2 * pair + 2, :]
                                   .rearrange("p a d -> p (a d)"), ident[:])
            ins.then_inc(ck_turned, 1)
            mod_turn(7)
            c_q = first_chunk("q")
            for n in range(8):
                i = c_q + n
                if n == 0:
                    pe.wait_ge(modrow_ready, 8)
                if n >= 2:
                    pe.wait_ge(q_ready if n < 6 else k_ready, n - 1 if n < 6 else n - 5)
                pe.wait_ge(lo_ready, i + 1)
                for k in range(KT):
                    if n == 0:
                        pe.wait_ge(h_ready, k + 1)
                    w = slice(P * k, P * k + P)
                    ins = three(ps[:, n % 2, 0:N], w_hi[:, i % SPLIT, w], w_lo[:, i % SPLIT, w], h_hi[:, k, :], h_lo[:, k, :],
                                k == 0, k == KT - 1)
                ins.then_inc(chunk_done, 1)
            pe.wait_ge(k_ready, 4)
            for pair in range(PAIRS):
                ins = pe.transpose(ps[:, 6, P * pair:P * pair + P], kT[:, pair, 0:NCTX], ident[:])
            ins.then_inc(kctx_turned, 1)

            def score_unit(u):
                h, part = u // 3, u % 3
                rows, pair = slice(HD * (h % 2), HD * (h % 2) + HD), h // 2
                bank = 3 + u % 2
                if u >= 2:
                    pe.wait_ge(exps, u - 1)
                if part == 0:
                    pe.matmul(ps[:, bank, 0:NCTX], qT[rows, pair, 0:NCTX], kT[rows, pair, 0:NCTX], start=True, stop=True)\
                        .then_inc(scores, 1)
                    return
                q = qT[rows, pair, P * part:P * part + P]
                pe.matmul(ps[:, bank, 0:NLAT], q, kT[rows, pair, NCTX:N], start=True, stop=True)
                pe.matmul(ps[:, bank, NLAT:N], q, ckT[rows, pair, :], start=True, stop=True).then_inc(scores, 1)

            def turn_unit(u):
                h, part = u // 3, u % 3
                pe.wait_ge(probs_ready, u + 1)
                if u >= 2:
                    pe.wait_ge(turned_out, u - 1)
                for a in range(1 if part == 0 else 3):
                    ins = pe.transpose(ps[:, 5 + u % 2, P * a:P * a + P], probs[:, u % 3, P * a:P * a + P], ident[:])
                ins.then_inc(turned, 1)
                if part < 2:
                    return
                pair, out = h // 2, slice(HD * (h % 2), HD * (h % 2) + HD)
                cols = slice(HD * h, HD * h + HD)
                if h == 0:
                    pe.wait_ge(v_ready, 2)
                    pe.wait_ge(cv_in, 16)
                if h % 2 == 0 and pair:
                    pe.wait_ge(at_ready, pair)
                pe.wait_ge(turned_out, u + 1)
                pe.matmul(ps[out, 7, 0:NCTX], v_tok[:, 0, cols], ptc[:], start=True, stop=True)
                for a in range(3):
                    v = v_tok[:, 1 + a, cols] if a < 2 else cv_tok[:, h, :]
                    ins = pe.matmul(ps[out, 7, NCTX:N], v, ptl[:, a, :, :].rearrange("p t q -> p (t q)"),
                                    start=a == 0, stop=a == 2)
                ins.then_inc(pv_done, 1)

            for what, n in WINDOW:
                if what == "chunk":
                    kind, j = SLOTS[n // 2]
                    pe.wait_ge(lo_ready, n + 1)
                    if kind in ("uf", "v"):
                        if kind == "uf" and n % 2 == 0:
                            pe.wait_ge(k_ready, 4)
                        if kind == "v" and n % 2 == 0:
                            pe.wait_ge(fn_ready, 2) if j == 0 else pe.wait_ge(v_ready, j)
                        token_chunk(n).then_inc(chunk_done, 1)
                    else:
                        if j == 1:
                            pe.wait_ge(ck_ready, 1)
                            pe.wait_ge(kout_ready, 1)
                        column_chunk(n, 3 + 2 * j + n % 2, h_hi, h_lo).then_inc(chunk_done, 1)
                elif what == "mod":
                    if n == MOD_WINDOW[0]:
                        pe.wait_ge(v_ready, 2)
                        pe.wait_ge(mod_copied, 1)
                    mod_slot(n)
                    if n > MOD_WINDOW[0]:
                        mod_turn(n - 1)
                elif what == "fpos":
                    if n == 0:
                        pe.wait_ge(u_ready, 1)
                        pe.wait_ge(dft_in, 16 * 4)
                    else:
                        pe.wait_ge(z_ready, 1)
                    f = slice(P * n, P * n + P)
                    pe.matmul(ps[:, 0, 0:2 * NCTX], u_tok[:, 0, f], ctx_w[:], start=True, stop=True).then_inc(fnet_pos, 1)
                    for a in range(2):
                        ins = pe.matmul(ps[:, 1, 0:2 * NLAT], u_tok[:, 1 + a, f], lat_w[:, a, :], start=a == 0, stop=a == 1)
                    ins.then_inc(fnet_pos, 1)
                elif what == "ffeat":
                    pe.wait_ge(z_ready, n + 1)
                    if n == 1:
                        pe.wait_ge(fn_ready, 1)
                    for a in range(2):
                        ins = pe.matmul(ps[:, 2, 0:N], feat_w[:, a, :], z_cs[:, a, :], start=a == 0, stop=a == 1)
                    ins.then_inc(fnet_feat, 1)
                elif what == "unit" and n < UNITS:
                    if n == 0:
                        pe.wait_ge(z_conv, 2)
                    score_unit(n)
                elif what == "turn" and n >= 0:
                    turn_unit(n)
            mod_turn(MOD_WINDOW[-1])
            pe.wait_ge(conv_done, 2)
            pe.wait_ge(z_conv, 2)
            for a in range(2):
                ins = pe.matmul(ps[:, 0, 0:CO], ones[:], acc[:, a, :], start=a == 0, stop=a == 1)
            ins.then_inc(ln_mean, 1)
            pe.wait_ge(ln_sq, 1)
            for a in range(2):
                ins = pe.matmul(ps[:, 1, 0:CO], ones[:], csq[:, a, :], start=a == 0, stop=a == 1)
            ins.then_inc(ln_var, 1)

            for kind, j in UG:
                c0 = first_chunk(kind, j)
                if kind == "mod":
                    mod_slot(j)
                    if j > MOD_LAST[0]:
                        mod_turn(j - 1)
                    if j == MOD_LAST[-1]:
                        mod_turn(j)
                    continue
                for b, i in ((1, c0), (2, c0 + 1)) if kind == "g12" else ((0, c0),):
                    pe.wait_ge(lo_ready, i + 1)
                    g = 3 * j + (b + 2) % 3
                    if g >= 2:
                        pe.wait_ge(gate_tanh, g - 1)
                    column_chunk(i, gate_bank(j, b), h_hi, h_lo).then_inc(chunk_done, 1)
                if kind == "g0b":
                    pe.wait_ge(lo_ready, c0 + 2)
                    if j == 0:
                        pe.wait_ge(at_ready, PAIRS)
                        pe.wait_ge(cv_ready, 2)
                        pe.wait_ge(mod_copied, 2)
                    else:
                        pe.wait_ge(merged, j)
                    column_chunk(c0 + 1, 0, at_hi, at_lo, 0, 4)
                    column_chunk(c0 + 1, 1, fn_hi, fn_lo, 4, 2)
                    column_chunk(c0 + 1, 2, cv_hi, cv_lo, 6, 2).then_inc(chunk_done, 1)
            for n in range(KT + 1):
                if n < KT:
                    pe.wait_ge(lo_ready, 2 * WO0 + n + 1)
                    if n == 0:
                        pe.wait_ge(mg_ready, KT)
                    if n >= 2:
                        pe.wait_ge(x1_ready, n - 1)
                    column_chunk(2 * WO0 + n, n % 2, mg_hi, mg_lo).then_inc(chunk_done, 1)
                if n >= 1:
                    ssq(KT + n - 1, 2)
            pe.wait_ge(gr_in, 64)
            tok_banks = (0, 4, 6)
            for k in range(KT):
                pe.wait_ge(h2_ready, k + 1)
                ins = pe.matmul(ps[0:GROUPS + NE, 3, 0:N], w_gr[:, k, :], h2T[:, k, :], start=k == 0, stop=k == KT - 1)
            ins.then_inc(logits, 1)
            for t in range(NT):
                for k in range(KT):
                    ins = pe.transpose(ps[:, tok_banks[t] + k // 4, P * (k % 4):P * (k % 4) + P],
                                       h2T[:, k, P * t:P * t + P], ident[:])
                ins.then_inc(h2_turned, 1)
                if t == 0:
                    pe.wait_ge(logits_out, 1)
                    for q in range(NT):
                        ins = pe.transpose(ps[:, 2, 36 * q:36 * q + 36], lgT[:, P * q:P * q + P], ident[0:36, 0:36])
                    ins.then_inc(logits_turned, 1)
            pe.wait_ge(group_hot, 1)
            hot = og[:].rearrange("p t g -> p (t g)")
            pe.matmul(ps[:, 3, 0:12], tri[:], hot, start=True, stop=True)
            pe.matmul(ps[:, 3, 16:28], ones[:], hot, start=True, stop=True).then_inc(ranks, 1)

            def gather(nx):
                pe.wait_ge(sel_ready, NT * nx + NT)
                for t in range(NT):
                    pe.matmul(ps[:, 7, 0:EPG], sel[:, t, :].bitcast(F32), comb[:, t, :], start=t == 0, stop=t == NT - 1)
                for half in range(2):
                    d = slice(512 * half, 512 * half + 512)
                    for t in range(NT):
                        pe.matmul(ps[:, 5 + half, :], sel[:, t, :], ht_hi[:, t, d], start=t == 0, stop=False)
                        ins = pe.matmul(ps[:, 5 + half, :], sel[:, t, :], ht_lo[:, t, d], start=False, stop=t == NT - 1)
                ins.then_inc(gathered, 1)

            def hg_turn(nx):
                pe.wait_ge(hg_out, nx + 1)
                for k in range(KT):
                    ins = pe.transpose(ps[:, 5 + k // 4, P * (k % 4):P * (k % 4) + P], hg32[:, P * k:P * k + P], ident[:])
                ins.then_inc(hg_turned, 1)

            pe.wait_ge(ht_ready, NT)
            gather(0)
            hg_turn(0)

            def put_back(k, bank):
                d = slice(P * k, P * k + P)
                pe.matmul(ps[:, bank, 0:N], y_hi[:, d], selT[:], start=True, stop=False)
                return pe.matmul(ps[:, bank, 0:N], y_lo[:, d], selT[:], start=False, stop=True)

            def item(it, g):
                def hid_turn(e):
                    n = it * EPG + e
                    pe.wait_ge(hid_ready, n + 1)
                    for a in range(2):
                        ins = pe.transpose(ps[:, 4, P * a:P * a + P], hid[:, e % 2, P * a:P * a + P], ident[:])
                    ins.then_inc(hid_turned, 1)

                for what, e, part, i in order:
                    b = (PRE_CH + i) % SPLIT
                    pe.wait_ge(lo_ready, it * ITEM_CH + PRE_CH + i + 1)
                    if what == "up":
                        if part == 0 and e == 0:
                            pe.wait_ge(hg_ready, it + 1)
                        if part == 0 and e >= 2:
                            pe.wait_ge(hid_ready, it * EPG + e - 1)
                        if part == 0 and e == EPG - 1:
                            gather(it + 1)
                        for k in range(2):
                            w, kk = slice(512 * k, 512 * k + 512), 2 * part + k
                            ins = three(ps[:, e % 2, :], hg_hi[:, kk, :], hg_lo[:, kk, :], w_hi[:, b, w], w_lo[:, b, w],
                                        kk == 0, kk == KT - 1)
                        ins.then_inc(chunk_done, 1)
                        if part == 1 and e >= 2:
                            hid_turn(e - 1)
                        if part == 2 and e == 1:
                            hid_turn(0)
                        if part == 2 and e == SEL_TURN:
                            pe.wait_ge(cmb_ready, it + 1)
                            for t in range(NT):
                                ins = pe.transpose(ps[:, 7, P * (t + 1):P * (t + 1) + P], sel[:, t, :].bitcast(F32), ident[:])
                            ins.then_inc(sel_turned, 1)
                    else:
                        if part == 0 and e == 0:
                            pe.wait_ge(y_ready, it + 1)
                        if part == 0 and e == EPG - 1:
                            hg_turn(it + 1)
                            hid_turn(e)
                        if part == 0:
                            pe.wait_ge(hd_ready, it * EPG + e + 1)
                        for half in range(2):
                            w = slice(512 * half, 512 * half + 512)
                            ins = three(ps[:, 2 + half, :], hd_hi[:, part, :], hd_lo[:, part, :], w_hi[:, b, w], w_lo[:, b, w],
                                        e == 0 and part == 0, e == EPG - 1 and part == 1)
                        ins.then_inc(chunk_done, 1)
                    k = i - COMBINE0
                    if 0 <= k < KT:
                        if k == 0:
                            pe.wait_ge(y_ready, it + 1)
                            pe.wait_ge(selT_ready, it + 1)
                        if k >= 2:
                            pe.wait_ge(added, it * 2 * KT + 2 * (k - 1))
                        put_back(k, 5 + k % 2).then_inc(combined, 1)

            rounds(pe, item)
            pe.transpose(ps[:, 4, 0:P], ident[:], ident[:]).then_inc(y_last, 1)
            pe.wait_ge(y_lo_last, 1)
            out_banks = (0, 2, 5)
            for k in range(KT + 1):
                if k < KT:
                    if k >= 2:
                        pe.wait_ge(x2_ready, 2 * (k - 1))
                    put_back(k, (4, 7)[k % 2]).then_inc(combined_last, 1)
                if k >= 1:
                    pe.wait_ge(x2_ready, 2 * k)
                    for t in range(NT):
                        ins = pe.transpose(ps[:, out_banks[t] + (k - 1) // 4, P * ((k - 1) % 4):P * ((k - 1) % 4) + P],
                                           xT[:, k - 1, P * t:P * t + P], ident[:])
                        if k == KT:
                            ins.then_inc(out_turned, 1)


_INS = ['x_prompt', 'x_sample', 'cache_k', 'cache_v', 'c', 'c_ctx', 'w_mod', 'b_mod', 'norm1_g', 'w_in', 'rpb',
        'w_attn_o', 'w_fnet', 'conv_dw', 'conv_b', 'conv_ln_g', 'conv_ln_b', 'w_conv_o', 'w_out', 'norm2_g',
        'w_group', 'b_group', 'w_router', 'b_router', 'w1', 'w3', 'w2', 'final_g']
_OUTS = [("y_prompt", (1, NCTX, D)), ("y_sample", (1, NLAT, D)), ("new_k", (1, 1, HEADS, NCTX, HD)),
         ("new_v", (1, 1, HEADS, NCTX, HD))]


def _dft(n, norm):
    import numpy as np
    a = 2.0 * np.pi * ((np.arange(n)[:, None] * np.arange(n)[None, :]) % n) / n
    return np.concatenate([np.cos(a) * norm, np.sin(a) * norm], axis=1)


def _constants():
    import numpy as np
    f = _dft(FG, 1.0)
    feat = np.zeros((P, 2 * P))
    for g in range(P // FG):
        rows = slice(FG * g, FG * g + FG)
        feat[rows, FG * g:FG * g + FG] = f[:, 0:FG]
        feat[rows, P + FG * g:P + FG * g + FG] = -f[:, FG:]
    return {"dft_lat": _dft(NLAT, (NLAT * FG) ** -0.5).astype(np.float32),
            "dft_ctx": _dft(NCTX, (NCTX * FG) ** -0.5).astype(np.float32), "dft_feat": feat.astype(np.float32)}


def _lay_out(inputs):
    import numpy as np
    arrays = {name: np.ascontiguousarray(a) for name, a in inputs.items()}
    arrays["rpb"] = np.tile(arrays["rpb"], (1, 1, 1, GRID_W))
    arrays.update(_constants())
    return arrays


def kernel(**inputs):
    import concourse.bacc as bacc
    from concourse.bass_utils import run_bass_kernel_spmd

    nc = bacc.Bacc("TRN2", target_bir_lowering=False, num_devices=1)
    arrays = _lay_out({name: inputs[name] for name in _INS})
    args = {}
    for name, a in arrays.items():
        args[name] = nc.dram_tensor(name, a.shape, mybir.dt.from_np(a.dtype), kind="ExternalInput").ap()
    for name, shape in _OUTS:
        args[name] = nc.dram_tensor(name, shape, F32, kind="ExternalOutput").ap()
    build(nc, **args)
    r = run_bass_kernel_spmd(nc, [arrays], core_ids=[0])
    return tuple(r.results[0][name] for name, _ in _OUTS)
```

```python
from contextlib import ExitStack

import concourse.bass as bass
from concourse import mybir

F32 = mybir.dt.float32
F32R = mybir.dt.float32r
I32 = mybir.dt.int32
ALU = mybir.AluOpType
ACT = mybir.ActivationFunctionType
AX = mybir.AxisListType.X

P = 128
D = 1024
KT = D // P
NCTX, NLAT = 128, 256
N = NCTX + NLAT
NT = N // P
SEG = ((0, NCTX, 0), (NCTX, N, 1))
HEADS, HD = 8, 64
PAIRS = HEADS // 2
GRID_W, GRID_H = 64, 4
NDR = 6
RPB_R, RPB_C = 15, 31
FW, FG = 256, 64
CW, CK = 256, 31
PAD = CK // 2
ZW = PAD + NCTX + PAD + NLAT + PAD
CO = ZW - 2 * PAD
LAT0 = NCTX + PAD
COL_Q, COL_K, COL_V = 0, 512, 1024
COL_F = 1536
COL_C = COL_F + FW
COL_G = COL_C + 2 * CW
GROUPS, EPG, EH = 4, 8, 256
NE = GROUPS * EPG
ROUNDS = (N + P - 1) // P
EPS = 1e-6
NEG = -1e30

RING = 6
SLOT = 2048
CH = SLOT // 2
SPLIT = 4

V_CTX, V_C, V_N1, V_N2, V_BM, V_CB, V_LG, V_LB = 0, 8, 16, 24, 32, 80, 82, 84
V_ROWS = 86
SMALL = ("c_ctx", "c", "norm1_g", "norm2_g", "b_mod", "conv_b", "conv_ln_g", "conv_ln_b")

SLOTS = ([("mod", j) for j in range(8)] + [("q", j) for j in range(2)] + [("k", j) for j in range(2)]
         + [("uf", 0), ("uc", 0), ("uc", 1), ("v", 0), ("v", 1)])
BIAS_AT = SLOTS.index(("k", 0))
MOD_WINDOW = range(8, 21)
SLOTS += [("mod", j) for j in MOD_WINDOW]
MOD_LAST = range(MOD_WINDOW[-1] + 1, 24)
UG = []
for _d in range(KT):
    UG += [("g12", _d), ("g0b", _d)]
UG0 = len(SLOTS)
SLOTS += UG
WO0 = len(SLOTS)
SLOTS += [("wo", j) for j in range(4)] + [("mod", j) for j in MOD_LAST]
PRE = len(SLOTS)
PRE_CH = 2 * PRE
BY_COLUMNS = ("q", "k", "uc", "wo")

ITEM = [("A", 0), ("B", 0)]
for _e in range(1, EPG):
    ITEM += [("A", _e), ("B", _e), ("C", _e - 1)]
ITEM += [("C", EPG - 1)]
ITEM_CH = 2 * len(ITEM)
assert len(ITEM) % RING == 0 and ITEM_CH % SPLIT == 0

COMBINE0 = 4
POOL_PHASE = 3
H2_BY_POOL = (1, 4, 6)
H_BY_DVE = (0, 2, 4)
MOD_UNITS = (3, 4, 5, 5, 6, 8, 9, 10, 11, 12, 14, 15, 17, 17, 18, 18, 18, 19, 19, 19, 20, 21, 21, 22, 23, 25)
LN_UNIT = 15
TAPS_PER_UNIT = 5
SEL_TURN = 4

UNITS = 3 * HEADS


def first_chunk(kind, j=0):
    return 2 * SLOTS.index((kind, j))


POOL_ITEM = [i % 6 == POOL_PHASE for i in range(ITEM_CH)]
POOL_PRE = [SLOTS[i // 2][0] == "v" or SLOTS[i // 2] in [("mod", j) for j in MOD_WINDOW]
            for i in range(PRE_CH)]
POOL_PRE[-2 * RING:] = POOL_ITEM[-2 * RING:]


def cut_count(i):
    by = POOL_PRE[i]
    return by, sum(b == by for b in POOL_PRE[:i + 1])


def cut_count_item(i):
    if i < 0:
        return cut_count(PRE_CH + i)
    by = POOL_ITEM[i]
    return by, sum(b == by for b in POOL_PRE) + sum(b == by for b in POOL_ITEM[:i + 1])


_uf, _uc, _v = first_chunk("uf"), first_chunk("uc"), first_chunk("v")
WINDOW = [("chunk", _uf), ("chunk", _uf + 1), ("chunk", _uc), ("fpos", 0), ("chunk", _uc + 1), ("ffeat", 0),
          ("fpos", 1), ("chunk", _uc + 2), ("ffeat", 1), ("chunk", _uc + 3), ("glu", 0), ("chunk", _v), ("glu", 1)]
_fill = {0: [("chunk", _v + 1)], 1: [("chunk", _v + 2)], 2: [("chunk", _v + 3)]}
for _i, _u in enumerate(MOD_UNITS):
    _fill.setdefault(_u, []).append(("mod", first_chunk("mod", MOD_WINDOW[0]) + _i))
for _i in range(9):
    _fill[LN_UNIT + _i] = _fill.get(LN_UNIT + _i, []) + [("ln", _i)]
for _u in range(UNITS + 3):
    WINDOW += [("unit", _u), ("pv", _u - 3)] + _fill.get(_u, []) + [("turn", _u - 2)]


def build(nc, x_prompt, x_sample, cache_k, cache_v, small_rows, w_mod, w_in, rpb, w_attn_o, w_fnet, conv_dw,
          w_conv_o, w_out, w_group, b_group, w_router, b_router, w1, w3, w2, final_g, dft_lat, dft_ctx, dft_feat,
          y_prompt, y_sample, new_k, new_v):
    ctx = ExitStack()
    with ctx:
        base = (nc.sbuf_base + 31) // 32 * 32
        top = nc.sbuf_usable_end

        class Region:

            def __init__(self, start, size=None):
                self.start, self.at, self.end = start, start, start + size if size else top

            def tile(self, name, shape, dt=F32):
                size = 4
                for s in shape[1:]:
                    size *= s
                t = nc.alloc_sbuf_tensor_at(name, shape, dt, offset=self.at)
                self.at += (size + 31) // 32 * 32
                assert self.at <= self.end, (name, self.at, self.end)
                return t

        R = Region(base)
        raw = R.tile("raw", [P, RING, SLOT])
        w_hi = R.tile("w_hi", [P, SPLIT, CH], F32R)
        w_lo = R.tile("w_lo", [P, SPLIT, CH], F32R)
        xT = R.tile("xT", [P, KT, N])
        ident = R.tile("ident", [P, P])
        ones = R.tile("ones", [P, P])
        tri = R.tile("tri", [P, P])
        iota_s = R.tile("iota_s", [P, P])
        vec_t = R.tile("vec_t", [P, V_ROWS])
        taps = R.tile("taps", [P, 2, CK])
        cond = R.tile("cond", [P, 2, KT])
        cond_t = R.tile("cond_t", [P, 2, KT])
        cond4 = R.tile("cond4", [P, KT, 4], F32R)
        modT = R.tile("modT", [P, 48, 2])
        scale1 = R.tile("scale1", [P, KT, 2])
        scale2 = R.tile("scale2", [P, KT, 2])
        eps_t = R.tile("eps_t", [P, 1])
        rstd = R.tile("rstd", [P, N])
        sq = R.tile("sq", [P, 2, N])
        modrow = R.tile("modrow", [4, 2, 256])
        w_gr = R.tile("w_gr", [P, KT, GROUPS + NE])
        b_gr = R.tile("b_gr", [P, GROUPS + NE])
        mod_tmp = R.tile("mod_tmp", [P, 32, 4])
        stats = R.tile("stats", [P, 3, 8])
        rt = R.tile("rt", [P, 3, 64])
        start_h = R.at
        Rh = Region(start_h, 2 * 4 * KT * N)
        h_hi = Rh.tile("h_hi", [P, KT, N], F32R)
        h_lo = Rh.tile("h_lo", [P, KT, N], F32R)
        start_b = Rh.at
        Rb = Region(start_b, 4 * 16 * N)
        at_hi = Rb.tile("at_hi", [P, PAIRS, N], F32R)
        at_lo = Rb.tile("at_lo", [P, PAIRS, N], F32R)
        fn_hi = Rb.tile("fn_hi", [P, 2, N], F32R)
        fn_lo = Rb.tile("fn_lo", [P, 2, N], F32R)
        start_cv = Rb.at
        cv_hi = Rb.tile("cv_hi", [P, 2, N], F32R)
        cv_lo = Rb.tile("cv_lo", [P, 2, N], F32R)
        k_out = Region(start_cv, 4 * 4 * N).tile("k_out", [P, HEADS * HD])
        start_x = Rb.at
        Rx = Region(start_x)
        qT = Rx.tile("qT", [P, PAIRS, N])
        kT = Rx.tile("kT", [P, PAIRS, N])
        v_tok = Rx.tile("v_tok", [P, NT, HEADS * HD])
        ckT = Rx.tile("ckT", [P, PAIRS, P])
        cv_tok = Rx.tile("cv_tok", [P, HEADS, HD])
        bias = Rx.tile("bias", [P, HEADS, NDR, GRID_W])
        probs = Rx.tile("probs", [P, 3, N])
        ptl = Rx.tile("ptl", [P, 3, 2, P])
        ptc = Rx.tile("ptc", [P, P])
        start_y = Rx.at
        h32 = Region(start_x, 4 * KT * N).tile("h32", [P, KT, N])
        ck_tok = Region(start_x + 4 * KT * N, 2048 * 3).tile("ck_tok", [P, HEADS, HD])
        Rs = Region(start_y)
        x_tok = Rs.tile("x_tok", [P, NT, D])
        Rs2 = Region(start_b)
        vec_rows = Rs2.tile("vec_rows", [V_ROWS, P])
        tap_rows = Rs2.tile("tap_rows", [2 * CK, P])
        Ry = Region(start_y)
        u_tok = Ry.tile("u_tok", [P, NT, FW])
        lat_w = Ry.tile("lat_w", [P, 2, 2 * NLAT])
        ctx_w = Ry.tile("ctx_w", [P, 2 * NCTX])
        feat_w = Ry.tile("feat_w", [P, 2, P])
        z_cs = Ry.tile("z_cs", [P, 2, N])
        Rc = Region(start_y)
        zpad = Rc.tile("zpad", [P, 2, ZW])
        acc = Rc.tile("acc", [P, 2, CO])
        csq = Rc.tile("csq", [P, 2, CO])
        crs = Rc.tile("crs", [P, CO])
        Rg = Region(start_x)
        mg_hi = Rg.tile("mg_hi", [P, KT, N], F32R)
        mg_lo = Rg.tile("mg_lo", [P, KT, N], F32R)
        th = Rg.tile("th", [P, 3, N])
        mg = Rg.tile("mg", [P, 2, N])
        mt = Rg.tile("mt", [P, 2, N])
        Rm = Region(start_h, 2 * 4 * KT * N)
        ht_hi = Rm.tile("ht_hi", [P, NT, D], F32R)
        ht_lo = Rm.tile("ht_lo", [P, NT, D], F32R)
        Rm = Region(start_b, 4 * 16 * N)
        sel = Rm.tile("sel", [P, NT, P], F32R)
        selT = Rm.tile("selT", [P, N], F32R)
        hg_hi = Rm.tile("hg_hi", [P, KT, P], F32R)
        hg_lo = Rm.tile("hg_lo", [P, KT, P], F32R)
        hd_hi = Rm.tile("hd_hi", [P, 2, P], F32R)
        hd_lo = Rm.tile("hd_lo", [P, 2, P], F32R)
        Rm = Region(start_x)
        y_hi = Rm.tile("y_hi", [P, D], F32R)
        y_lo = Rm.tile("y_lo", [P, D], F32R)
        hg32 = Rm.tile("hg32", [P, D])
        th_e = Rm.tile("th_e", [P, 2, EH])
        s_e = Rm.tile("s_e", [P, 2, EH])
        hid = Rm.tile("hid", [P, 2, EH])
        out_t = Rm.tile("out_t", [P, 2, D])
        junk = Rm.tile("junk", [P, D])
        fg_b = Rm.tile("fg_b", [P, D])
        Rm = Region(start_x + 6 * 4 * KT * N // 2)
        h2T = Rm.tile("h2T", [P, KT, N])
        lgT = Rm.tile("lgT", [GROUPS + NE, N])
        lg = Rm.tile("lg", [P, NT, GROUPS + NE])
        og = Rm.tile("og", [P, NT, GROUPS])
        pr = Rm.tile("pr", [P, NT, EPG, GROUPS])
        e_sel = Rm.tile("e_sel", [P, NT, EPG])
        o1 = Rm.tile("o1", [P, NT, EPG])
        o2 = Rm.tile("o2", [P, NT, EPG])
        comb = Rm.tile("comb", [P, NT, EPG])
        rk = Rm.tile("rk", [P, NT, GROUPS])
        key = Rm.tile("key", [P, NT])
        i_base = Rm.tile("i_base", [P, 16])
        keysh = Rm.tile("keysh", [P, 16, NT])
        goff = Rm.tile("goff", [P, GROUPS])
        tot = Rm.tile("tot", [P, NT, GROUPS])
        cmb = Rm.tile("cmb", [P, EPG])
        over = Rm.tile("over", [P, 1], I32)
        fin = Rm.tile("fin", [P, 8])

        out_tiles = [out_t[:, 0, :], out_t[:, 1, :], hg32[:]]
        ps = ctx.enter_context(nc.psum_tensor("ps", [P, 8, 512], F32))

        def sem(name):
            return ctx.enter_context(nc.semaphore(name))

        raw_ready = [sem(f"raw_ready{i}") for i in range(RING)]
        hi_ready, chunk_done = sem("hi_ready"), sem("chunk_done")
        lo_ready, lo_ready_pool = sem("lo_ready"), sem("lo_ready_pool")
        rows_in, taps_in, x_in, ck_in, cv_in, dft_in, bias_in, gr_in, fg_in = (
            sem(n) for n in ("rows_in", "taps_in", "x_in", "ck_in", "cv_in", "dft_in", "bias_in", "gr_in", "fg_in"))
        ident_step, consts_ready, mask_step = (
            sem(n) for n in ("ident_step", "consts_ready", "mask_step"))
        vec_turned, vec_ready, cond_tanh, cond_ready = (
            sem(n) for n in ("vec_turned", "vec_ready", "cond_tanh", "cond_ready"))
        x_turned, x_ready, sq_ready, ssq_step, std_ready, norm_ready = (
            sem(n) for n in ("x_turned", "x_ready", "sq_ready", "ssq_step", "std_ready", "norm_ready"))
        modrow_ready, mod_turned, mod_copied, mod_ready = (
            sem(n) for n in ("modrow_ready", "mod_turned", "mod_copied", "mod_ready"))
        h32_ready, h_hi_ready, h_ready = sem("h32_ready"), sem("h_hi_ready"), sem("h_ready")
        q_ready, k_ready, ck_turned, ck_ready, kctx_turned, kout_ready, store_k, store_v, u_ready, v_ready = (
            sem(n) for n in ("q_ready", "k_ready", "ck_turned", "ck_ready", "kctx_turned", "kout_ready", "store_k",
                             "store_v", "u_ready", "v_ready"))
        fnet_pos, z_ready, fnet_feat, fn_hi_ready, fn_ready = (
            sem(n) for n in ("fnet_pos", "z_ready", "fnet_feat", "fn_hi_ready", "fn_ready"))
        glu_tanh, zpad_zero, z_conv, conv_step, ln_mean, ln_centred, ln_sq, ln_var, ln_std, ln_out, ln_tanh = (
            sem(n) for n in ("glu_tanh", "zpad_zero", "z_conv", "conv_step", "ln_mean", "ln_centred", "ln_sq",
                             "ln_var", "ln_std", "ln_out", "ln_tanh"))
        silu_ready, cv_hi_ready, cv_ready = sem("silu_ready"), sem("cv_hi_ready"), sem("cv_ready")
        scores, negmax, exps, probs_ready, turned, turned_out, pv_done, at_hi_ready, at_ready = (
            sem(n) for n in ("scores", "negmax", "exps", "probs_ready", "turned", "turned_out", "pv_done",
                             "at_hi_ready", "at_ready"))
        gate_tanh, merged, mg_hi_ready, mg_ready, x1_ready, h2_ready = (
            sem(n) for n in ("gate_tanh", "merged", "mg_hi_ready", "mg_ready", "x1_ready", "h2_ready"))
        logits, logits_out, logits_turned, h2_turned, ht_hi_ready, ht_ready, grp_shift, grp_exp, exp_gap, exp2 = (
            sem(n) for n in ("logits", "logits_out", "logits_turned", "h2_turned", "ht_hi_ready", "ht_ready",
                             "grp_shift", "grp_exp", "exp_gap", "exp2"))
        group_hot, ranks, routed = sem("group_hot"), sem("ranks"), sem("routed")
        sel_ready, gathered, hg_out, hg_turned, hg_hi_ready, hg_ready, sel_turned, selT_ready, cmb_ready = (
            sem(n) for n in ("sel_ready", "gathered", "hg_out", "hg_turned", "hg_hi_ready", "hg_ready",
                             "sel_turned", "selT_ready", "cmb_ready"))
        rstd_ready, h_scaled, h32_ready_dve = sem("rstd_ready"), sem("h_scaled"), sem("h32_ready_dve")
        h2_ready_pool = sem("h2_ready_pool")
        h2_scaled, comb_ready, weighted = sem("h2_scaled"), sem("comb_ready"), sem("weighted")
        silu_e, x2_ready, y_zero, y_last, y_hi_last, y_lo_last, combined_last = (
            sem(n) for n in ("silu_e", "x2_ready", "y_zero", "y_last", "y_hi_last", "y_lo_last", "combined_last"))
        e_tanh, hid_ready, hid_turned, hd_hi_ready, hd_ready, y_hi_ready, y_ready, combined, added = (
            sem(n) for n in ("e_tanh", "hid_ready", "hid_turned", "hd_hi_ready", "hd_ready", "y_hi_ready",
                             "y_ready", "combined", "added"))
        out_turned, out_std, out_ready = sem("out_turned"), sem("out_std"), sem("out_ready")
        store_y = [sem(f"store_y{t}") for t in range(NT)]
        act_step, dve_step = sem("act_step"), sem("dve_step")

        w_mod_v = w_mod[0].rearrange("(k p) c -> p k c", p=P)
        w_in_v = w_in[0].rearrange("(k p) c -> p k c", p=P)
        w_out_v = w_out[0].rearrange("(k p) c -> p k c", p=P)
        w_at_v = w_attn_o[0].rearrange("(k p) c -> p k c", p=P)
        w_fn_v = w_fnet[0].rearrange("(k p) c -> p k c", p=P)
        w_cv_v = w_conv_o[0].rearrange("(k p) c -> p k c", p=P)
        w1_v = w1[0].rearrange("e (k p) f -> e p k f", p=P)
        w3_v = w3[0].rearrange("e (k p) f -> e p k f", p=P)
        w2_v = w2[0].rearrange("e (k p) d -> e p k d", p=P)

        def slot_loads(kind, j, r):
            full = raw[:, r, :].rearrange("p (k c) -> p k c", k=KT)
            halves = raw[:, r, :].rearrange("p (h k c) -> p h k c", h=2, k=KT)
            if kind == "mod":
                return [(full, w_mod_v[:, :, 256 * j:256 * j + 256])]
            if kind in ("q", "k", "v", "uf"):
                c0 = {"q": COL_Q, "k": COL_K, "v": COL_V, "uf": COL_F}[kind] + 256 * j
                return [(full, w_in_v[:, :, c0:c0 + 256])]
            if kind == "uc":
                return [(full[:, :, 128 * i:128 * i + 128], w_in_v[:, :, COL_C + CW * i + P * j:COL_C + CW * i + P * j + P])
                        for i in range(2)]
            cols = slice(P * j, P * j + P)
            gate = lambda b: w_in_v[:, :, COL_G + D * b + P * j:COL_G + D * b + P * j + P]
            if kind == "g0b":
                return [(halves[:, 0, :, :], gate(0)), (halves[:, 1, 0:4, :], w_at_v[:, :, cols]),
                        (halves[:, 1, 4:6, :], w_fn_v[:, :, cols]), (halves[:, 1, 6:8, :], w_cv_v[:, :, cols])]
            if kind == "g12":
                return [(halves[:, i, :, :], gate(1 + i)) for i in range(2)]
            return [(full, w_out_v[:, :, 256 * j:256 * j + 256])]

        def item_loads(kind, e, g, r):
            ex = bass.ds(g * EPG + e, 1)
            if kind == "C":
                return [(raw[:, r, :].rearrange("p (k c) -> p k c", k=2), w2_v[ex].rearrange("e p k d -> (e p) k d"))]
            full = raw[:, r, :].rearrange("p (k w c) -> p k w c", k=4, w=2)
            ks = slice(0, 4) if kind == "A" else slice(4, 8)
            return [(full[:, :, i, :], w[ex].rearrange("e p k f -> (e p) k f")[:, ks, :]) for i, w in enumerate((w1_v, w3_v))]

        N_LOADS = {"mod": 1, "q": 1, "k": 1, "v": 1, "uf": 1, "uc": 2, "g0b": 4, "g12": 2, "wo": 1, "A": 2, "B": 2, "C": 1}
        seen = [0] * RING
        pre_count = []
        for s, (kind, j) in enumerate(SLOTS):
            seen[s % RING] += 16 * N_LOADS[kind]
            pre_count.append(seen[s % RING])
        per_item = [0] * RING
        item_count = []
        for s, (kind, e) in enumerate(ITEM):
            r = (PRE + s) % RING
            per_item[r] += 16 * N_LOADS[kind]
            item_count.append(seen[r] + per_item[r])

        def raw_chunk(slot_kind, r, half):
            if slot_kind in BY_COLUMNS:
                return raw[:, r, :].rearrange("p (k c) -> p k c", k=KT)[:, :, P * half:P * half + P]
            return raw[:, r, CH * half:CH * half + CH]

        def cut_chunk(t, slot_kind, b):
            return t[:, b, :].rearrange("p (k c) -> p k c", k=KT) if slot_kind in BY_COLUMNS else t[:, b, :]

        def modulate_h(eng, k):
            for a, b, which in SEG:
                ins = eng.tensor_scalar(h32[:, k, a:b], h32[:, k, a:b], scale1[:, k, which:which + 1],
                                        modT[:, k, which:which + 1], ALU.mult, ALU.add)
            return ins

        def mod_bank(j):
            return 2 if j == MOD_LAST[-1] else 1 if j in MOD_WINDOW else j % 2

        def gate_bank(d, b):
            return 3 + (3 * d + (b + 2) % 3) % 2

        def act_split(act, i):
            kind, r = SLOTS[i // 2][0], (i // 2) % RING
            if i % 2 == 0:
                act.wait_ge(raw_ready[r], pre_count[i // 2])
            if i >= SPLIT:
                act.wait_ge(chunk_done, i - SPLIT + 1)
            act.activation(cut_chunk(w_hi, kind, i % SPLIT), raw_chunk(kind, r, i % 2), ACT.Copy).then_inc(hi_ready, 1)

        def wait_lo(eng, i):
            by_pool, n = cut_count(i)
            eng.wait_ge(lo_ready_pool if by_pool else lo_ready, n)

        def low_split(eng, i):
            kind, r = SLOTS[i // 2][0], (i // 2) % RING
            eng.wait_ge(hi_ready, i + 1)
            eng.tensor_tensor(cut_chunk(w_lo, kind, i % SPLIT), raw_chunk(kind, r, i % 2),
                              cut_chunk(w_hi, kind, i % SPLIT).bitcast(F32), ALU.subtract)\
                .then_inc(lo_ready_pool if POOL_PRE[i] else lo_ready, 1)

        def act_split_item(act, it, i):
            r, b = (PRE + i // 2) % RING, (PRE_CH + i) % SPLIT
            if i % 2 == 0:
                act.wait_ge(raw_ready[r], it * per_item[r] + item_count[i // 2])
            act.wait_ge(chunk_done, it * ITEM_CH + (PRE_CH + i - SPLIT + 1))
            act.activation(w_hi[:, b, :], raw[:, r, CH * (i % 2):CH * (i % 2) + CH], ACT.Copy).then_inc(hi_ready, 1)

        def wait_lo_item(eng, it, i):
            by_pool, n = cut_count_item(i)
            eng.wait_ge(lo_ready_pool if by_pool else lo_ready, it * sum(b == by_pool for b in POOL_ITEM) + n)

        def low_split_item(eng, it, i):
            r, b = (PRE + i // 2) % RING, (PRE_CH + i) % SPLIT
            eng.wait_ge(hi_ready, it * ITEM_CH + (PRE_CH + i + 1))
            eng.tensor_tensor(w_lo[:, b, :], raw[:, r, CH * (i % 2):CH * (i % 2) + CH], w_hi[:, b, :].bitcast(F32),
                              ALU.subtract).then_inc(lo_ready_pool if POOL_ITEM[i] else lo_ready, 1)

        def dve_split_item(dve, it, i):
            if not POOL_ITEM[i]:
                low_split_item(dve, it, i)

        up_chunks, down_chunks, order = {}, {}, []
        for s, (kind, e) in enumerate(ITEM):
            (down_chunks if kind == "C" else up_chunks).setdefault(e, []).extend([2 * s, 2 * s + 1])
        for s, (kind, e) in enumerate(ITEM):
            for half in range(2):
                order.append(("down" if kind == "C" else "up", e, (2 if kind == "B" else 0) + half, 2 * s + half))

        def rounds(eng, item):
            with eng.Fori(0, GROUPS) as g:
                item(g, g)
            eng.wait_ge(routed, 1)
            n_over = eng.value_load(over[0:1, 0:1])
            with eng.If(n_over > 0):
                with eng.Fori(1, ROUNDS) as r:
                    with eng.Fori(0, GROUPS) as g:
                        item(r * GROUPS + g, g)

        block = ctx.enter_context(nc.Block())

        @block.sync
        def _(sp):
            sp.dma_start(vec_rows[:], small_rows).then_inc(rows_in, 16)
            for i in range(2):
                sp.dma_start(tap_rows[CK * i:CK * i + CK, :], conv_dw[0, :, P * i:P * i + P]).then_inc(taps_in, 16)
            for t in range(NT):
                src = x_prompt[0] if t == 0 else x_sample[0, (t - 1) * P:t * P, :]
                sp.dma_start(x_tok[:, t, :], src).then_inc(x_in, 16)
            for s, (kind, j) in enumerate(SLOTS):
                if BIAS_AT <= s < BIAS_AT + HEADS:
                    h = s - BIAS_AT
                    for half in range(2):
                        at = (h * RPB_R + 5 - half) * RPB_C * GRID_W + 15
                        sp.dma_start(bias[64 * half:64 * half + 64, h, :, :],
                                     bass.AP(rpb.tensor, at, [[RPB_C - 1, 64], [RPB_C * GRID_W, NDR], [1, GRID_W]]))\
                            .then_inc(bias_in, 16)
                if s == UG0:
                    sp.dma_start(w_gr[:, :, 0:GROUPS], w_group[0].rearrange("(k p) g -> p k g", p=P)).then_inc(gr_in, 16)
                    sp.dma_start(w_gr[:, :, GROUPS:], w_router[0].rearrange("(k p) g -> p k g", p=P)).then_inc(gr_in, 16)
                    sp.dma_start(b_gr[:, 0:GROUPS], b_group.to_broadcast([P, GROUPS])).then_inc(gr_in, 16)
                    sp.dma_start(b_gr[:, GROUPS:], b_router.to_broadcast([P, NE])).then_inc(gr_in, 16)
                if s >= RING:
                    for half in range(2):
                        wait_lo(sp, 2 * (s - RING) + half)
                for dst, src in slot_loads(kind, j, s % RING):
                    sp.dma_start(dst, src).then_inc(raw_ready[s % RING], 16)

            def item(it, g):
                for s, (kind, e) in enumerate(ITEM):
                    last = 2 * (s - RING) + 1
                    if POOL_ITEM[last] or POOL_ITEM[last - 1]:
                        sp.wait_ge(chunk_done, it * ITEM_CH + (PRE_CH + last + 1))
                    else:
                        wait_lo_item(sp, it, last)
                    r = (PRE + s) % RING
                    for dst, src in item_loads(kind, e, g, r):
                        sp.dma_start(dst, src).then_inc(raw_ready[r], 16)

            rounds(sp, item)
            for t in range(NT):
                dst = y_prompt[0] if t == 0 else y_sample[0, (t - 1) * P:t * P, :]
                sp.wait_ge(out_ready, t + 1)
                sp.dma_start(dst, out_tiles[t]).then_inc(store_y[t], 16)
            for t in range(NT):
                sp.wait_ge(store_y[t], 16)
            sp.wait_ge(store_k, 16)
            sp.wait_ge(store_v, 16)

        @block.gpsimd
        def _(pool):
            pool.memset(ident[:], 0.0).then_inc(ident_step, 1)
            pool.memset(tri[:], 1.0).then_inc(ident_step, 1)
            pool.wait_ge(ident_step, 2)
            pool.affine_select(out=ident[:], in_=ident[:], compare_op=ALU.not_equal, fill=1.0, base=0,
                               pattern=[[-1, P]], channel_multiplier=1).then_inc(consts_ready, 1)
            pool.memset(ones[:], 1.0).then_inc(consts_ready, 1)
            pool.memset(eps_t[:], EPS).then_inc(consts_ready, 1)
            pool.affine_select(out=tri[:], in_=tri[:], compare_op=ALU.is_gt, fill=0.0, base=0,
                               pattern=[[1, P]], channel_multiplier=-1).then_inc(consts_ready, 1)
            pool.iota(iota_s[:], pattern=[[1, P]], base=0, channel_multiplier=0,
                      allow_small_or_imprecise_dtypes=True).then_inc(consts_ready, 1)
            pool.wait_ge(rstd_ready, 1)
            for k in range(KT):
                pool.tensor_tensor(h32[:, k, :], xT[:, k, :], rstd[:], ALU.mult).then_inc(h_scaled, 1)
            pool.wait_ge(h_scaled, KT)
            pool.wait_ge(mod_ready, 1)
            for k in range(KT):
                if k not in H_BY_DVE:
                    modulate_h(pool, k).then_inc(h32_ready, 1)
            pool.wait_ge(bias_in, 16 * 2 * HEADS)
            for half in range(2):
                b = bias[64 * half:64 * half + 64].rearrange("p h s c -> p (h s) c")
                lo, hi = b[:, :, 0:GRID_W - 16], b[:, :, 16:GRID_W]
                pool.affine_select(out=lo, in_=lo, compare_op=ALU.is_ge, fill=NEG, base=8,
                                   pattern=[[0, HEADS * NDR], [1, GRID_W - 16]], channel_multiplier=-1)\
                    .then_inc(mask_step, 1)
                pool.wait_ge(mask_step, 2 * half + 1)
                pool.affine_select(out=hi, in_=hi, compare_op=ALU.is_ge, fill=NEG, base=7 - 16,
                                   pattern=[[0, HEADS * NDR], [-1, GRID_W - 16]], channel_multiplier=1)\
                    .then_inc(mask_step, 1)
            pool.wait_ge(mask_step, 4)
            for i in range(PRE_CH):
                if POOL_PRE[i]:
                    low_split(pool, i)
            for k in H2_BY_POOL:
                pool.wait_ge(h2_scaled, k + 1)
                for a, b, which in SEG:
                    ins = pool.tensor_scalar(h2T[:, k, a:b], h2T[:, k, a:b], scale2[:, k, which:which + 1],
                                             modT[:, 24 + k, which:which + 1], ALU.mult, ALU.add)
                ins.then_inc(h2_ready_pool, 1)
            pool.wait_ge(mg_ready, KT)
            pool.iota(i_base[:], pattern=[[P, 4], [N, 4]], base=0, channel_multiplier=0,
                      allow_small_or_imprecise_dtypes=True).then_inc(consts_ready, 1)
            pool.iota(goff[:], pattern=[[N, GROUPS]], base=0, channel_multiplier=0,
                      allow_small_or_imprecise_dtypes=True).then_inc(consts_ready, 1)

            pool.memset(selT[:].bitcast(F32), 0.0).then_inc(selT_ready, 1)

            def item(it, g):
                for i in range(ITEM_CH):
                    if POOL_ITEM[i]:
                        low_split_item(pool, it, i)

            rounds(pool, item)

        @block.scalar
        def _(act):
            step = 0

            def link(ins):
                nonlocal step
                step += 1
                ins.then_inc(act_step, 1)
                act.wait_ge(act_step, step)

            split_at = 0

            def split_to(n):
                nonlocal split_at
                while split_at < min(n, PRE_CH):
                    act_split(act, split_at)
                    split_at += 1

            act.wait_ge(vec_ready, 1)
            act.activation(cond_t[:].rearrange("p a k -> p (a k)"), vec_t[:, V_CTX:V_CTX + 16], ACT.Tanh, scale=0.5)\
                .then_inc(cond_tanh, 1)

            def square(n, src):
                if n >= 2:
                    act.wait_ge(ssq_step, n - 1)
                act.activation(sq[:, n % 2, :], src, ACT.Square).then_inc(sq_ready, 1)

            def std(n, bank):
                act.wait_ge(ssq_step, KT * (n + 1))
                act.activation(rstd[:], ps[:, bank, 0:N], ACT.Sqrt, bias=eps_t[:, 0:1], scale=1.0 / D)\
                    .then_inc(std_ready, 1)

            act.wait_ge(consts_ready, 3)
            link(act.activation(stats[:, 0, 7:8], eps_t[:, 0:1], ACT.Sqrt))
            def mod_row(j):
                act.wait_ge(chunk_done, first_chunk("mod", j) + 2)
                if j >= 2:
                    act.wait_ge(mod_turned, j - 1)
                bank = mod_bank(j)
                act.activation(modrow[:, j % 2, :], ps[0:4, bank, 0:256], ACT.Copy).then_inc(modrow_ready, 1)

            for j in range(8):
                split_to(2 * j + 4)
                if j < KT // 2:
                    for k in (2 * j, 2 * j + 1):
                        act.wait_ge(x_ready, k + 1)
                        square(k, xT[:, k, :])
                mod_row(j)
                split_to(2 * j + 5)
                if j == KT // 2:
                    std(0, 7)
                    act.dma_start(ck_tok[:], cache_k[0, 0].rearrange("h n d -> n h d")).then_inc(ck_in, 16)
                    act.dma_start(cv_tok[:], cache_v[0, 0].rearrange("h n d -> n h d")).then_inc(cv_in, 16)
                    for a in range(2):
                        act.dma_start(lat_w[:, a, :], dft_lat[P * a:P * a + P, :]).then_inc(dft_in, 16)
                    act.dma_start(ctx_w[:], dft_ctx).then_inc(dft_in, 16)
                    act.dma_start(feat_w[:].rearrange("p a c -> p (a c)"), dft_feat).then_inc(dft_in, 16)
            for k in range(KT):
                if k in H_BY_DVE:
                    act.wait_ge(h32_ready_dve, H_BY_DVE.index(k) + 1)
                else:
                    act.wait_ge(h32_ready, sum(q not in H_BY_DVE for q in range(k + 1)))
                act.activation(h_hi[:, k, :], h32[:, k, :], ACT.Copy).then_inc(h_hi_ready, 1)
            c_q, c_k = first_chunk("q"), first_chunk("k")
            for n in range(4):
                split_to(c_q + n + 4)
                act.wait_ge(chunk_done, c_q + n + 1)
                if n == 0:
                    act.wait_ge(h_ready, KT)
                act.activation(qT[:, n, :], ps[:, n % 2, 0:N], ACT.Copy, scale=HD ** -0.5).then_inc(q_ready, 1)
            for n in range(4):
                split_to(c_k + n + 4)
            act.wait_ge(ck_turned, 1)
            act.activation(ckT[:].rearrange("p a n -> p (a n)"), ps[:, 5, :], ACT.Copy).then_inc(ck_ready, 1)
            act.wait_ge(kout_ready, 1)
            act.dma_start(new_k[0, 0].rearrange("h n d -> n h d"), k_out[:].rearrange("p (h d) -> p h d", h=HEADS))\
                .then_inc(store_k, 16)

            def exp_unit(u):
                b, part = u % 3, u % 3
                act.wait_ge(negmax, u + 1)
                if part == 0:
                    act.activation(probs[:, b, 0:NCTX], ps[:, 3 + u % 2, 0:NCTX], ACT.Exp, bias=stats[:, b, 2:3],
                                   accum_out=stats[:, b, 3:4]).then_inc(exps, 1)
                else:
                    act.activation(probs[:, b, 0:NLAT], probs[:, b, 0:NLAT], ACT.Exp, bias=stats[:, b, 2:3],
                                   accum_out=stats[:, b, 3:4])
                    act.activation(probs[:, b, NLAT:N], ps[:, 3 + u % 2, NLAT:N], ACT.Exp, bias=stats[:, b, 2:3],
                                   accum_out=stats[:, b, 4:5]).then_inc(exps, 1)

            def ln_act(stage):
                if stage == 2:
                    act.wait_ge(ln_centred, 1)
                    act.activation(csq[:], acc[:], ACT.Square).then_inc(ln_sq, 1)
                elif stage == 3:
                    act.wait_ge(ln_var, 1)
                    act.activation(crs[:], ps[:, 0, 0:CO], ACT.Sqrt, bias=eps_t[:, 0:1], scale=1.0 / CW).then_inc(ln_std, 1)
                elif stage == 6:
                    act.wait_ge(ln_out, 1)
                    act.activation(csq[:], acc[:], ACT.Tanh, scale=0.5).then_inc(ln_tanh, 1)
                elif stage == 7:
                    act.wait_ge(silu_ready, 1)
                    act.wait_ge(store_k, 16)
                    for at, o in ((0, 0), (LAT0, NCTX)):
                        w = NCTX if o == 0 else NLAT
                        act.activation(cv_hi[:, :, o:o + w], acc[:, :, at:at + w], ACT.Copy, scale=0.5)\
                            .then_inc(cv_hi_ready, 1)

            def turned_copy(u):
                h, part = u // 3, u % 3
                act.wait_ge(turned, u + 1)
                if h >= 1:
                    act.wait_ge(pv_done, h)
                if part == 0:
                    act.activation(ptc[:], ps[:, 5 + u % 2, 0:P], ACT.Copy).then_inc(turned_out, 1)
                else:
                    act.activation(ptl[:, :, part - 1, :], ps[:, 5 + u % 2, 0:3 * P].rearrange("p (a q) -> p a q", a=3),
                                   ACT.Copy).then_inc(turned_out, 1)

            for what, n in WINDOW:
                if what == "chunk":
                    kind, j = SLOTS[n // 2]
                    split_to(n + 4)
                elif what == "mod":
                    if n % 2 == 0 and SLOTS[n // 2][1] > MOD_WINDOW[0]:
                        mod_row(SLOTS[n // 2][1] - 1)
                    split_to(n + 4)
                elif what == "ln":
                    ln_act(n)
                elif what == "glu":
                    act.wait_ge(chunk_done, first_chunk("uc", n) + 2)
                    act.wait_ge(zpad_zero, 1)
                    act.activation(csq[:, n, 0:N], ps[:, 4 + 2 * n, 0:N], ACT.Tanh, scale=0.5).then_inc(glu_tanh, 1)
                elif what == "fpos":
                    act.wait_ge(fnet_pos, 2 * n + 1)
                    if n == 1:
                        act.wait_ge(fnet_feat, 1)
                    act.activation(z_cs[:, :, 0:NCTX], ps[:, 0, 0:2 * NCTX].rearrange("p (a n) -> p a n", a=2), ACT.Copy)
                    act.wait_ge(fnet_pos, 2 * n + 2)
                    act.activation(z_cs[:, :, NCTX:N], ps[:, 1, 0:2 * NLAT].rearrange("p (a n) -> p a n", a=2), ACT.Copy)\
                        .then_inc(z_ready, 1)
                elif what == "ffeat":
                    act.wait_ge(fnet_feat, n + 1)
                    act.activation(fn_hi[:, n, :], ps[:, 2, 0:N], ACT.Copy).then_inc(fn_hi_ready, 1)
                elif what == "unit" and n < UNITS:
                    exp_unit(n)
                elif what == "turn" and 0 <= n:
                    if n < UNITS:
                        turned_copy(n)
                    if n and n % 6 == 0:
                        pair = n // 6 - 1
                        act.wait_ge(pv_done, 2 * pair + 2)
                        act.activation(at_hi[:, pair, :], ps[:, 7, 0:N], ACT.Copy).then_inc(at_hi_ready, 1)
            act.wait_ge(v_ready, 2)
            act.dma_start(new_v[0, 0].rearrange("h n d -> n h d"), v_tok[:, 0, :].rearrange("p (h d) -> p h d", h=HEADS))\
                .then_inc(store_v, 16)
            mod_row(MOD_WINDOW[-1])
            act.wait_ge(store_v, 16)
            for kind, j in UG:
                c0 = first_chunk(kind, j)
                for b, i in ((1, c0), (2, c0 + 1)) if kind == "g12" else ((0, c0),):
                    split_to(i + 4)
                    act.wait_ge(chunk_done, i + 1)
                    if j >= 1:
                        act.wait_ge(merged, j)
                    act.activation(th[:, b, :], ps[:, gate_bank(j, b), 0:N], ACT.Tanh, scale=0.5).then_inc(gate_tanh, 1)
                    if b == 1 and j >= 1:
                        act.activation(mg_hi[:, j - 1, :], mg[:, (j - 1) % 2, :], ACT.Copy, scale=0.5)\
                            .then_inc(mg_hi_ready, 1)
                if kind == "g0b":
                    split_to(c0 + 5)
            act.wait_ge(merged, KT)
            act.activation(mg_hi[:, KT - 1, :], mg[:, (KT - 1) % 2, :], ACT.Copy, scale=0.5).then_inc(mg_hi_ready, 1)
            link(act.activation(stats[:, 0, 7:8], eps_t[:, 0:1], ACT.Sqrt))
            for n in range(KT):
                split_to(2 * WO0 + n + 4)
                act.wait_ge(x1_ready, n + 1)
                square(KT + n, xT[:, n, :])
            std(1, 2)
            mod_row(MOD_LAST[0])
            split_to(PRE_CH - 2)
            for k in range(KT):
                if k in H2_BY_POOL:
                    continue
                act.wait_ge(h2_scaled, k + 1)
                for a, b, which in SEG:
                    ins = act.activation(h2T[:, k, a:b], h2T[:, k, a:b], ACT.Identity, scale=scale2[:, k, which:which + 1],
                                         bias=modT[:, 24 + k, which:which + 1])
                ins.then_inc(h2_ready, 1)
            mod_row(MOD_LAST[-2])
            split_to(PRE_CH)
            act.wait_ge(logits, 1)
            act.activation(lgT[:], ps[0:GROUPS + NE, 3, 0:N], ACT.Copy).then_inc(logits_out, 1)
            tok_banks = (0, 4, 6)
            for t in range(NT):
                act.wait_ge(h2_turned, t + 1)
                act.activation(ht_hi[:, t, :], ps[:, tok_banks[t]:tok_banks[t] + 2, :].rearrange("p a n -> p (a n)"),
                               ACT.Copy).then_inc(ht_hi_ready, 1)
            mod_row(MOD_LAST[-1])
            act.wait_ge(grp_shift, 1)
            act.activation(rt[:, :, 8:12], rt[:, :, 4:8], ACT.Exp).then_inc(grp_exp, 1)
            act.wait_ge(exp_gap, 1)
            act.activation(rt[:, :, 21:22], rt[:, :, 20:21], ACT.Exp).then_inc(exp2, 1)

            def hg_copy(nx, bank=5):
                act.wait_ge(gathered, nx + 1)
                act.activation(hg32[:], ps[:, bank:bank + 2, :].rearrange("p a n -> p (a n)"), ACT.Copy).then_inc(hg_out, 1)

            def hg_high(nx, bank=5):
                act.wait_ge(hg_turned, nx + 1)
                act.activation(hg_hi[:].rearrange("p k s -> p (k s)"), ps[:, bank:bank + 2, :].rearrange("p a n -> p (a n)"),
                               ACT.Copy).then_inc(hg_hi_ready, 1)

            hg_copy(0, 0)
            hg_high(0, 0)
            act.dma_start(fg_b[:], final_g.rearrange("(a n) -> a n", a=1).to_broadcast([P, D])).then_inc(fg_in, 16)

            def item(it, g):
                for i in range(3):
                    act_split_item(act, it, i)
                act.wait_ge(weighted, it + 1)
                act.activation(cmb[:], ps[:, 7, 0:EPG], ACT.Copy).then_inc(cmb_ready, 1)

                def tanh_e(e):
                    act.wait_ge(chunk_done, it * ITEM_CH + PRE_CH + up_chunks[e][3] + 1)
                    if e >= 2:
                        act.wait_ge(hid_ready, it * EPG + e - 1)
                    act.activation(th_e[:, e % 2, :], ps[:, e % 2, 0:EH], ACT.Tanh, scale=0.5).then_inc(e_tanh, 1)

                def hd_high(e):
                    act.wait_ge(hid_turned, it * EPG + e + 1)
                    act.activation(hd_hi[:].rearrange("p a n -> p (a n)"), ps[:, 4, 0:2 * P], ACT.Copy).then_inc(hd_hi_ready, 1)

                for what, e, part, i in order:
                    if what == "up" and part == 1 and e == 1:
                        tanh_e(0)
                    if what == "down" and part == (0 if e == EPG - 2 else 1) and e < EPG - 1:
                        tanh_e(e + 1)
                    if what == "up" and part == 3 and e >= 1:
                        hd_high(e - 1)
                    if i + 3 < ITEM_CH:
                        act_split_item(act, it, i + 3)
                    if i == 0:
                        act.wait_ge(y_zero, 1)
                        act.wait_ge(chunk_done, it * ITEM_CH + PRE_CH)
                        act.activation(y_hi[:], ps[:, 2:4, :].rearrange("p a n -> p (a n)"), ACT.Copy)\
                            .then_inc(y_hi_ready, 1)
                    if what == "up" and part == 2 and e == SEL_TURN:
                        act.wait_ge(sel_turned, it + 1)
                        act.activation(selT[:], ps[:, 7, P:4 * P], ACT.Copy).then_inc(selT_ready, 1)
                    if what == "up" and part == 3 and e == EPG - 1:
                        hg_copy(it + 1)
                    if what == "down" and part == 1 and e == EPG - 2:
                        hd_high(EPG - 1)
                        hg_high(it + 1)

            rounds(act, item)
            act.wait_ge(y_last, 1)
            for half in range(2):
                act.activation(y_hi[:, 512 * half:512 * half + 512], ps[:, 2 + half, :], ACT.Copy).then_inc(y_hi_last, 1)
            link(act.activation(stats[:, 0, 7:8], eps_t[:, 0:1], ACT.Sqrt))
            out_banks = (0, 2, 5)
            for t in range(NT):
                act.wait_ge(out_turned, t + 1)
                link(act.activation(junk[:], ps[:, out_banks[t]:out_banks[t] + 2, :].rearrange("p a n -> p (a n)"),
                                    ACT.Square, accum_out=fin[:, t:t + 1]))
                act.activation(fin[:, 3 + t:4 + t], fin[:, t:t + 1], ACT.Sqrt, bias=eps_t[:, 0:1], scale=1.0 / D)\
                    .then_inc(out_std, 1)

        @block.vector
        def _(dve):
            step = 0

            def link(ins):
                nonlocal step
                step += 1
                ins.then_inc(dve_step, 1)
                dve.wait_ge(dve_step, step)

            split_at = 0

            def split_to(n):
                nonlocal split_at
                while split_at < min(n, PRE_CH):
                    if not POOL_PRE[split_at]:
                        low_split(dve, split_at)
                    split_at += 1

            dve.wait_ge(vec_turned, 1)
            dve.tensor_copy(vec_t[:], ps[:, 3, 0:V_ROWS]).then_inc(vec_ready, 1)
            dve.wait_ge(vec_turned, 2)
            link(dve.tensor_scalar(taps[:].rearrange("p a t -> p (a t)"), ps[:, 2, 0:2 * CK], 0.5, None, ALU.mult))
            dve.wait_ge(cond_tanh, 1)
            both = cond[:].rearrange("p a k -> p (a k)")
            link(dve.scalar_tensor_tensor(out=both, in0=cond_t[:].rearrange("p a k -> p (a k)"), scalar=1.0,
                                          in1=vec_t[:, V_CTX:V_CTX + 16], op0=ALU.add, op1=ALU.mult))
            link(dve.tensor_scalar(both, both, 0.5, None, ALU.mult))
            link(dve.tensor_copy(cond4[:, :, 0:2], cond[:].rearrange("p a k -> p k a")))
            dve.tensor_tensor(cond4[:, :, 2:4], cond[:].rearrange("p a k -> p k a"), cond4[:, :, 0:2].bitcast(F32),
                              ALU.subtract).then_inc(cond_ready, 1)
            for j in range(8):
                if j < KT // 2:
                    for k in (2 * j, 2 * j + 1):
                        dve.wait_ge(x_turned, k + 1)
                        dve.tensor_copy(xT[:, k, :], ps[:, 4 + k % 3, 0:N]).then_inc(x_ready, 1)
                if j == KT // 2 + 1:
                    dve.wait_ge(std_ready, 1)
                    dve.reciprocal(rstd[:], rstd[:]).then_inc(rstd_ready, 1)
                split_to(min(2 * j + 4, first_chunk("q") + 1))
                split_to(min(2 * j + 5, first_chunk("q") + 1))

            def mod_finish(first, n, bank):
                dve.tensor_copy(mod_tmp[:, 0:n, :], ps[:, bank, 4 * first:4 * (first + n)]
                                .rearrange("p (t r) -> p t r", r=4)).then_inc(mod_copied, 1)
                dve.wait_ge(mod_copied, {0: 1, 2 * MOD_WINDOW[0]: 2, 2 * MOD_LAST[0]: 3, 2 * MOD_LAST[-1]: 4}[first])
                m = modT[:, first:first + n, :]
                link(dve.tensor_tensor(m, mod_tmp[:, 0:n, 0:2], mod_tmp[:, 0:n, 2:4], ALU.add))
                for a in range(2):
                    ins = dve.tensor_tensor(modT[:, first:first + n, a], modT[:, first:first + n, a],
                                            vec_t[:, V_BM + first:V_BM + first + n], ALU.add)
                    link(ins)

            def norm_scale(dst, mod, vec):
                for a in range(2):
                    ins = dve.scalar_tensor_tensor(out=dst[:, :, a], in0=modT[:, 8 * mod:8 * mod + 8, a], scalar=1.0,
                                                   in1=vec_t[:, vec:vec + 8], op0=ALU.add, op1=ALU.mult)
                    if a == 0:
                        link(ins)
                return ins

            dve.wait_ge(mod_turned, 8)
            mod_finish(0, 16, 2)
            norm_scale(scale1, 1, V_N1).then_inc(mod_ready, 1)
            dve.wait_ge(mod_ready, 1)
            dve.wait_ge(h_scaled, KT)
            for k in H_BY_DVE:
                modulate_h(dve, k).then_inc(h32_ready_dve, 1)
            for k in range(KT):
                dve.wait_ge(h_hi_ready, k + 1)
                dve.tensor_tensor(h_lo[:, k, :], h32[:, k, :], h_hi[:, k, :].bitcast(F32), ALU.subtract).then_inc(h_ready, 1)
            c_q, c_k = first_chunk("q"), first_chunk("k")
            for n in range(4):
                split_to(c_q + n + 4)
            dve.wait_ge(h_ready, KT)
            for n in range(4):
                split_to(c_k + n + 4)
                dve.wait_ge(chunk_done, c_k + n + 1)
                dve.tensor_copy(kT[:, n, :], ps[:, n % 2, 0:N]).then_inc(k_ready, 1)
            dve.wait_ge(kctx_turned, 1)
            dve.tensor_copy(k_out[:], ps[:, 6, :]).then_inc(kout_ready, 1)

            def max_unit(u):
                b, part, h = u % 3, u % 3, u // 3
                dve.wait_ge(scores, u + 1)
                if u >= 3:
                    dve.wait_ge(turned, u - 2)
                s = ps[:, 3 + u % 2, :]
                if part == 0:
                    link(dve.reduce_max(stats[:, b, 0:1], s[:, 0:NCTX], AX))
                    dve.tensor_scalar(stats[:, b, 2:3], stats[:, b, 0:1], -1.0, None, ALU.mult).then_inc(negmax, 1)
                    return
                t = part - 1
                if u == 1:
                    dve.wait_ge(mask_step, 4)
                rows = bias[:, h, 2 - 2 * t:6 - 2 * t, :].rearrange("p s c -> p (s c)")
                dve.reduce_max(stats[:, b, 0:1], s[:, NLAT:N], AX)
                link(dve.tensor_tensor_reduce(out=probs[:, b, 0:NLAT], in0=s[:, 0:NLAT], in1=rows, scale=1.0,
                                              scalar=-3e38, op0=ALU.add, op1=ALU.max, accum_out=stats[:, b, 1:2]))
                dve.tensor_scalar(stats[:, b, 2:3], stats[:, b, 0:1], stats[:, b, 1:2], -1.0, ALU.max, ALU.mult)\
                    .then_inc(negmax, 1)

            def normalise_unit(u):
                b, part = u % 3, u % 3
                dve.wait_ge(exps, u + 1)
                total, w = stats[:, b, 3:4], NCTX
                if part:
                    link(dve.tensor_tensor(stats[:, b, 5:6], stats[:, b, 3:4], stats[:, b, 4:5], ALU.add))
                    total, w = stats[:, b, 5:6], N
                link(dve.reciprocal(stats[:, b, 6:7], total))
                dve.tensor_scalar(probs[:, b, 0:w], probs[:, b, 0:w], stats[:, b, 6:7], None, ALU.mult)\
                    .then_inc(probs_ready, 1)

            conv_n = 0

            def conv_taps(n):
                nonlocal conv_n
                for _ in range(n):
                    if conv_n == 2 * CK:
                        return
                    t, a = conv_n // 2, conv_n % 2
                    if t == 0:
                        ins = dve.tensor_scalar(acc[:, a, :], zpad[:, a, 0:CO], taps[:, a, 0:1],
                                                vec_t[:, V_CB + a:V_CB + a + 1], ALU.mult, ALU.add)
                    else:
                        dve.wait_ge(conv_step, conv_n - 1)
                        ins = dve.scalar_tensor_tensor(out=acc[:, a, :], in0=zpad[:, a, t:t + CO], scalar=taps[:, a, t:t + 1],
                                                       in1=acc[:, a, :], op0=ALU.mult, op1=ALU.add)
                    ins.then_inc(conv_step, 1)
                    conv_n += 1

            def ln_dve(stage):
                if stage == 0:
                    conv_taps(2 * CK)
                elif stage == 2:
                    dve.wait_ge(ln_mean, 1)
                    for a in range(2):
                        ins = dve.scalar_tensor_tensor(out=acc[:, a, :], in0=ps[:, 0, 0:CO], scalar=-1.0 / CW,
                                                       in1=acc[:, a, :], op0=ALU.mult, op1=ALU.add)
                    ins.then_inc(ln_centred, 1)
                elif stage == 4:
                    dve.wait_ge(ln_std, 1)
                    link(dve.reciprocal(crs[:], crs[:]))
                elif stage == 5:
                    dve.wait_ge(ln_centred, 1)
                    dve.wait_ge(ln_sq, 1)
                    for a in range(2):
                        link(dve.tensor_tensor(acc[:, a, :], acc[:, a, :], crs[:], ALU.mult))
                    for a in range(2):
                        ins = dve.tensor_scalar(acc[:, a, :], acc[:, a, :], vec_t[:, V_LG + a:V_LG + a + 1],
                                                vec_t[:, V_LB + a:V_LB + a + 1], ALU.mult, ALU.add)
                        if a == 0:
                            link(ins)
                        else:
                            ins.then_inc(ln_out, 1)
                elif stage == 6:
                    dve.wait_ge(ln_out, 1)
                    dve.wait_ge(ln_tanh, 1)
                    dve.scalar_tensor_tensor(out=acc[:], in0=csq[:], scalar=1.0, in1=acc[:], op0=ALU.add, op1=ALU.mult)\
                        .then_inc(silu_ready, 1)
                elif stage == 8:
                    for i, (at, o) in enumerate(((0, 0), (LAT0, NCTX))):
                        w = NCTX if o == 0 else NLAT
                        dve.wait_ge(cv_hi_ready, i + 1)
                        dve.scalar_tensor_tensor(out=cv_lo[:, :, o:o + w], in0=acc[:, :, at:at + w], scalar=0.5,
                                                 in1=cv_hi[:, :, o:o + w].bitcast(F32), op0=ALU.mult, op1=ALU.subtract)\
                            .then_inc(cv_ready, 1)

            conv_open = False
            for what, n in WINDOW:
                if what == "chunk":
                    kind, j = SLOTS[n // 2]
                    split_to(n + 4)
                    if kind in ("uf", "v") and n % 2 == 1:
                        dve.wait_ge(chunk_done, n + 1)
                        dst = u_tok[:] if kind == "uf" else v_tok[:, :, 256 * j:256 * j + 256]
                        dve.tensor_copy(dst, ps[:, 0:3, 0:256]).then_inc(u_ready if kind == "uf" else v_ready, 1)
                elif what == "mod":
                    split_to(n + 4)
                elif what == "ln":
                    ln_dve(n)
                elif what == "glu":
                    dve.wait_ge(glu_tanh, n + 1)
                    for i, (a, b, which) in enumerate(SEG):
                        at = PAD if which == 0 else PAD + LAT0
                        ins = dve.scalar_tensor_tensor(out=zpad[:, n, at:at + b - a], in0=csq[:, n, a:b], scalar=1.0,
                                                       in1=ps[:, 3 + 2 * n, a:b], op0=ALU.add, op1=ALU.mult)
                        if i == 0:
                            link(ins)
                        else:
                            ins.then_inc(z_conv, 1)
                    conv_open = conv_open or n == 1
                elif what == "ffeat":
                    dve.wait_ge(fn_hi_ready, n + 1)
                    dve.tensor_tensor(fn_lo[:, n, :], ps[:, 2, 0:N], fn_hi[:, n, :].bitcast(F32), ALU.subtract)\
                        .then_inc(fn_ready, 1)
                    if n == 1:
                        dve.memset(zpad[:].rearrange("p a z -> p (a z)"), 0.0).then_inc(zpad_zero, 1)
                        dve.wait_ge(zpad_zero, 1)
                elif what == "unit":
                    if n < UNITS:
                        max_unit(n)
                    if 1 <= n <= UNITS:
                        normalise_unit(n - 1)
                    if conv_open:
                        if conv_n == 0:
                            dve.wait_ge(z_conv, 2)
                        conv_taps(TAPS_PER_UNIT)
                elif what == "turn" and n > 0 and n % 6 == 0:
                    pair = n // 6 - 1
                    dve.wait_ge(at_hi_ready, pair + 1)
                    dve.tensor_tensor(at_lo[:, pair, :], ps[:, 7, 0:N], at_hi[:, pair, :].bitcast(F32), ALU.subtract)\
                        .then_inc(at_ready, 1)
            def merge_low(d):
                dve.wait_ge(mg_hi_ready, d + 1)
                dve.scalar_tensor_tensor(out=mg_lo[:, d, :], in0=mg[:, d % 2, :], scalar=0.5,
                                         in1=mg_hi[:, d, :].bitcast(F32), op0=ALU.mult, op1=ALU.subtract)\
                    .then_inc(mg_ready, 1)

            for kind, j in UG:
                c0 = first_chunk(kind, j)
                if kind != "g0b":
                    split_to(c0 + 5)
                    if kind == "g12" and j >= 1:
                        merge_low(j - 1)
                    continue
                if j == 0:
                    dve.wait_ge(mod_turned, MOD_WINDOW[-1] + 1)
                    mod_finish(2 * MOD_WINDOW[0], 2 * len(MOD_WINDOW), 2)
                    link(norm_scale(scale2, 4, V_N2))
                split_to(c0 + 5)
                dve.wait_ge(gate_tanh, 3 * j + 3)
                dve.wait_ge(chunk_done, c0 + 2)
                m = mg[:, j % 2, :]
                link(dve.scalar_tensor_tensor(out=m, in0=th[:, 0, :], scalar=1.0, in1=ps[:, 0, 0:N],
                                              op0=ALU.add, op1=ALU.mult))
                for b in (1, 2):
                    link(dve.scalar_tensor_tensor(out=mt[:, b - 1, :], in0=th[:, b, :], scalar=1.0, in1=ps[:, b, 0:N],
                                                  op0=ALU.add, op1=ALU.mult))
                    ins = dve.tensor_tensor(m, m, mt[:, b - 1, :], ALU.add)
                    if b == 1:
                        link(ins)
                    else:
                        ins.then_inc(merged, 1)
            merge_low(KT - 1)
            for n in range(KT):
                split_to(2 * WO0 + n + 4)
                dve.wait_ge(chunk_done, 2 * WO0 + n + 1)
                for a, b, which in SEG:
                    ins = dve.scalar_tensor_tensor(out=xT[:, n, a:b], in0=ps[:, 5 + n % 2, a:b],
                                                   scalar=modT[:, 16 + n, which:which + 1], in1=xT[:, n, a:b],
                                                   op0=ALU.mult, op1=ALU.add)
                ins.then_inc(x1_ready, 1)
            dve.wait_ge(x1_ready, KT)
            dve.wait_ge(std_ready, 2)
            link(dve.reciprocal(rstd[:], rstd[:]))
            for k in range(KT):
                dve.tensor_tensor(h2T[:, k, :], xT[:, k, :], rstd[:], ALU.mult).then_inc(h2_scaled, 1)
            split_to(PRE_CH)
            dve.wait_ge(mod_turned, 23)
            mod_finish(2 * MOD_LAST[0], 2 * (len(MOD_LAST) - 1), 7)
            dve.wait_ge(logits_turned, 1)
            dve.wait_ge(gr_in, 64)
            for t in range(NT):
                ins = dve.tensor_tensor(lg[:, t, :], ps[:, 2, 36 * t:36 * t + 36], b_gr[:], ALU.add)
            link(ins)

            def bc(ap, n):
                return ap.to_broadcast([P, NT, n])

            def first_max(dst, src, n, m, scratch):
                link(dve.tensor_reduce(m, src, axis=AX, op=ALU.max))
                link(dve.tensor_tensor(dst, src, bc(m, n), ALU.is_equal))
                w = iota_s[:, P - n:P].rearrange("p (a e) -> p a e", a=1).to_broadcast([P, NT, n])
                link(dve.tensor_scalar(scratch[1], w, -1.0, float(P), ALU.mult, ALU.add))
                link(dve.tensor_tensor(dst, dst, scratch[1], ALU.mult))
                link(dve.tensor_reduce(scratch[0], dst, axis=AX, op=ALU.max))
                return dve.tensor_tensor(dst, dst, bc(scratch[0], n), ALU.is_equal)

            glog = lg[:, :, 0:GROUPS]
            first_max(og[:], glog, GROUPS, rt[:, :, 0:1], (rt[:, :, 14:15], rt[:, :, 24:28])).then_inc(group_hot, 1)
            dve.wait_ge(group_hot, 1)
            dve.tensor_tensor(rt[:, :, 4:8], glog, bc(rt[:, :, 0:1], GROUPS), ALU.subtract).then_inc(grp_shift, 1)
            dve.wait_ge(ranks, 1)
            link(dve.tensor_copy(rk[:], ps[:, 3, 0:12].rearrange("p (t g) -> p t g", t=NT)))
            link(dve.tensor_copy(tot[:], ps[:, 3, 16:28].rearrange("p (t g) -> p t g", t=NT)))
            for t in range(1, NT):
                link(dve.tensor_tensor(rk[:, t, :], rk[:, t, :], tot[:, t - 1, :], ALU.add))
                link(dve.tensor_tensor(tot[:, t, :], tot[:, t, :], tot[:, t - 1, :], ALU.add))
            dve.wait_ge(consts_ready, 7)
            link(dve.tensor_tensor(rk[:], rk[:], goff[:].rearrange("p (a g) -> p a g", a=1).to_broadcast([P, NT, GROUPS]),
                                   ALU.add))
            link(dve.tensor_tensor(rk[:], rk[:], og[:], ALU.mult))
            link(dve.tensor_reduce(key[:], rk[:], axis=AX, op=ALU.add))
            link(dve.tensor_tensor(keysh[:], key[:].rearrange("p (a t) -> p a t", a=1).to_broadcast([P, 16, NT]),
                                   i_base[:].rearrange("p (i a) -> p i a", a=1).to_broadcast([P, 16, NT]), ALU.subtract))
            link(dve.tensor_reduce(rt[:, 0, 15:16], tot[:, NT - 1, :], axis=AX, op=ALU.max))
            dve.tensor_scalar(over[:], rt[:, 0, 15:16], float(P), None, ALU.is_gt).then_inc(routed, 1)
            def select(nx):
                for t in range(NT):
                    ins = dve.tensor_scalar(sel[:, t, :], iota_s[:], keysh[:, bass.ds(nx, 1), t] if not isinstance(nx, int)
                                            else keysh[:, nx:nx + 1, t], None, ALU.is_equal)
                    ins.then_inc(sel_ready, 1)

            def hg_low(nx, bank=5):
                dve.wait_ge(hg_hi_ready, nx + 1)
                dve.tensor_tensor(hg_lo[:].rearrange("p k s -> p (k s)"), ps[:, bank:bank + 2, :].rearrange("p a n -> p (a n)"),
                                  hg_hi[:].rearrange("p k s -> p (k s)").bitcast(F32), ALU.subtract).then_inc(hg_ready, 1)

            select(0)
            tok_banks = (0, 4, 6)
            for t in range(NT):
                dve.wait_ge(ht_hi_ready, t + 1)
                dve.tensor_tensor(ht_lo[:, t, :], ps[:, tok_banks[t]:tok_banks[t] + 2, :].rearrange("p a n -> p (a n)"),
                                  ht_hi[:, t, :].bitcast(F32), ALU.subtract).then_inc(ht_ready, 1)
            for t in range(NT):
                el = lg[:, t, GROUPS:].rearrange("p (g e) -> p e g", g=GROUPS)
                ins = dve.tensor_tensor(pr[:, t, :, :], el, og[:, t:t + 1, :].to_broadcast([P, EPG, GROUPS]), ALU.mult)
            link(ins)
            link(dve.tensor_reduce(e_sel[:].rearrange("p t e -> p (t e)"), pr[:].rearrange("p t e g -> p (t e) g"),
                                   axis=AX, op=ALU.add))
            link(first_max(o1[:], e_sel[:], EPG, rt[:, :, 16:17], (rt[:, :, 14:15], rt[:, :, 24:32])))
            link(dve.scalar_tensor_tensor(out=e_sel[:], in0=o1[:], scalar=NEG, in1=e_sel[:], op0=ALU.mult, op1=ALU.add))
            link(first_max(o2[:], e_sel[:], EPG, rt[:, :, 17:18], (rt[:, :, 14:15], rt[:, :, 24:32])))
            dve.tensor_tensor(rt[:, :, 20:21], rt[:, :, 17:18], rt[:, :, 16:17], ALU.subtract).then_inc(exp_gap, 1)
            dve.wait_ge(grp_exp, 1)
            link(dve.tensor_reduce(rt[:, :, 12:13], rt[:, :, 8:12], axis=AX, op=ALU.add))
            dve.wait_ge(exp2, 1)
            link(dve.tensor_scalar(rt[:, :, 22:23], rt[:, :, 21:22], 1.0, None, ALU.add))
            link(dve.tensor_tensor(rt[:, :, 22:23], rt[:, :, 22:23], rt[:, :, 12:13], ALU.mult))
            link(dve.reciprocal(rt[:, :, 23:24], rt[:, :, 22:23]))
            link(dve.tensor_scalar(rt[:, :, 23:24], rt[:, :, 23:24], 0.5, None, ALU.mult))
            link(dve.tensor_tensor(rt[:, :, 21:22], rt[:, :, 21:22], rt[:, :, 23:24], ALU.mult))
            link(dve.tensor_tensor(o1[:], o1[:], bc(rt[:, :, 23:24], EPG), ALU.mult))
            link(dve.tensor_tensor(o2[:], o2[:], bc(rt[:, :, 21:22], EPG), ALU.mult))
            dve.tensor_tensor(comb[:], o1[:], o2[:], ALU.add).then_inc(comb_ready, 1)

            dve.wait_ge(mod_turned, 24)
            mod_finish(2 * MOD_LAST[-1], 2, 2)
            dve.memset(ps[:, 2:4, :].rearrange("p a n -> p (a n)"), 0.0).then_inc(y_zero, 1)
            hg_low(0, 0)

            def add_back(k, bank, combined, n, added):
                dve.wait_ge(combined, n)
                for a, b, which in SEG:
                    dve.scalar_tensor_tensor(out=xT[:, k, a:b], in0=ps[:, bank, a:b],
                                             scalar=modT[:, 40 + k, which:which + 1], in1=xT[:, k, a:b],
                                             op0=ALU.mult, op1=ALU.add).then_inc(added, 1)

            def item(it, g):
                for i in range(3):
                    dve_split_item(dve, it, i)

                def hid_e(e):
                    n = it * EPG + e
                    dve.wait_ge(e_tanh, n + 1)
                    if e == 0:
                        dve.wait_ge(cmb_ready, it + 1)
                    if e >= 2:
                        dve.wait_ge(hid_turned, n - 1)
                    dve.scalar_tensor_tensor(out=s_e[:, e % 2, :], in0=th_e[:, e % 2, :], scalar=1.0, in1=ps[:, e % 2, 0:EH],
                                             op0=ALU.add, op1=ALU.mult).then_inc(silu_e, 1)
                    dve.wait_ge(silu_e, n + 1)
                    dve.scalar_tensor_tensor(out=hid[:, e % 2, :], in0=s_e[:, e % 2, :], scalar=cmb[:, e:e + 1],
                                             in1=ps[:, e % 2, EH:2 * EH], op0=ALU.mult, op1=ALU.mult).then_inc(hid_ready, 1)

                def hd_low(e):
                    dve.wait_ge(hd_hi_ready, it * EPG + e + 1)
                    dve.tensor_tensor(hd_lo[:].rearrange("p a n -> p (a n)"), ps[:, 4, 0:2 * P],
                                      hd_hi[:].rearrange("p a n -> p (a n)").bitcast(F32), ALU.subtract).then_inc(hd_ready, 1)

                for what, e, part, i in order:
                    if (what == "up" and part == 2 and e == 1) or (what == "up" and part == 0 and e >= 2):
                        hid_e(e - 1)
                    if what == "down" and part == 0 and e == EPG - 2:
                        hid_e(EPG - 1)
                    if what == "up" and part == 3 and e >= 1:
                        hd_low(e - 1)
                    if i + 3 < ITEM_CH:
                        dve_split_item(dve, it, i + 3)
                    if i == 0:
                        dve.wait_ge(y_hi_ready, it + 1)
                        dve.tensor_tensor(y_lo[:], ps[:, 2:4, :].rearrange("p a n -> p (a n)"), y_hi[:].bitcast(F32),
                                          ALU.subtract).then_inc(y_ready, 1)
                    if COMBINE0 < i <= COMBINE0 + KT:
                        add_back(i - COMBINE0 - 1, 5 + (i - COMBINE0 - 1) % 2, combined, it * KT + i - COMBINE0, added)
                    if what == "up" and part == 1 and e == EPG - 2:
                        dve.wait_ge(sel_turned, it + 1)
                        select(it + 1)
                    if what == "down" and part == 1 and e == EPG - 2:
                        hd_low(EPG - 1)
                        hg_low(it + 1)

            rounds(dve, item)
            for half in range(2):
                cols = slice(512 * half, 512 * half + 512)
                dve.wait_ge(y_hi_last, half + 1)
                dve.tensor_tensor(y_lo[:, cols], ps[:, 2 + half, :], y_hi[:, cols].bitcast(F32), ALU.subtract)\
                    .then_inc(y_lo_last, 1)
            for k in range(KT):
                add_back(k, (4, 7)[k % 2], combined_last, k + 1, x2_ready)
            dve.wait_ge(fg_in, 16)
            out_banks = (0, 2, 5)
            for t in range(NT):
                dve.wait_ge(out_std, t + 1)
                link(dve.reciprocal(fin[:, 3 + t:4 + t], fin[:, 3 + t:4 + t]))
                dve.scalar_tensor_tensor(out=out_tiles[t],
                                         in0=ps[:, out_banks[t]:out_banks[t] + 2, :].rearrange("p a n -> p (a n)"),
                                         scalar=fin[:, 3 + t:4 + t], in1=fg_b[:], op0=ALU.mult, op1=ALU.mult)\
                    .then_inc(out_ready, 1)

        @block.tensor
        def _(pe):
            def three(out, a_hi, a_lo, b_hi, b_lo, start, stop):
                pe.matmul(out, a_hi, b_hi, start=start, stop=False)
                pe.matmul(out, a_hi, b_lo, start=False, stop=False)
                return pe.matmul(out, a_lo, b_hi, start=False, stop=stop)

            def column_chunk(i, bank, x_hi, x_lo, k0=0, kn=KT, x_ready=None):
                b = i % SPLIT
                for k in range(k0, k0 + kn):
                    if x_ready is not None:
                        pe.wait_ge(x_ready, k + 1)
                    w = slice(P * k, P * k + P)
                    ins = three(ps[:, bank, 0:N], w_hi[:, b, w], w_lo[:, b, w], x_hi[:, k - k0, :], x_lo[:, k - k0, :],
                                k == k0, k == k0 + kn - 1)
                return ins

            def token_chunk(i):
                b, half = i % SPLIT, i % 2
                for k in range(4):
                    w = slice(256 * k, 256 * k + 256)
                    for t in range(NT):
                        x = slice(P * t, P * t + P)
                        ins = three(ps[:, t, 0:256], h_hi[:, 4 * half + k, x], h_lo[:, 4 * half + k, x],
                                    w_hi[:, b, w], w_lo[:, b, w], half == 0 and k == 0, half == 1 and k == 3)
                return ins

            def mod_slot(j, halves=range(2)):
                bank, c0 = mod_bank(j), first_chunk("mod", j)
                if j >= 2 and halves[0] == 0:
                    pe.wait_ge(modrow_ready, j if j in MOD_WINDOW else j - 1)
                for half in halves:
                    i = c0 + half
                    wait_lo(pe, i)
                    for k in range(4):
                        w = slice(256 * k, 256 * k + 256)
                        pe.matmul(ps[0:4, bank, 0:256], cond4[:, 4 * half + k, :], w_hi[:, i % SPLIT, w],
                                  start=half == 0 and k == 0, stop=False)
                        ins = pe.matmul(ps[0:4, bank, 0:256], cond4[:, 4 * half + k, :], w_lo[:, i % SPLIT, w],
                                        start=False, stop=half == 1 and k == 3)
                    ins.then_inc(chunk_done, 1)

            def mod_turn(j):
                pe.wait_ge(modrow_ready, j + 1)
                bank = 7 if j in MOD_LAST[:-1] else 2
                for t in range(2):
                    at = 4 * (2 * j + t)
                    ins = pe.transpose(ps[:, bank, at:at + 4], modrow[:, j % 2, P * t:P * t + P], ident[0:4, 0:4])
                ins.then_inc(mod_turned, 1)

            def ssq(n, bank):
                pe.wait_ge(sq_ready, n + 1)
                pe.matmul(ps[:, bank, 0:N], ones[:], sq[:, n % 2, :], start=n % KT == 0, stop=n % KT == KT - 1)\
                    .then_inc(ssq_step, 1)

            pe.wait_ge(consts_ready, 5)
            pe.wait_ge(rows_in, 16)
            pe.transpose(ps[:, 3, 0:V_ROWS], vec_rows[:], ident[0:V_ROWS, 0:V_ROWS]).then_inc(vec_turned, 1)
            pe.wait_ge(taps_in, 32)
            pe.transpose(ps[:, 2, 0:2 * CK], tap_rows[:], ident[0:2 * CK, 0:2 * CK]).then_inc(vec_turned, 1)
            pe.wait_ge(x_in, 16 * NT)
            for j in range(8):
                if j < KT // 2:
                    for k in (2 * j, 2 * j + 1):
                        if k >= 3:
                            pe.wait_ge(x_ready, k - 2)
                        for t in range(NT):
                            ins = pe.transpose(ps[:, 4 + k % 3, P * t:P * t + P], x_tok[:, t, P * k:P * k + P], ident[:])
                        ins.then_inc(x_turned, 1)
                if j == 0:
                    pe.wait_ge(cond_ready, 1)
                mod_slot(j)
                if j < KT // 2:
                    ssq(2 * j, 7)
                    ssq(2 * j + 1, 7)
                if j:
                    mod_turn(j - 1)
            pe.wait_ge(ck_in, 16)
            for pair in range(PAIRS):
                ins = pe.transpose(ps[:, 5, P * pair:P * pair + P], ck_tok[:, 2 * pair:2 * pair + 2, :]
                                   .rearrange("p a d -> p (a d)"), ident[:])
            ins.then_inc(ck_turned, 1)
            mod_turn(7)
            c_q = first_chunk("q")
            for n in range(8):
                i = c_q + n
                if n == 0:
                    pe.wait_ge(modrow_ready, 8)
                if n >= 2:
                    pe.wait_ge(q_ready if n < 6 else k_ready, n - 1 if n < 6 else n - 5)
                wait_lo(pe, i)
                for k in range(KT):
                    if n == 0:
                        pe.wait_ge(h_ready, k + 1)
                    w = slice(P * k, P * k + P)
                    ins = three(ps[:, n % 2, 0:N], w_hi[:, i % SPLIT, w], w_lo[:, i % SPLIT, w], h_hi[:, k, :], h_lo[:, k, :],
                                k == 0, k == KT - 1)
                ins.then_inc(chunk_done, 1)
            pe.wait_ge(k_ready, 4)
            for pair in range(PAIRS):
                ins = pe.transpose(ps[:, 6, P * pair:P * pair + P], kT[:, pair, 0:NCTX], ident[:])
            ins.then_inc(kctx_turned, 1)

            def score_unit(u):
                h, part = u // 3, u % 3
                rows, pair = slice(HD * (h % 2), HD * (h % 2) + HD), h // 2
                bank = 3 + u % 2
                if u >= 2:
                    pe.wait_ge(exps, u - 1)
                if part == 0:
                    pe.matmul(ps[:, bank, 0:NCTX], qT[rows, pair, 0:NCTX], kT[rows, pair, 0:NCTX], start=True, stop=True)\
                        .then_inc(scores, 1)
                    return
                q = qT[rows, pair, P * part:P * part + P]
                pe.matmul(ps[:, bank, 0:NLAT], q, kT[rows, pair, NCTX:N], start=True, stop=True)
                pe.matmul(ps[:, bank, NLAT:N], q, ckT[rows, pair, :], start=True, stop=True).then_inc(scores, 1)

            def turn_unit(u):
                h, part = u // 3, u % 3
                pe.wait_ge(probs_ready, u + 1)
                if u >= 2:
                    pe.wait_ge(turned_out, u - 1)
                for a in range(1 if part == 0 else 3):
                    ins = pe.transpose(ps[:, 5 + u % 2, P * a:P * a + P], probs[:, u % 3, P * a:P * a + P], ident[:])
                ins.then_inc(turned, 1)

            def pv_unit(u):
                h, part = u // 3, u % 3
                if part < 2:
                    return
                pair, out = h // 2, slice(HD * (h % 2), HD * (h % 2) + HD)
                cols = slice(HD * h, HD * h + HD)
                if h == 0:
                    pe.wait_ge(v_ready, 2)
                    pe.wait_ge(cv_in, 16)
                if h % 2 == 0 and pair:
                    pe.wait_ge(at_ready, pair)
                pe.wait_ge(turned_out, u + 1)
                pe.matmul(ps[out, 7, 0:NCTX], v_tok[:, 0, cols], ptc[:], start=True, stop=True)
                for a in range(3):
                    v = v_tok[:, 1 + a, cols] if a < 2 else cv_tok[:, h, :]
                    ins = pe.matmul(ps[out, 7, NCTX:N], v, ptl[:, a, :, :].rearrange("p t q -> p (t q)"),
                                    start=a == 0, stop=a == 2)
                ins.then_inc(pv_done, 1)

            def ln_pe(stage):
                if stage == 1:
                    pe.wait_ge(conv_step, 2 * CK)
                    for a in range(2):
                        ins = pe.matmul(ps[:, 0, 0:CO], ones[:], acc[:, a, :], start=a == 0, stop=a == 1)
                    ins.then_inc(ln_mean, 1)
                elif stage == 3:
                    pe.wait_ge(ln_sq, 1)
                    for a in range(2):
                        ins = pe.matmul(ps[:, 0, 0:CO], ones[:], csq[:, a, :], start=a == 0, stop=a == 1)
                    ins.then_inc(ln_var, 1)

            for what, n in WINDOW:
                if what == "chunk":
                    kind, j = SLOTS[n // 2]
                    wait_lo(pe, n)
                    if kind in ("uf", "v"):
                        if kind == "uf" and n % 2 == 0:
                            pe.wait_ge(k_ready, 4)
                        if kind == "v" and n % 2 == 0:
                            pe.wait_ge(fn_ready, 2) if j == 0 else pe.wait_ge(v_ready, j)
                        token_chunk(n).then_inc(chunk_done, 1)
                    else:
                        if j == 1:
                            pe.wait_ge(ck_ready, 1)
                            pe.wait_ge(kout_ready, 1)
                        column_chunk(n, 3 + 2 * j + n % 2, h_hi, h_lo).then_inc(chunk_done, 1)
                elif what == "mod":
                    j = SLOTS[n // 2][1]
                    if j == MOD_WINDOW[0]:
                        pe.wait_ge(v_ready, 2)
                        pe.wait_ge(mod_copied, 1)
                    mod_slot(j, (n % 2,))
                    if n % 2 == 1 and j > MOD_WINDOW[0] + 1:
                        mod_turn(j - 2)
                elif what == "ln":
                    ln_pe(n)
                elif what == "fpos":
                    if n == 0:
                        pe.wait_ge(u_ready, 1)
                        pe.wait_ge(dft_in, 16 * 4)
                    else:
                        pe.wait_ge(z_ready, 1)
                    f = slice(P * n, P * n + P)
                    pe.matmul(ps[:, 0, 0:2 * NCTX], u_tok[:, 0, f], ctx_w[:], start=True, stop=True).then_inc(fnet_pos, 1)
                    for a in range(2):
                        ins = pe.matmul(ps[:, 1, 0:2 * NLAT], u_tok[:, 1 + a, f], lat_w[:, a, :], start=a == 0, stop=a == 1)
                    ins.then_inc(fnet_pos, 1)
                elif what == "ffeat":
                    pe.wait_ge(z_ready, n + 1)
                    if n == 1:
                        pe.wait_ge(fn_ready, 1)
                    for a in range(2):
                        ins = pe.matmul(ps[:, 2, 0:N], feat_w[:, a, :], z_cs[:, a, :], start=a == 0, stop=a == 1)
                    ins.then_inc(fnet_feat, 1)
                elif what == "unit" and n < UNITS:
                    if n == 0:
                        pe.wait_ge(z_conv, 2)
                    score_unit(n)
                elif what == "pv" and n >= 0:
                    pv_unit(n)
                elif what == "turn" and 0 <= n < UNITS:
                    turn_unit(n)
            for j in MOD_WINDOW[-2:]:
                mod_turn(j)
            for kind, j in UG:
                c0 = first_chunk(kind, j)
                for b, i in ((1, c0), (2, c0 + 1)) if kind == "g12" else ((0, c0),):
                    wait_lo(pe, i)
                    g = 3 * j + (b + 2) % 3
                    if g >= 2:
                        pe.wait_ge(gate_tanh, g - 1)
                    column_chunk(i, gate_bank(j, b), h_hi, h_lo).then_inc(chunk_done, 1)
                if kind == "g0b":
                    wait_lo(pe, c0 + 1)
                    if j == 0:
                        pe.wait_ge(at_ready, PAIRS)
                        pe.wait_ge(cv_ready, 2)
                        pe.wait_ge(mod_copied, 2)
                    else:
                        pe.wait_ge(merged, j)
                    column_chunk(c0 + 1, 0, at_hi, at_lo, 0, 4)
                    column_chunk(c0 + 1, 1, fn_hi, fn_lo, 4, 2)
                    column_chunk(c0 + 1, 2, cv_hi, cv_lo, 6, 2).then_inc(chunk_done, 1)
            for n in range(KT + 1):
                if n < KT:
                    wait_lo(pe, 2 * WO0 + n)
                    if n >= 2:
                        pe.wait_ge(x1_ready, n - 1)
                    column_chunk(2 * WO0 + n, 5 + n % 2, mg_hi, mg_lo, x_ready=mg_ready if n == 0 else None)\
                        .then_inc(chunk_done, 1)
                if n >= 1:
                    ssq(KT + n - 1, 2)
            for j in MOD_LAST[:-1]:
                mod_slot(j)
                if j > MOD_LAST[0]:
                    mod_turn(j - 1)
            pe.wait_ge(gr_in, 64)
            tok_banks = (0, 4, 6)
            for k in range(KT):
                if k in H2_BY_POOL:
                    pe.wait_ge(h2_ready_pool, H2_BY_POOL.index(k) + 1)
                else:
                    pe.wait_ge(h2_ready, sum(q not in H2_BY_POOL for q in range(k + 1)))
                ins = pe.matmul(ps[0:GROUPS + NE, 3, 0:N], w_gr[:, k, :], h2T[:, k, :], start=k == 0, stop=k == KT - 1)
            ins.then_inc(logits, 1)
            mod_turn(MOD_LAST[-2])
            for t in range(NT):
                if t == 0:
                    pe.wait_ge(modrow_ready, 23)
                if t == 2:
                    pe.wait_ge(mod_copied, 3)
                for k in range(KT):
                    ins = pe.transpose(ps[:, tok_banks[t] + k // 4, P * (k % 4):P * (k % 4) + P],
                                       h2T[:, k, P * t:P * t + P], ident[:])
                ins.then_inc(h2_turned, 1)
                if t == 0:
                    pe.wait_ge(logits_out, 1)
                    for q in range(NT):
                        ins = pe.transpose(ps[:, 2, 36 * q:36 * q + 36], lgT[:, P * q:P * q + P], ident[0:36, 0:36])
                    ins.then_inc(logits_turned, 1)
            pe.wait_ge(group_hot, 1)
            hot = og[:].rearrange("p t g -> p (t g)")
            pe.matmul(ps[:, 3, 0:12], tri[:], hot, start=True, stop=True)
            pe.matmul(ps[:, 3, 16:28], ones[:], hot, start=True, stop=True).then_inc(ranks, 1)

            def gather(nx, bank=5):
                pe.wait_ge(sel_ready, NT * nx + NT)
                for half in range(2):
                    d = slice(512 * half, 512 * half + 512)
                    for t in range(NT):
                        if isinstance(nx, int) and half == 0:
                            pe.wait_ge(ht_ready, t + 1)
                        pe.matmul(ps[:, bank + half, :], sel[:, t, :], ht_hi[:, t, d], start=t == 0, stop=False)
                        ins = pe.matmul(ps[:, bank + half, :], sel[:, t, :], ht_lo[:, t, d], start=False, stop=t == NT - 1)
                ins.then_inc(gathered, 1)

            def gather_weights(nx):
                for t in range(NT):
                    ins = pe.matmul(ps[:, 7, 0:EPG], sel[:, t, :].bitcast(F32), comb[:, t, :], start=t == 0, stop=t == NT - 1)
                ins.then_inc(weighted, 1)

            def hg_turn(nx, bank=5):
                pe.wait_ge(hg_out, nx + 1)
                for k in range(KT):
                    ins = pe.transpose(ps[:, bank + k // 4, P * (k % 4):P * (k % 4) + P], hg32[:, P * k:P * k + P], ident[:])
                ins.then_inc(hg_turned, 1)

            mod_slot(MOD_LAST[-1])
            gather(0, 0)
            mod_turn(MOD_LAST[-1])
            hg_turn(0, 0)
            pe.wait_ge(comb_ready, 1)
            gather_weights(0)

            def put_back(k, bank):
                d = slice(P * k, P * k + P)
                pe.matmul(ps[:, bank, 0:N], y_hi[:, d], selT[:], start=True, stop=False)
                return pe.matmul(ps[:, bank, 0:N], y_lo[:, d], selT[:], start=False, stop=True)

            def item(it, g):
                def hid_turn(e):
                    n = it * EPG + e
                    pe.wait_ge(hid_ready, n + 1)
                    for a in range(2):
                        ins = pe.transpose(ps[:, 4, P * a:P * a + P], hid[:, e % 2, P * a:P * a + P], ident[:])
                    ins.then_inc(hid_turned, 1)

                for what, e, part, i in order:
                    b = (PRE_CH + i) % SPLIT
                    wait_lo_item(pe, it, i)
                    if what == "up":
                        if part == 0 and e == 0:
                            pe.wait_ge(hg_ready, it + 1)
                        if part == 0 and e >= 2:
                            pe.wait_ge(hid_ready, it * EPG + e - 1)
                        if part == 0 and e == EPG - 1:
                            gather_weights(it + 1)
                            gather(it + 1)
                        for k in range(2):
                            w, kk = slice(512 * k, 512 * k + 512), 2 * part + k
                            ins = three(ps[:, e % 2, :], hg_hi[:, kk, :], hg_lo[:, kk, :], w_hi[:, b, w], w_lo[:, b, w],
                                        kk == 0, kk == KT - 1)
                        ins.then_inc(chunk_done, 1)
                        if part == 1 and e >= 2:
                            hid_turn(e - 1)
                        if part == 2 and e == 1:
                            hid_turn(0)
                        if part == 2 and e == SEL_TURN:
                            pe.wait_ge(cmb_ready, it + 1)
                            for t in range(NT):
                                ins = pe.transpose(ps[:, 7, P * (t + 1):P * (t + 1) + P], sel[:, t, :].bitcast(F32), ident[:])
                            ins.then_inc(sel_turned, 1)
                    else:
                        if part == 0 and e == 0:
                            pe.wait_ge(y_ready, it + 1)
                        if part == 0 and e == EPG - 1:
                            hid_turn(e)
                            hg_turn(it + 1)
                        if part == 0:
                            pe.wait_ge(hd_ready, it * EPG + e + 1)
                        for half in range(2):
                            w = slice(512 * half, 512 * half + 512)
                            ins = three(ps[:, 2 + half, :], hd_hi[:, part, :], hd_lo[:, part, :], w_hi[:, b, w], w_lo[:, b, w],
                                        e == 0 and part == 0, e == EPG - 1 and part == 1)
                        ins.then_inc(chunk_done, 1)
                    k = i - COMBINE0
                    if 0 <= k < KT:
                        if k == 0:
                            pe.wait_ge(y_ready, it + 1)
                            pe.wait_ge(selT_ready, it + 1)
                        if k >= 2:
                            pe.wait_ge(added, it * 2 * KT + 2 * (k - 1))
                        put_back(k, 5 + k % 2).then_inc(combined, 1)

            rounds(pe, item)
            pe.transpose(ps[:, 4, 0:P], ident[:], ident[:]).then_inc(y_last, 1)
            out_banks = (0, 2, 5)
            for k in range(KT + 1):
                if k < KT:
                    if k >= 2:
                        pe.wait_ge(x2_ready, 2 * (k - 1))
                    pe.wait_ge(y_lo_last, 1 + k // 4)
                    put_back(k, (4, 7)[k % 2]).then_inc(combined_last, 1)
                if k >= 1:
                    pe.wait_ge(x2_ready, 2 * k)
                    for t in range(NT):
                        ins = pe.transpose(ps[:, out_banks[t] + (k - 1) // 4, P * ((k - 1) % 4):P * ((k - 1) % 4) + P],
                                           xT[:, k - 1, P * t:P * t + P], ident[:])
                        if k == KT:
                            ins.then_inc(out_turned, 1)


_INS = ['x_prompt', 'x_sample', 'cache_k', 'cache_v', 'c', 'c_ctx', 'w_mod', 'b_mod', 'norm1_g', 'w_in', 'rpb',
        'w_attn_o', 'w_fnet', 'conv_dw', 'conv_b', 'conv_ln_g', 'conv_ln_b', 'w_conv_o', 'w_out', 'norm2_g',
        'w_group', 'b_group', 'w_router', 'b_router', 'w1', 'w3', 'w2', 'final_g']
_OUTS = [("y_prompt", (1, NCTX, D)), ("y_sample", (1, NLAT, D)), ("new_k", (1, 1, HEADS, NCTX, HD)),
         ("new_v", (1, 1, HEADS, NCTX, HD))]


def _dft(n, norm):
    import numpy as np
    a = 2.0 * np.pi * ((np.arange(n)[:, None] * np.arange(n)[None, :]) % n) / n
    return np.concatenate([np.cos(a) * norm, np.sin(a) * norm], axis=1)


def _constants():
    import numpy as np
    f = _dft(FG, 1.0)
    feat = np.zeros((P, 2 * P))
    for g in range(P // FG):
        rows = slice(FG * g, FG * g + FG)
        feat[rows, FG * g:FG * g + FG] = f[:, 0:FG]
        feat[rows, P + FG * g:P + FG * g + FG] = -f[:, FG:]
    return {"dft_lat": _dft(NLAT, (NLAT * FG) ** -0.5).astype(np.float32),
            "dft_ctx": _dft(NCTX, (NCTX * FG) ** -0.5).astype(np.float32), "dft_feat": feat.astype(np.float32)}


def _lay_out(inputs):
    import numpy as np
    arrays = {name: np.ascontiguousarray(a) for name, a in inputs.items()}
    arrays["small_rows"] = np.concatenate([arrays.pop(n).reshape(-1, P) for n in SMALL])
    arrays["rpb"] = np.tile(arrays["rpb"], (1, 1, 1, GRID_W))
    arrays.update(_constants())
    return arrays


def kernel(**inputs):
    import concourse.bacc as bacc
    from concourse.bass_utils import run_bass_kernel_spmd

    nc = bacc.Bacc("TRN2", target_bir_lowering=False, num_devices=1)
    arrays = _lay_out({name: inputs[name] for name in _INS})
    args = {}
    for name, a in arrays.items():
        args[name] = nc.dram_tensor(name, a.shape, mybir.dt.from_np(a.dtype), kind="ExternalInput").ap()
    for name, shape in _OUTS:
        args[name] = nc.dram_tensor(name, shape, F32, kind="ExternalOutput").ap()
    build(nc, **args)
    r = run_bass_kernel_spmd(nc, [arrays], core_ids=[0])
    return tuple(r.results[0][name] for name, _ in _OUTS)
```
